# Optimizing a Trainium2 kernel written in Bass

```python
import jax, jax.numpy as jnp
from jax import lax
import numpy as np
import math
import jax
import jax.numpy as jnp

D_MODEL = 1024
BATCH = 1
SEQ = 256
DEPTH = 2

HEAD_DIM = 64
N_MIX_HEADS = D_MODEL // HEAD_DIM
A_Q_HEADS = N_MIX_HEADS // 2
A_KV_HEADS = 2
B_Q_HEADS = N_MIX_HEADS - A_Q_HEADS
B_KV_HEADS = 2
MIX_WIDTH = (A_Q_HEADS + B_Q_HEADS) * HEAD_DIM
QA_W = A_Q_HEADS * HEAD_DIM
KVA_W = A_KV_HEADS * HEAD_DIM
QB_W = B_Q_HEADS * HEAD_DIM
KVB_W = B_KV_HEADS * HEAD_DIM
IN_WIDTH = QA_W + 2 * KVA_W + QB_W + 2 * KVB_W
SPLITS = [QA_W, QA_W + KVA_W, QA_W + 2 * KVA_W, QA_W + 2 * KVA_W + QB_W,
          QA_W + 2 * KVA_W + QB_W + KVB_W]

BLOCK = 128
WINDOW = 128
GRID_W = 64
ROPE_THETA = 10000.0
ROPE_FREQS = HEAD_DIM // 4

PEER_HEADS = 8
PEER_NKEYS = 128
PEER_EXPERTS = PEER_NKEYS * PEER_NKEYS
PEER_DKEY = 256
PEER_TOPK = 16
PEER_CHUNK = 128

DEEPNORM_ALPHA = (2.0 * DEPTH) ** 0.25
DEEPNORM_BETA = (8.0 * DEPTH) ** -0.25
LN_EPS = 1e-5
RMS_EPS = 1e-6
NEG_INF = -1e30


def alibi_slopes(n):
    return (2.0 ** (-(np.arange(1, n + 1, dtype=np.float32) * 8.0 / n))).astype(np.float32)

def layer_norm(x, g, b):
    xf = x.astype(jnp.float32)
    mu = xf.mean(-1, keepdims=True)
    var = jnp.square(xf - mu).mean(-1, keepdims=True)
    return ((xf - mu) * lax.rsqrt(var + LN_EPS) * g + b).astype(x.dtype)

def rms_norm(x, g):
    xf = x.astype(jnp.float32)
    return (xf * lax.rsqrt(jnp.square(xf).mean(-1, keepdims=True) + RMS_EPS) * g).astype(x.dtype)

def axial_rope_tables(S):
    rows = S // GRID_W
    row = jnp.repeat(jnp.arange(rows), GRID_W)
    col = jnp.tile(jnp.arange(GRID_W), rows)
    pos = jnp.stack([row, col], axis=-1).astype(jnp.float32)
    inv_freq = ROPE_THETA ** (-jnp.arange(ROPE_FREQS, dtype=jnp.float32) / ROPE_FREQS)
    ang = pos[:, :, None] * inv_freq
    return jnp.cos(ang), jnp.sin(ang)

def apply_axial_rope(x, cos, sin):
    B, S, H, dh = x.shape
    xr = x.astype(jnp.float32).reshape(B, S, H, 2, 2, ROPE_FREQS)
    x1, x2 = xr[..., 0, :], xr[..., 1, :]
    c, s = cos[None, :, None], sin[None, :, None]
    out = jnp.stack([x1 * c - x2 * s, x1 * s + x2 * c], axis=-2)
    return out.reshape(B, S, H, dh).astype(x.dtype)

def global_attention(q, k, v):
    B, S, Hq, dh = q.shape
    Hkv = k.shape[2]
    G = Hq // Hkv
    nb = S // BLOCK
    scale = dh ** -0.5
    qb = q.reshape(B, nb, BLOCK, Hkv, G, dh).transpose(1, 0, 2, 3, 4, 5)

    def one_block(qblk):
        sc = jnp.einsum('bqkgd,bskd->bkgqs', qblk, k, preferred_element_type=jnp.float32) * scale
        p = jax.nn.softmax(sc, axis=-1).astype(v.dtype)
        return jnp.einsum('bkgqs,bskd->bqkgd', p, v)

    o = lax.map(one_block, qb)
    return o.transpose(1, 0, 2, 3, 4, 5).reshape(B, S, Hq, dh)

def window_sink_attention(q, k, v, sink, slopes):
    B, S, Hq, dh = q.shape
    Hkv = k.shape[2]
    G = Hq // Hkv
    nb = S // BLOCK
    span = BLOCK + 2 * WINDOW
    scale = dh ** -0.5
    qb = q.reshape(B, nb, BLOCK, Hkv, G, dh).transpose(1, 0, 2, 3, 4, 5)
    pad = ((0, 0), (WINDOW, WINDOW), (0, 0), (0, 0))
    kp = jnp.pad(k, pad)
    vp = jnp.pad(v, pad)
    slope = slopes.reshape(Hkv, G, 1, 1)
    sink_l = sink.astype(jnp.float32).reshape(Hkv, G, 1)
    q_off = jnp.arange(BLOCK)
    k_off = jnp.arange(span) - WINDOW

    def one_block(args):
        qblk, j = args
        start = j * BLOCK
        kb = lax.dynamic_slice_in_dim(kp, start, span, axis=1)
        vb = lax.dynamic_slice_in_dim(vp, start, span, axis=1)
        t = start + q_off
        s_pos = start + k_off
        dist = jnp.abs(t[:, None] - s_pos[None, :])
        valid = (dist <= WINDOW) & (s_pos >= 0)[None, :] & (s_pos < S)[None, :]
        sc = jnp.einsum('bqkgd,bskd->bkgqs', qblk, kb, preferred_element_type=jnp.float32) * scale
        sc = sc - slope * dist.astype(jnp.float32)
        sc = jnp.where(valid, sc, NEG_INF)
        m = jnp.maximum(sc.max(-1), sink_l)
        p = jnp.exp(sc - m[..., None])
        denom = p.sum(-1) + jnp.exp(sink_l - m)
        p = (p / denom[..., None]).astype(v.dtype)
        return jnp.einsum('bkgqs,bskd->bqkgd', p, vb)

    o = lax.map(one_block, (qb, jnp.arange(nb)))
    return o.transpose(1, 0, 2, 3, 4, 5).reshape(B, S, Hq, dh)

def peer_ffn(x, wq, sub_keys, u, v):
    B, S, D = x.shape
    xt = x.reshape(-1, PEER_CHUNK, D)
    half = PEER_DKEY // 2

    def chunk(xc):
        q = (xc @ wq).reshape(PEER_CHUNK, PEER_HEADS, 2, half)
        sc = jnp.einsum('chpd,hpnd->chpn', q, sub_keys, preferred_element_type=jnp.float32)
        s1, i1 = lax.top_k(sc[:, :, 0], PEER_TOPK)
        s2, i2 = lax.top_k(sc[:, :, 1], PEER_TOPK)
        cand = (s1[..., :, None] + s2[..., None, :]).reshape(PEER_CHUNK, PEER_HEADS, PEER_TOPK * PEER_TOPK)
        cidx = (i1[..., :, None] * PEER_NKEYS + i2[..., None, :]).reshape(PEER_CHUNK, PEER_HEADS, PEER_TOPK * PEER_TOPK)
        top_s, pos = lax.top_k(cand, PEER_TOPK)
        eidx = jnp.take_along_axis(cidx, pos, axis=-1)
        g = jax.nn.softmax(top_s, axis=-1)
        u_sel = jnp.take(u, eidx, axis=0)
        a = jax.nn.gelu(jnp.einsum('chkd,cd->chk', u_sel, xc, preferred_element_type=jnp.float32), approximate=False)
        w = (g * a).astype(x.dtype)
        v_sel = jnp.take(v, eidx, axis=0)
        return jnp.einsum('chk,chkd->cd', w, v_sel)

    return lax.map(chunk, xt).reshape(B, S, D)

def first_inputs(seed: int = 0) -> dict:
    key = jax.random.key(seed)
    ks = jax.random.split(key, 24)
    L, D = DEPTH, D_MODEL
    beta = DEEPNORM_BETA

    def nrm(k, shape, std):
        return jax.random.normal(k, shape, jnp.float32) * std

    x = nrm(ks[0], (BATCH, SEQ, D), 1.0)
    ln_in_g = 1.0 + nrm(ks[1], (D,), 0.02)
    ln_in_b = nrm(ks[2], (D,), 0.02)
    col_scale = jnp.concatenate([
        jnp.ones((QA_W + KVA_W,), jnp.float32), jnp.full((KVA_W,), beta, jnp.float32),
        jnp.ones((QB_W + KVB_W,), jnp.float32), jnp.full((KVB_W,), beta, jnp.float32)])
    w_in = nrm(ks[3], (L, D, IN_WIDTH), D ** -0.5) * col_scale
    qn_g = 1.0 + nrm(ks[4], (L, HEAD_DIM), 0.02)
    kn_g = 1.0 + nrm(ks[5], (L, HEAD_DIM), 0.02)
    sink = nrm(ks[6], (L, B_Q_HEADS), 0.5)
    gn_a_g = 1.0 + nrm(ks[7], (L, QA_W), 0.02)
    gn_b_g = 1.0 + nrm(ks[8], (L, QB_W), 0.02)
    w_o = nrm(ks[9], (L, MIX_WIDTH, D), beta * MIX_WIDTH ** -0.5)
    ln1_g = 1.0 + nrm(ks[10], (L, D), 0.02)
    ln1_b = nrm(ks[11], (L, D), 0.02)
    peer_wq = nrm(ks[12], (L, D, PEER_HEADS * PEER_DKEY), D ** -0.5)
    peer_keys = nrm(ks[13], (L, PEER_HEADS, 2, PEER_NKEYS, PEER_DKEY // 2), (PEER_DKEY // 2) ** -0.5)
    peer_u = nrm(ks[14], (L, PEER_EXPERTS, D), D ** -0.5)
    peer_v = nrm(ks[15], (L, PEER_EXPERTS, D), beta * (PEER_HEADS * PEER_TOPK) ** -0.5)
    ln2_g = 1.0 + nrm(ks[16], (L, D), 0.02)
    ln2_b = nrm(ks[17], (L, D), 0.02)
    return {'x': x, 'ln_in_g': ln_in_g, 'ln_in_b': ln_in_b, 'w_in': w_in,
            'qn_g': qn_g, 'kn_g': kn_g, 'sink': sink, 'gn_a_g': gn_a_g, 'gn_b_g': gn_b_g,
            'w_o': w_o, 'ln1_g': ln1_g, 'ln1_b': ln1_b, 'peer_wq': peer_wq,
            'peer_keys': peer_keys, 'peer_u': peer_u, 'peer_v': peer_v,
            'ln2_g': ln2_g, 'ln2_b': ln2_b}

def first_block(x, ln_in_g, ln_in_b, w_in, qn_g, kn_g, sink, gn_a_g, gn_b_g, w_o,
              ln1_g, ln1_b, peer_wq, peer_keys, peer_u, peer_v, ln2_g, ln2_b):
    B, S, D = x.shape
    cos, sin = axial_rope_tables(S)
    slopes = jnp.asarray(alibi_slopes(B_Q_HEADS))
    h = layer_norm(x, ln_in_g, ln_in_b)
    for l in range(DEPTH):
        proj = h @ w_in[l]
        qa, ka, va, qb, kb, vb = jnp.split(proj, SPLITS, axis=-1)
        qa = qa.reshape(B, S, A_Q_HEADS, HEAD_DIM)
        ka = ka.reshape(B, S, A_KV_HEADS, HEAD_DIM)
        va = va.reshape(B, S, A_KV_HEADS, HEAD_DIM)
        qb = qb.reshape(B, S, B_Q_HEADS, HEAD_DIM)
        kb = kb.reshape(B, S, B_KV_HEADS, HEAD_DIM)
        vb = vb.reshape(B, S, B_KV_HEADS, HEAD_DIM)
        qa = apply_axial_rope(rms_norm(qa, qn_g[l]), cos, sin)
        ka = apply_axial_rope(rms_norm(ka, kn_g[l]), cos, sin)
        oa = global_attention(qa, ka, va)
        ob = window_sink_attention(qb, kb, vb, sink[l], slopes)
        oa = rms_norm(oa, gn_a_g[l].reshape(A_Q_HEADS, HEAD_DIM)).reshape(B, S, QA_W)
        ob = rms_norm(ob, gn_b_g[l].reshape(B_Q_HEADS, HEAD_DIM)).reshape(B, S, QB_W)
        mix = jnp.concatenate([oa, ob], axis=-1) @ w_o[l]
        h = layer_norm(DEEPNORM_ALPHA * h + mix, ln1_g[l], ln1_b[l])
        ffn = peer_ffn(h, peer_wq[l], peer_keys[l], peer_u[l], peer_v[l])
        h = layer_norm(DEEPNORM_ALPHA * h + ffn, ln2_g[l], ln2_b[l])
    return h


DEPTH_2 = 1

CTX_LEN = 256
H_RET = 4
RET_DK = 128
RET_DV = 128
RET_W = H_RET * RET_DV
H_GDN = 4
GDN_DK = 128
GDN_DV = 128
GDN_W = H_GDN * GDN_DV
SHORT_CONV = 3
CHUNK = 128
ROPE_BASE = 10000.0
N_STATE = 2 * RET_W + 2 * GDN_W + 4 * H_GDN
N_QUERY = 2 * RET_W + 2 * GDN_W + 2 * D_MODEL
N_IN = N_STATE + N_QUERY
N_EXPERTS = 64
TOP_K = 8
N_GROUPS = 8
TOPK_GROUPS = 4
D_EXPERT = 256
D_SHARED = 256
ROUTED_SCALE = 2.5
EXPERT_BLOCK = 128
EPS = 1e-6


def _rmsnorm(t, g):
    tf = t.astype(jnp.float32)
    y = tf * lax.rsqrt(jnp.mean(tf * tf, axis=-1, keepdims=True) + EPS)
    return (y * g.astype(jnp.float32)).astype(t.dtype)

def _l2norm(t):
    return t * lax.rsqrt(jnp.sum(t * t, axis=-1, keepdims=True) + EPS)

def _group_norm(t):
    tc = t - jnp.mean(t, axis=-1, keepdims=True)
    return tc * lax.rsqrt(jnp.mean(tc * tc, axis=-1, keepdims=True) + EPS)

def _head_rms(t):
    return t * lax.rsqrt(jnp.mean(t * t, axis=-1, keepdims=True) + EPS)

def _split_heads(t, n_heads):
    b, l, w = t.shape
    return t.reshape(b, l, n_heads, w // n_heads).transpose(0, 2, 1, 3)

def _merge_heads(t):
    b, h, l, d = t.shape
    return t.transpose(0, 2, 1, 3).reshape(b, l, h * d)

def _dwconv(t, w):
    return lax.conv_general_dilated(t, w[:, None, :].astype(t.dtype), (1,), 'SAME',
                                    dimension_numbers=('NWC', 'WIO', 'NWC'),
                                    feature_group_count=t.shape[-1])

def _modulation(cvec, w, b, n):
    m = jax.nn.silu(cvec) @ w[:, : n * D_MODEL] + b[: n * D_MODEL]
    return jnp.split(m, n, axis=-1)

def _axial_rope(n):
    rows = n // GRID_W
    pos_r = jnp.repeat(jnp.arange(rows, dtype=jnp.float32), GRID_W)
    pos_c = jnp.tile(jnp.arange(GRID_W, dtype=jnp.float32), rows)
    n_freq = RET_DK // 4
    inv = ROPE_BASE ** (-jnp.arange(n_freq, dtype=jnp.float32) / n_freq)
    ang = jnp.concatenate([pos_r[:, None] * inv, pos_c[:, None] * inv], axis=-1)
    return jnp.cos(ang), jnp.sin(ang)

def _apply_rope(t, cos, sin):
    half = RET_DK // 2
    t1, t2 = t[..., :half], t[..., half:]
    return jnp.concatenate([t1 * cos - t2 * sin, t1 * sin + t2 * cos], axis=-1)

def _retention_scan(q, k, v, log_g, s0):
    b, h, l, dk = k.shape
    n = l // CHUNK
    kc = k.reshape(b, h, n, CHUNK, dk)
    vc = v.reshape(b, h, n, CHUNK, -1)
    lg = log_g.astype(jnp.float32)[:, None]
    idx = jnp.arange(CHUNK, dtype=jnp.float32)
    kv = jnp.einsum('bhncd,hc,bhnce->bhnde', kc, jnp.exp(lg * (CHUNK - 1 - idx)), vc)
    chunk_decay = jnp.exp(lg[:, 0] * CHUNK)[None, :, None, None]

    def step(s, kv_n):
        return chunk_decay * s + kv_n, (None if q is None else s)

    s_fin, s_prev = lax.scan(step, s0, jnp.moveaxis(kv, 2, 0))
    if q is None:
        return s_fin
    qc = q.reshape(b, h, n, CHUNK, dk)
    dist = idx[:, None] - idx[None, :]
    dmat = jnp.where(dist >= 0, jnp.exp(lg[:, :, None] * jnp.maximum(dist, 0.0)), 0.0)
    scores = jnp.einsum('bhnid,bhnjd->bhnij', qc, kc) * dmat[None, :, None]
    o = jnp.einsum('bhnij,bhnje->bhnie', scores, vc)
    o = o + jnp.einsum('bhnid,nbhde->bhnie', qc, s_prev) * jnp.exp(lg * (idx + 1.0))[None, :, None, :, None]
    return o.reshape(b, h, l, -1), s_fin

def _gdn_scan(q, k, v, log_a, beta, s0):
    b, h, l, dk = k.shape
    dv = v.shape[-1]
    n = l // CHUNK
    kc = k.reshape(b, h, n, CHUNK, dk)
    vc = v.reshape(b, h, n, CHUNK, dv)
    bc = beta.reshape(b, h, n, CHUNK, 1)
    g = jnp.cumsum(log_a.reshape(b, h, n, CHUNK), axis=-1)
    idx = jnp.arange(CHUNK)
    strict = idx[:, None] > idx[None, :]
    rel = g[..., :, None] - g[..., None, :]
    a = jnp.einsum('bhnid,bhnjd->bhnij', kc, kc) * bc * jnp.where(strict, jnp.exp(jnp.where(strict, rel, 0.0)), 0.0)
    rhs = jnp.concatenate([bc * vc, bc * jnp.exp(g)[..., None] * kc], axis=-1)
    sol = lax.linalg.triangular_solve(a + jnp.eye(CHUNK, dtype=a.dtype), rhs,
                                      left_side=True, lower=True, unit_diagonal=True)
    u, wk = sol[..., :dv], sol[..., dv:]
    g_last = g[..., -1]
    k_tail = kc * jnp.exp(g_last[..., None] - g)[..., None]

    def step(s, inp):
        u_n, w_n, kt_n, gl_n = inp
        v_new = u_n - jnp.einsum('bhck,bhkv->bhcv', w_n, s)
        s_next = jnp.exp(gl_n)[..., None, None] * s + jnp.einsum('bhck,bhcv->bhkv', kt_n, v_new)
        return s_next, (None if q is None else (v_new, s))

    xs = tuple(jnp.moveaxis(t, 2, 0) for t in (u, wk, k_tail, g_last))
    s_fin, ys = lax.scan(step, s0, xs)
    if q is None:
        return s_fin
    v_new, s_prev = ys
    qc = q.reshape(b, h, n, CHUNK, dk)
    incl = idx[:, None] >= idx[None, :]
    qk = jnp.einsum('bhnid,bhnjd->bhnij', qc, kc) * jnp.where(incl, jnp.exp(jnp.where(incl, rel, 0.0)), 0.0)
    o = jnp.einsum('bhnij,nbhjv->bhniv', qk, v_new)
    o = o + jnp.einsum('bhnik,nbhkv->bhniv', qc * jnp.exp(g)[..., None], s_prev)
    return o.reshape(b, h, l, -1), s_fin

def _state_features(h, w_in_l, conv_l, a_log_l, dt_bias_l):
    p = h @ w_in_l[:, :N_STATE]
    rk = _split_heads(p[..., :RET_W].astype(jnp.float32), H_RET) * RET_DK ** -0.5
    rv = _split_heads(p[..., RET_W:2 * RET_W].astype(jnp.float32), H_RET)
    gkv = jax.nn.silu(_dwconv(p[..., 2 * RET_W:2 * RET_W + 2 * GDN_W], conv_l[:, GDN_W:])).astype(jnp.float32)
    gk = _l2norm(_split_heads(gkv[..., :GDN_W], H_GDN))
    gv = _split_heads(gkv[..., GDN_W:], H_GDN)
    b, l = h.shape[:2]
    gab = p[..., 2 * RET_W + 2 * GDN_W:].astype(jnp.float32).reshape(b, l, 2, 2, H_GDN).transpose(2, 3, 0, 4, 1)
    log_a = -jnp.exp(a_log_l.astype(jnp.float32))[:, None, :, None] * jax.nn.softplus(
        gab[0] + dt_bias_l.astype(jnp.float32)[:, None, :, None])
    beta = jax.nn.sigmoid(gab[1])
    return rk, rv, gk, gv, log_a, beta

def _query_features(h, w_in_l, conv_l):
    p = h @ w_in_l[:, N_STATE:]
    rq = _split_heads(p[..., :RET_W].astype(jnp.float32), H_RET)
    rg = p[..., RET_W:2 * RET_W]
    gq = jax.nn.silu(_dwconv(p[..., 2 * RET_W:2 * RET_W + GDN_W], conv_l[:, :GDN_W])).astype(jnp.float32)
    gq = _l2norm(_split_heads(gq, H_GDN)) * GDN_DK ** -0.5
    gz = p[..., 2 * RET_W + GDN_W:2 * RET_W + 2 * GDN_W]
    gates = jax.nn.sigmoid(p[..., 2 * RET_W + 2 * GDN_W:].astype(jnp.float32))
    return rq, rg, gq, gz, gates

def _recurrent_mixers(sf, rq, gq, init, ret_log_decay_l):
    rk, rv, gk, gv, log_a, beta = sf
    flip = lambda t: jnp.flip(t, axis=2)
    r_f = _retention_scan(rq, rk, rv, ret_log_decay_l[0], init[0])
    r_b = _retention_scan(None if rq is None else flip(rq), flip(rk), flip(rv), ret_log_decay_l[1], init[1])
    g_f = _gdn_scan(gq, gk, gv, log_a[0], beta[0], init[2])
    g_b = _gdn_scan(None if gq is None else flip(gq), flip(gk), flip(gv), flip(log_a[1]), flip(beta[1]), init[3])
    if rq is None:
        return (r_f, r_b, g_f, g_b)
    return r_f[0] + flip(r_b[0]), g_f[0] + flip(g_b[0]), (r_f[1], r_b[1], g_f[1], g_b[1])

def _mixer_out(ret_o, gdn_o, rg, gz, gates, ret_gn_w_l, gdn_norm_w_l, w_ret_out_l, w_gdn_out_l, w_o_l):
    dt = w_o_l.dtype
    ret_y = _merge_heads(_group_norm(ret_o)) * ret_gn_w_l.astype(jnp.float32) * jax.nn.silu(rg.astype(jnp.float32))
    gdn_y = _merge_heads(_head_rms(gdn_o)) * gdn_norm_w_l.astype(jnp.float32) * jax.nn.silu(gz.astype(jnp.float32))
    merged = (gates[..., :D_MODEL] * (ret_y.astype(dt) @ w_ret_out_l)
              + gates[..., D_MODEL:] * (gdn_y.astype(dt) @ w_gdn_out_l))
    return merged.astype(dt) @ w_o_l

def _moe(h, w_router_l, bias_l, w_gate_l, w_up_l, w_down_l, w_sh_gate_l, w_sh_up_l, w_sh_down_l):
    b, l, d = h.shape
    t = b * l
    xt = h.reshape(t, d)
    scores = jax.nn.sigmoid((xt @ w_router_l).astype(jnp.float32))
    biased = scores + bias_l.astype(jnp.float32)
    per_group = N_EXPERTS // N_GROUPS
    grp_score = lax.top_k(biased.reshape(t, N_GROUPS, per_group), 2)[0].sum(-1)
    grp_keep = jax.nn.one_hot(lax.top_k(grp_score, TOPK_GROUPS)[1], N_GROUPS, dtype=jnp.float32).sum(1) > 0
    cand = jnp.where(jnp.repeat(grp_keep, per_group, axis=1), biased, -jnp.inf)
    sel = lax.top_k(cand, TOP_K)[1]
    wts = jnp.take_along_axis(scores, sel, axis=1)
    wts = wts / jnp.sum(wts, axis=-1, keepdims=True) * ROUTED_SCALE
    n_assign = t * TOP_K
    flat_e = sel.reshape(-1)
    order = jnp.argsort(flat_e)
    e_sorted = flat_e[order]
    sizes = jnp.bincount(flat_e, length=N_EXPERTS).astype(jnp.int32)
    padded = (sizes + EXPERT_BLOCK - 1) // EXPERT_BLOCK * EXPERT_BLOCK
    pad_end = jnp.cumsum(padded)
    slot = (pad_end - padded)[e_sorted] + jnp.arange(n_assign, dtype=jnp.int32) - (jnp.cumsum(sizes) - sizes)[e_sorted]
    n_blocks = -(-n_assign // EXPERT_BLOCK) + N_EXPERTS
    n_slots = n_blocks * EXPERT_BLOCK
    slot_tok = jnp.full((n_slots,), t, jnp.int32).at[slot].set((order // TOP_K).astype(jnp.int32))
    slot_w = jnp.zeros((n_slots,), jnp.float32).at[slot].set(wts.reshape(-1)[order])
    block_e = jnp.minimum(jnp.searchsorted(pad_end, jnp.arange(n_blocks, dtype=jnp.int32) * EXPERT_BLOCK, side='right'),
                          N_EXPERTS - 1)
    xb = jnp.concatenate([xt, jnp.zeros((1, d), xt.dtype)])[slot_tok].reshape(n_blocks, EXPERT_BLOCK, d)

    def expert_block(args):
        xe, e = args
        return (jax.nn.silu(xe @ w_gate_l[e]) * (xe @ w_up_l[e])) @ w_down_l[e]

    yb = lax.map(expert_block, (xb, block_e)).reshape(n_slots, d)
    routed = jax.ops.segment_sum(yb * slot_w[:, None].astype(yb.dtype), slot_tok, num_segments=t + 1)[:t]
    shared = (jax.nn.silu(xt @ w_sh_gate_l) * (xt @ w_sh_up_l)) @ w_sh_down_l
    return (routed + shared).reshape(b, l, d)

def second_inputs(seed: int = 0) -> dict:
    key = jax.random.key(seed)
    ks = jax.random.split(key, 32)
    f32 = jnp.float32
    D = D_MODEL

    def nrm(k, shape, fan_in, scale=1.0):
        return jax.random.normal(k, shape, f32) * (scale * fan_in ** -0.5)

    def gain(k, shape):
        return 1.0 + 0.05 * jax.random.normal(k, shape, f32)

    base_decay = jnp.log1p(-jnp.power(2.0, -5.0 - jnp.arange(H_RET, dtype=f32)))
    dt = jnp.exp(jax.random.uniform(ks[12], (DEPTH_2, 2, H_GDN), f32, math.log(1e-3), math.log(1e-1)))
    return {
        'x': jax.random.normal(ks[0], (BATCH, SEQ, D), f32),
        'c': jax.random.normal(ks[1], (BATCH, D), f32),
        'ctx': jax.random.normal(ks[2], (BATCH, CTX_LEN, D), f32),
        'c_ctx': jax.random.normal(ks[3], (D,), f32),
        'w_mod': nrm(ks[4], (DEPTH_2, D, 6 * D), D, 0.3),
        'b_mod': 0.02 * jax.random.normal(ks[5], (DEPTH_2, 6 * D), f32),
        'norm_mix_pre': gain(ks[6], (DEPTH_2, D)),
        'norm_mix_post': gain(ks[7], (DEPTH_2, D)),
        'norm_ffn_pre': gain(ks[8], (DEPTH_2, D)),
        'norm_ffn_post': gain(ks[9], (DEPTH_2, D)),
        'w_in': nrm(ks[10], (DEPTH_2, D, N_IN), D),
        'gdn_conv': nrm(ks[11], (DEPTH_2, SHORT_CONV, 3 * GDN_W), SHORT_CONV),
        'ret_log_decay': base_decay * (1.0 + 0.05 * jax.random.normal(ks[13], (DEPTH_2, 2, H_RET), f32)),
        'gdn_a_log': jnp.log(jax.random.uniform(ks[14], (DEPTH_2, 2, H_GDN), f32, 1.0, 16.0)),
        'gdn_dt_bias': dt + jnp.log(-jnp.expm1(-dt)),
        'ret_gn_w': gain(ks[15], (DEPTH_2, RET_W)),
        'gdn_norm_w': gain(ks[16], (DEPTH_2, GDN_W)),
        'w_ret_out': nrm(ks[17], (DEPTH_2, RET_W, D), RET_W),
        'w_gdn_out': nrm(ks[18], (DEPTH_2, GDN_W, D), GDN_W),
        'w_o': nrm(ks[19], (DEPTH_2, D, D), D),
        'w_router': nrm(ks[20], (DEPTH_2, D, N_EXPERTS), D),
        'router_bias': 0.01 * jax.random.normal(ks[21], (DEPTH_2, N_EXPERTS), f32),
        'w_gate': nrm(ks[22], (DEPTH_2, N_EXPERTS, D, D_EXPERT), D),
        'w_up': nrm(ks[23], (DEPTH_2, N_EXPERTS, D, D_EXPERT), D),
        'w_down': nrm(ks[24], (DEPTH_2, N_EXPERTS, D_EXPERT, D), D_EXPERT),
        'w_sh_gate': nrm(ks[25], (DEPTH_2, D, D_SHARED), D),
        'w_sh_up': nrm(ks[26], (DEPTH_2, D, D_SHARED), D),
        'w_sh_down': nrm(ks[27], (DEPTH_2, D_SHARED, D), D_SHARED),
    }

def second_block(x, c, ctx, c_ctx, w_mod, b_mod, norm_mix_pre, norm_mix_post, norm_ffn_pre, norm_ffn_post,
              w_in, gdn_conv, ret_log_decay, gdn_a_log, gdn_dt_bias, ret_gn_w, gdn_norm_w,
              w_ret_out, w_gdn_out, w_o, w_router, router_bias, w_gate, w_up, w_down,
              w_sh_gate, w_sh_up, w_sh_down):
    b, n, _ = x.shape
    cos, sin = _axial_rope(n)
    zr = jnp.zeros((b, H_RET, RET_DK, RET_DV), jnp.float32)
    zg = jnp.zeros((b, H_GDN, GDN_DK, GDN_DV), jnp.float32)
    zero_state = (zr, zr, zg, zg)
    for i in range(DEPTH_2):
        last = i == DEPTH_2 - 1
        out_p = (ret_gn_w[i], gdn_norm_w[i], w_ret_out[i], w_gdn_out[i], w_o[i])
        moe_p = (w_router[i], router_bias[i], w_gate[i], w_up[i], w_down[i], w_sh_gate[i], w_sh_up[i], w_sh_down[i])
        sh1, sc1, g1, sh2, sc2, g2 = [m[:, None, :] for m in _modulation(c, w_mod[i], b_mod[i], 6)]
        cm = _modulation(c_ctx, w_mod[i], b_mod[i], 2 if last else 6)
        hc = _rmsnorm(ctx, norm_mix_pre[i]) * (1.0 + cm[1]) + cm[0]
        sf_c = _state_features(hc, w_in[i], gdn_conv[i], gdn_a_log[i], gdn_dt_bias[i])
        if last:
            init = _recurrent_mixers(sf_c, None, None, zero_state, ret_log_decay[i])
        else:
            rq_c, rg_c, gq_c, gz_c, gates_c = _query_features(hc, w_in[i], gdn_conv[i])
            ret_c, gdn_c, init = _recurrent_mixers(sf_c, rq_c, gq_c, zero_state, ret_log_decay[i])
            ctx = ctx + cm[2] * _rmsnorm(_mixer_out(ret_c, gdn_c, rg_c, gz_c, gates_c, *out_p), norm_mix_post[i])
            h2c = _rmsnorm(ctx, norm_ffn_pre[i]) * (1.0 + cm[4]) + cm[3]
            ctx = ctx + cm[5] * _rmsnorm(_moe(h2c, *moe_p), norm_ffn_post[i])
        hx = _rmsnorm(x, norm_mix_pre[i]) * (1.0 + sc1) + sh1
        rk, rv, gk, gv, log_a, beta = _state_features(hx, w_in[i], gdn_conv[i], gdn_a_log[i], gdn_dt_bias[i])
        rq, rg, gq, gz, gates = _query_features(hx, w_in[i], gdn_conv[i])
        sf_x = (_apply_rope(rk, cos, sin), rv, gk, gv, log_a, beta)
        ret_x, gdn_x, _ = _recurrent_mixers(sf_x, _apply_rope(rq, cos, sin), gq, init, ret_log_decay[i])
        x = x + g1 * _rmsnorm(_mixer_out(ret_x, gdn_x, rg, gz, gates, *out_p), norm_mix_post[i])
        h2 = _rmsnorm(x, norm_ffn_pre[i]) * (1.0 + sc2) + sh2
        x = x + g2 * _rmsnorm(_moe(h2, *moe_p), norm_ffn_post[i])
    return x


def setup_inputs(seed=0):
    out = dict(first_inputs(seed))
    for name, value in second_inputs(seed + 1).items():
        if name != "x":
            out[name + "_2"] = value
    return out


def reference(
    x, ln_in_g, ln_in_b, w_in, qn_g, kn_g, sink, gn_a_g, gn_b_g, w_o, ln1_g, ln1_b, peer_wq,
    peer_keys, peer_u, peer_v, ln2_g, ln2_b, c_2, ctx_2, c_ctx_2, w_mod_2, b_mod_2,
    norm_mix_pre_2, norm_mix_post_2, norm_ffn_pre_2, norm_ffn_post_2, w_in_2, gdn_conv_2,
    ret_log_decay_2, gdn_a_log_2, gdn_dt_bias_2, ret_gn_w_2, gdn_norm_w_2, w_ret_out_2,
    w_gdn_out_2, w_o_2, w_router_2, router_bias_2, w_gate_2, w_up_2, w_down_2, w_sh_gate_2,
    w_sh_up_2, w_sh_down_2,
):
    x = first_block(
        x, ln_in_g, ln_in_b, w_in, qn_g, kn_g, sink, gn_a_g, gn_b_g, w_o, ln1_g, ln1_b, peer_wq,
        peer_keys, peer_u, peer_v, ln2_g, ln2_b,
    )
    return second_block(
        x, c_2, ctx_2, c_ctx_2, w_mod_2, b_mod_2, norm_mix_pre_2, norm_mix_post_2,
        norm_ffn_pre_2, norm_ffn_post_2, w_in_2, gdn_conv_2, ret_log_decay_2, gdn_a_log_2,
        gdn_dt_bias_2, ret_gn_w_2, gdn_norm_w_2, w_ret_out_2, w_gdn_out_2, w_o_2, w_router_2,
        router_bias_2, w_gate_2, w_up_2, w_down_2, w_sh_gate_2, w_sh_up_2, w_sh_down_2,
    )


_drawn_inputs = setup_inputs


def setup_inputs(seed=0):
    import zlib

    import numpy as np

    out = dict(_drawn_inputs(seed))
    spreads = {}
    factors = {'qn_g': 5.567,
     'kn_g': 4.302,
     'sink': 8.0,
     'gn_a_g': 3.649,
     'gn_b_g': 3.804,
     'norm_mix_post_2': 4.389,
     'norm_ffn_post_2': 6.248,
     'ret_gn_w_2': 5.081,
     'gdn_norm_w_2': 3.755}
    for name, (base, spread) in spreads.items():
        noise = np.random.default_rng([zlib.crc32(name.encode()), seed]).standard_normal(out[name].shape)
        drawn = base * np.exp(spread * noise) if base else spread * noise
        out[name] = jnp.asarray(drawn.astype(out[name].dtype))
    for name, factor in factors.items():
        out[name] = (out[name] * factor).astype(out[name].dtype)
    return out
```

```python
import concourse.bass as bass
from concourse import mybir
from contextlib import ExitStack

P = 128
ALU = mybir.AluOpType
ACT = mybir.ActivationFunctionType
F32 = mybir.dt.float32
U32 = mybir.dt.uint32
AX = mybir.AxisListType.X

T, D, NC_ = 256, 1024, 2
LAYERS = 2
NEXP = 16384
ALPHA = (2.0 * LAYERS) ** 0.25
RING = 20
ARENA = 22528


class Queue:

    def __init__(self, name, sem, chained):
        self.name, self.sem, self.chained = name, sem, chained
        self.items, self.n, self.pending = [], 0, []

    @property
    def now(self):
        return (self.sem, self.n)

    def op(self, emit, after=(), inc=True, chain=True):
        waits = [a.now if isinstance(a, Queue) else a for a in after] + self.pending
        self.pending = []
        if self.chained and chain and self.n:
            waits.append(self.now)
        if inc:
            self.n += 1
        self.items.append((emit, waits, self.sem if inc else None, 1))
        return self.now

    def hold_for(self, *producers):
        self.pending += [a.now if isinstance(a, Queue) else a for a in producers]

    def dma(self, emit, after, sem):
        self.items.append((emit, after, sem, 16))

    def play(self, eng):
        seen = {}

        def wait(w):
            if isinstance(w, Slot):
                for x in w.released:
                    wait(x)
                return
            s, v = w
            if v and seen.get(s.num, 0) < v:
                seen[s.num] = v
                eng.wait_ge(s, v)

        for emit, waits, sem, by in self.items:
            for w in waits:
                wait(w)
            ins = emit(eng)
            if sem is not None:
                ins.then_inc(sem, by)


class Slot:

    def __init__(self, ap, first):
        self.ap, self.first, self.ready, self.released = ap, first, None, []

    def free(self, *tokens):
        self.released.extend(tokens)


def build(nc, d, out, dump=None, stop=None):
    import numpy as np
    ctx = ExitStack()
    with ctx:
        def sb(name, n, dt=F32):
            return ctx.enter_context(nc.sbuf_tensor(name, [P, n], dt))

        def sem(name):
            return ctx.enter_context(nc.semaphore(name))

        y_dram = out.rearrange("(c p) n -> p c n", p=P)
        PE = Queue("pe", sem("s_pe"), False)
        V = Queue("v", sem("s_v"), True)
        A = Queue("a", sem("s_a"), True)
        G = Queue("g", sem("s_g"), True)
        SP = Queue("sp", sem("s_sp"), False)
        s_small = sem("s_small")
        s_out = sem("s_out")
        ring_sems = [sem(f"s_r{i}") for i in range(RING)]
        gath_sems = [sem(f"s_g{i}") for i in range(RING)]
        ring_count, gath_count = [0] * RING, [0] * RING

        h_sb = sb("h", 2048)
        hT_sb = sb("hT", 2048)
        ring = sb("ring", RING * 1024)
        arena = sb("arena", ARENA)
        cst = sb("cst", CONST_COLS)
        small = sb("small", 1000)
        idx_u = sb("idx_u", 256, U32)
        banks = [ctx.enter_context(nc.psum_tensor(f"ps{i}", [P, 512], F32)) for i in range(8)]

        h = h_sb[:, :].rearrange("p (c n) -> p c n", c=2)
        hT = hT_sb[:, :].rearrange("p (k t) -> p k t", k=8)

        def C(name):
            o, n = CONST_AT[name]
            return cst[:, o:o + n]

        ident = C("ident")

        small_at = [0]

        def sm(n):
            o = small_at[0]
            small_at[0] += n
            assert small_at[0] <= 1000
            return small[:, o:o + n]

        owners = [None] * RING
        rpos = [0]

        def take(k, sems=None, count=None):
            sems, count = sems or ring_sems, count or ring_count
            if rpos[0] % RING + k > RING:
                rpos[0] += RING - rpos[0] % RING
            s = rpos[0] % RING
            rpos[0] += k
            slot = Slot(ring[:, s * 1024:(s + k) * 1024], s)
            before = []
            for i in range(s, s + k):
                if owners[i] is not None and owners[i] not in before:
                    before.append(owners[i])
                owners[i] = slot
            count[s] += 16
            slot.ready = (sems[s], count[s])
            return slot, before

        def load(src, k=None):
            n = src.shape[-1]
            k = k or -(-n // 1024)
            slot, before = take(k)
            dst = slot.ap[:, 0:n]
            SP.dma(lambda e: e.dma_start(dst, src), before, ring_sems[slot.first])
            return slot

        def load_row(name, row):
            src = d[name][row:row + 1, :].to_broadcast([P, d[name].shape[1]])
            return load(src)

        bank_slots = [Slot(b, i) for i, b in enumerate(banks)]
        bpos = [0]
        held = set()

        def bank():
            while bpos[0] % 8 in held:
                bpos[0] += 1
            i = bpos[0] % 8
            bpos[0] += 1
            new = Slot(banks[i], i)
            new.before = bank_slots[i]
            bank_slots[i] = new
            return new

        def mm(b, o, lhsT, rhs, start=True, stop=True, after=(), last=False):
            return PE.op(lambda e: e.matmul(o, lhsT, rhs, start=start, stop=stop, skip_group_check=True),
                         (b.before, *after), inc=last)

        def tr(b, o, src, after=(), last=False):
            return PE.op(lambda e: e.transpose(o, src, ident), (b.before, *after), inc=last)

        def tt(q, o, a, b, op, after=(), **k):
            return q.op(lambda e: e.tensor_tensor(o, a, b, op), after, **k)

        def ts(q, o, a, s1, s2, op0, op1, after=(), **k):
            if op1 is None:
                return q.op(lambda e: e.tensor_scalar(o, a, s1, None, op0), after, **k)
            return q.op(lambda e: e.tensor_scalar(o, a, s1, s2, op0, op1), after, **k)

        def stt(o, a, s, b, op0, op1, after=(), **k):
            return V.op(lambda e: e.scalar_tensor_tensor(out=o, in0=a, scalar=s, in1=b, op0=op0, op1=op1), after, **k)

        def rsqrt(o, a, scale, eps, after=()):
            ts(V, o, a, scale, eps, ALU.mult, ALU.add, after)
            n = o.shape[-1]
            t = tt(G, o, o, C("mhalf")[:, 0:n], ALU.pow, (V,))
            V.hold_for(t)
            return t

        def red(o, a, op=ALU.add, after=()):
            return V.op(lambda e: e.tensor_reduce(o, a, AX, op), after)

        def act(o, a, f, after=(), **k):
            return A.op(lambda e: e.activation(o, a, f, **k), after)

        def cp(q, o, a, after=()):
            if q is A:
                return A.op(lambda e: e.activation(o, a, ACT.Copy), after)
            return q.op(lambda e: e.tensor_copy(o, a), after)

        def bc(a, axis, n):
            u = a.unsqueeze(axis)
            s = list(u.shape)
            s[axis] = n
            return u.to_broadcast(s)

        def heads(a, n):
            return a.rearrange("p (h x) -> p h x", h=n)

        def show(name, ap, after):
            if dump is not None:
                n = 1
                for x in ap.shape[1:]:
                    n *= x
                o = dump(name, [P] + list(ap.shape[1:]))
                SP.dma(lambda e: e.dma_start(o, ap), [a.now if isinstance(a, Queue) else a for a in after], s_out)
                n_out[0] += 16

        n_out = [0]

        SP.dma(lambda e: e.dma_start(cst[:, :], d["consts"]), [], s_small)
        SP.dma(lambda e: e.dma_start(h, d["x"].rearrange("(c p) n -> p c n", p=P)), [], s_small)
        smalls = {}
        n_small = 32
        for name in ("qn_g", "kn_g", "sink", "a_log", "dt_bias", "ret_decay"):
            n = d[name].shape[1]
            smalls[name] = sm(n)
            SP.dma(lambda e, o=smalls[name], s=d[name].to_broadcast([P, n]): e.dma_start(o, s), [], s_small)
            n_small += 16
        for name in ("b_mod", "cvec", "conv", "norm_cols", "router_bias"):
            if name == "router_bias":
                continue
            n = d[name].shape[1]
            smalls[name] = sm(n)
            SP.dma(lambda e, o=smalls[name], s=d[name]: e.dma_start(o, s), [], s_small)
            n_small += 16
        loaded = (s_small, n_small)

        st = {n: sm(8) for n in ("sum", "ss", "rs")}
        first = [loaded]

        def transpose_to(dst, src_of, nk, after, affine=None):
            for c in range(2):
                for k0 in range(0, nk, 4):
                    b = bank()
                    for j in range(4):
                        t = tr(b, b.ap[:, j * P:(j + 1) * P], src_of(c, k0 + j), after, last=(j == 3))
                    if affine is None:
                        q = (V, A)[(k0 // 4) % 2]
                        b.free(cp(q, dst[:, k0:k0 + 4, c * P:(c + 1) * P], b.ap[:, :].rearrange("p (k t) -> p k t", k=4),
                                  (PE,)))
                    else:
                        for j in range(4):
                            s1, s2 = affine(k0 + j)
                            u = ts(V, dst[:, k0 + j, c * P:(c + 1) * P], b.ap[:, j * P:(j + 1) * P], s1, s2,
                                   ALU.mult, ALU.add, (PE,))
                        b.free(u)

        def token_mm(xT, w, n, take_out, after, nk=8, woff=0, wstride=512):
            wv = w.ap
            for c in range(2):
                b = bank()
                for k in range(nk):
                    mm(b, b.ap[:, 0:n], xT[:, k, c * P:(c + 1) * P], wv[:, woff + k * wstride:woff + k * wstride + n],
                       k == 0, k == nk - 1, (w.ready, *after), last=(k == nk - 1))
                b.free(take_out(c, b.ap[:, 0:n]))

        def feat_mm(xT, w, m, o, b, after):
            for k in range(8):
                t = mm(b, o, w.ap[:, k * 512 + m * P:k * 512 + (m + 1) * P], xT[:, k, :],
                       k == 0, k == 7, (w.ready, *after), last=(k == 7))
            return t

        def layer_norm(g, b, scratch, after=()):
            for c in range(2):
                x, y = h[:, c, :], scratch[:, c, :]
                red(st["sum"][:, c:c + 1], x, after=(A, G, *after))
                ts(V, st["sum"][:, c:c + 1], st["sum"][:, c:c + 1], -1.0 / D, None, ALU.mult, None)
                ts(V, x, x, st["sum"][:, c:c + 1], None, ALU.add, None)
                act(y, x, ACT.Square, (V,), accum_out=st["ss"][:, c:c + 1])
                rsqrt(st["rs"][:, c:c + 1], st["ss"][:, c:c + 1], 1.0 / D, 1e-5, (A,))
                stt(x, x, st["rs"][:, c:c + 1], g.ap, ALU.mult, ALU.mult, (g.ready,))
                tt(V, x, x, b.ap, ALU.add, (b.ready,))
            g.free(V.now)
            b.free(V.now)

        def ar(o, n):
            assert o + n <= ARENA
            return arena[:, o:o + n]

        V.op(lambda e: e.memset(st["sum"], 0.0), (loaded,))
        PE.op(lambda e: e.transpose(banks[0][:, 0:P], ident, ident), (loaded,), inc=True)
        A.op(lambda e: e.activation(st["ss"], st["sum"], ACT.Copy), (loaded, V))
        G.op(lambda e: e.memset(st["rs"], 0.0), (loaded,))
        bank_slots[0].free(PE.now)
        lnscr = ar(0, 2048).rearrange("p (c n) -> p c n", c=2)
        g0, b0 = load_row("rows", 0), load_row("rows", 1)
        layer_norm(g0, b0, lnscr)

        def attention(l):
            proj = ar(0, 3072).rearrange("p (c n) -> p c n", c=2)
            qkT = ar(3072, 5120).rearrange("p (i t) -> p i t", i=20)
            S = ar(8192, 2048)
            PT = ar(10240, 2048)
            mix = ar(12288, 2048).rearrange("p (c n) -> p c n", c=2)
            rot = ar(14336, 1280).rearrange("p (c n) -> p c n", c=2)
            tmp = ar(15616, 2048)
            scr = ar(17664, 2048).rearrange("p (c n) -> p c n", c=2)
            ss, rs, mx, den, snk = (asm[n] for n in ("ss", "rs", "mx", "den", "snk"))
            w = [load(d["w_in"][l, i]) for i in range(3)]
            transpose_to(hT, lambda c, k: h[:, c, k * P:(k + 1) * P], 8, (V, A, G))
            for i in range(3):
                def out(c, ps, i=i):
                    return cp((V, A)[(i + c) % 2], proj[:, c, i * 512:(i + 1) * 512], ps, (PE,))
                token_mm(hT, w[i], 512, out, (V, A))
                w[i].free(PE.now)
            cos, sin = C("cos1"), C("sin1")
            for c in range(2):
                x, r = proj[:, c, 0:640], rot[:, c, :]
                tt(V, tmp[:, 0:640], x, x, ALU.mult, (A, PE))
                red(ss[:, 0:10], heads(tmp[:, 0:640], 10))
                rsqrt(rs[:, 0:10], ss[:, 0:10], 1.0 / 64, 1e-6)
                tt(V, heads(x, 10), heads(x, 10), bc(rs[:, 0:10], 2, 64), ALU.mult)
                tt(V, heads(x[:, 0:512], 8), heads(x[:, 0:512], 8),
                   bc(smalls["qn_g"][:, l * 64:(l + 1) * 64], 1, 8), ALU.mult)
                tt(V, heads(x[:, 512:640], 2), heads(x[:, 512:640], 2),
                   bc(smalls["kn_g"][:, l * 64:(l + 1) * 64], 1, 2), ALU.mult)
                xv = x.rearrange("p (h a w f) -> p h a w f", h=10, a=2, w=2)
                rv = r.rearrange("p (h a w f) -> p h a w f", h=10, a=2, w=2)
                tv = tmp[:, 0:320].rearrange("p (h a f) -> p h a f", h=10, a=2)
                tg = tmp[:, 1024:1344].rearrange("p (h a f) -> p h a f", h=10, a=2)
                cc = bc(cos[:, c * 32:(c + 1) * 32].rearrange("p (a f) -> p a f", a=2), 1, 10)
                sn = bc(sin[:, c * 32:(c + 1) * 32].rearrange("p (a f) -> p a f", a=2), 1, 10)
                x1, x2 = xv[:, :, :, 0, :], xv[:, :, :, 1, :]
                tt(V, rv[:, :, :, 0, :], x1, cc, ALU.mult)
                tt(G, tg, x1, sn, ALU.mult, (V,))
                tt(V, tv, x2, sn, ALU.mult)
                tt(G, rv[:, :, :, 1, :], x2, cc, ALU.mult)
                tt(V, rv[:, :, :, 0, :], rv[:, :, :, 0, :], tv, ALU.subtract)
                tt(G, rv[:, :, :, 1, :], rv[:, :, :, 1, :], tg, ALU.add)
                V.hold_for(G)
            for c in range(2):
                for i0 in range(0, 20, 4):
                    b = bank()
                    for j in range(4):
                        i = i0 + j
                        src = rot[:, c, i * 64:(i + 1) * 64] if i < 10 else proj[:, c, 128 + i * 64:192 + i * 64]
                        tr(b, b.ap[0:64, j * P:(j + 1) * P], src, (V, G, A), last=(j == 3))
                    b.free(cp((V, A)[(i0 // 4) % 2], qkT[0:64, i0:i0 + 4, c * P:(c + 1) * P],
                              b.ap[0:64, :].rearrange("p (k t) -> p k t", k=4), (PE,)))
            for br in range(2):
                voff = 640 if br == 0 else 1408
                for c in range(2):
                    dist, mask = C("dist")[:, c * 256:(c + 1) * 256], C("mask")[:, c * 256:(c + 1) * 256]
                    for k in range(4):
                        b = bank()
                        for hd in (2 * k, 2 * k + 1):
                            mm(b, b.ap[:, (hd % 2) * 256:(hd % 2) * 256 + 256],
                               qkT[0:64, br * 10 + hd, c * P:(c + 1) * P],
                               qkT[0:64, br * 10 + 8 + hd // 4, :], after=(V, A), last=(hd % 2 == 1))
                        if br == 0:
                            u = ts(V, S[:, k * 512:(k + 1) * 512], b.ap[:, :], 0.125, None, ALU.mult, None, (PE,))
                        else:
                            for hd in (2 * k, 2 * k + 1):
                                tm = tmp[:, hd * 256:hd * 256 + 256]
                                slope = float(np.float32(2.0 ** (-(hd + 1.0))))
                                stt(tm, dist, -slope, mask, ALU.mult, ALU.add, (A,))
                                u = stt(S[:, hd * 256:hd * 256 + 256], b.ap[:, (hd % 2) * 256:(hd % 2) * 256 + 256],
                                        0.125, tm, ALU.mult, ALU.add, (PE,))
                        b.free(u)
                    Sv = heads(S, 8)
                    red(mx, Sv, ALU.max)
                    if br == 1:
                        tt(V, mx, mx, smalls["sink"][:, l * 8:(l + 1) * 8], ALU.max)
                        tt(V, snk, smalls["sink"][:, l * 8:(l + 1) * 8], mx, ALU.subtract)
                    tt(V, Sv, Sv, bc(mx, 2, 256), ALU.subtract)
                    act(S, S, ACT.Exp, (V,))
                    if br == 1:
                        act(snk, snk, ACT.Exp)
                    red(den, Sv, after=(A,))
                    if br == 1:
                        tt(V, den, den, snk, ALU.add)
                    V.op(lambda e: e.reciprocal(den, den))
                    for i0 in range(0, 16, 4):
                        b = bank()
                        for j in range(4):
                            i = i0 + j
                            tr(b, b.ap[:, j * P:(j + 1) * P], S[:, i * P:(i + 1) * P], (A, V), last=(j == 3))
                        b.free(cp((V, A)[(i0 // 4) % 2], PT[:, i0 * P:(i0 + 4) * P], b.ap[:, :], (PE,)))
                    b = bank()
                    for hd in range(8):
                        g = hd // 4
                        for s in range(2):
                            mm(b, b.ap[:, hd * 64:(hd + 1) * 64], PT[:, (hd * 2 + s) * P:(hd * 2 + s + 1) * P],
                               proj[:, s, voff + g * 64:voff + (g + 1) * 64], s == 0, s == 1, (V, A),
                               last=(hd == 7 and s == 1))
                    b.free(tt(V, heads(mix[:, c, br * 512:(br + 1) * 512], 8), heads(b.ap[:, :], 8),
                              bc(den, 2, 64), ALU.mult, (PE,)))
            w = [load(d["w_o"][l, i]) for i in range(2)]
            gn = load_row("rows", 2 + 5 * l)
            for c in range(2):
                m = mix[:, c, :]
                tt(V, tmp[:, 0:1024], m, m, ALU.mult, (PE,))
                red(ss, heads(tmp[:, 0:1024], 16))
                rsqrt(rs, ss, 1.0 / 64, 1e-6)
                tt(V, heads(m, 16), heads(m, 16), bc(rs, 2, 64), ALU.mult)
                tt(V, m, m, gn.ap, ALU.mult, (gn.ready,))
            gn.free(V.now)
            transpose_to(hT, lambda c, k: mix[:, c, k * P:(k + 1) * P], 8, (V, PE))
            for i in range(2):
                def out(c, ps, i=i):
                    x = h[:, c, i * 512:(i + 1) * 512]
                    return stt(x, x, ALPHA, ps, ALU.mult, ALU.add, (PE,))
                token_mm(hT, w[i], 512, out, (V, A))
                w[i].free(PE.now)
            g1, b1 = load_row("rows", 3 + 5 * l), load_row("rows", 4 + 5 * l)
            layer_norm(g1, b1, scr)

        def peer(l):
            qT = ar(0, 4096).rearrange("p (m t) -> p m t", m=16)
            SC = ar(4096, 2048)
            SC2 = ar(6144, 2048)
            OH = ar(8192, 2048)
            junk = ar(10240, 1024)
            accs = ar(11264, 2048).rearrange("p (c n) -> p c n", c=2)
            v16 = ar(13312, 256)
            i16u = iu[:, 0:256]
            i16 = ar(13568, 256)
            tsv = ar(13824, 128)
            pf1 = ar(13952, 128)
            pf2 = ar(14080, 128)
            e1 = ar(14208, 128)
            e2 = ar(14336, 128)
            gs = ar(14464, 256)
            aa = ar(14720, 256)
            wgt = ar(14976, 256)
            scr = ar(17664, 2048).rearrange("p (c n) -> p c n", c=2)
            w = [load(d["peer_wq"][l, i]) for i in range(4)]
            kt = load(d["peer_keys"][l])
            transpose_to(hT, lambda c, k: h[:, c, k * P:(k + 1) * P], 8, (V, A, G))
            for i in range(4):
                for m0 in range(0, 4, 2):
                    b = bank()
                    for m in (m0, m0 + 1):
                        feat_mm(hT, w[i], m, b.ap[:, (m - m0) * 256:(m - m0) * 256 + 256], b, (V, A))
                    b.free(cp((V, A)[(m0 // 2) % 2], qT[:, i * 4 + m0:i * 4 + m0 + 2, :],
                              b.ap[:, :].rearrange("p (m t) -> p m t", m=2), (PE,)))
                w[i].free(PE.now)
            i_ready = []
            for c in range(2):
                for j in range(4):
                    b = bank()
                    for m in range(4):
                        hp = 4 * j + m
                        mm(b, b.ap[:, m * P:(m + 1) * P], qT[:, hp, c * P:(c + 1) * P],
                           kt.ap[:, hp * P:(hp + 1) * P], after=(kt.ready, V, A), last=(m == 3))
                    b.free(cp((V, A)[j % 2], SC[:, j * 512:(j + 1) * 512], b.ap[:, :], (PE, V)))
                V.hold_for(A, G)
                for grp, n, vals, ids, src, alt in ((16, P, v16, i16u, SC, SC2),):
                    topk(grp, n, vals, ids, src, alt)
                cp(V, i16, i16u)
                v4 = v16.rearrange("p (h s k) -> p h s k", h=8, s=2)
                i4 = i16.rearrange("p (h s k) -> p h s k", h=8, s=2)
                cand = SC.rearrange("p (h a b) -> p h a b", h=8, a=16)
                tt(V, cand, bc(v4[:, :, 0, :], 3, 16), bc(v4[:, :, 1, :], 2, 16), ALU.add)
                pos = iu[:, 256:384]
                topk(8, 256, tsv, pos, SC, SC2)
                pu = iu[:, 384:512]
                ts(V, pu, pos, 4, None, ALU.logical_shift_right, None)
                cp(V, pf1, pu)
                ts(V, pu, pos, 15, None, ALU.bitwise_and, None)
                cp(V, pf2, pu)
                for s, pf, ee in ((0, pf1, e1), (1, pf2, e2)):
                    tt(V, OH.rearrange("p (s k) -> p s k", k=16), bc(C("iota16"), 1, 128), bc(pf, 2, 16), ALU.is_equal)
                    o4 = OH.rearrange("p (h s k) -> p h s k", h=8, s=16)
                    tt(V, o4, o4, bc(i4[:, :, s, :], 2, 16), ALU.mult)
                    red(ee, OH.rearrange("p (s k) -> p s k", k=16))
                stt(e1, e1, 128.0, e2, ALU.mult, ALU.add)
                ts(V, e1, e1, float(l * NEXP), None, ALU.add, None)
                i_ready.append(cp(V, idx_u[:, c * P:(c + 1) * P], e1, (G,)))
                g = gs[:, c * P:(c + 1) * P]
                t3 = heads(tsv, 8)
                tt(V, heads(g, 8), t3, t3[:, :, 0:1].to_broadcast([P, 8, 16]), ALU.subtract)
                act(g, g, ACT.Exp, (V,))
                red(st["sum"], heads(g, 8), after=(A,))
                V.op(lambda e: e.reciprocal(st["sum"], st["sum"]))
                tt(V, heads(g, 8), heads(g, 8), bc(st["sum"], 2, 16), ALU.mult)
            kt.free(PE.now)
            if dump is not None:
                show(f"eidx{l}", idx_u[:, :], (V,))

            def gather(table, c, s):
                slot, before = take(1, gath_sems, gath_count)
                G.dma(lambda e: e.indirect_dma_start(
                    out=slot.ap, out_offset=None, in_=d[table],
                    in_offset=bass.IndirectOffsetOnAxis(ap=idx_u[:, c * P + s:c * P + s + 1], axis=0)),
                    [i_ready[c], *before], gath_sems[slot.first])
                return slot

            V.op(lambda e: e.memset(accs, 0.0), (A,))
            pend = []

            def dots(c, s, slot):
                slot.free(V.op(lambda e: e.tensor_tensor_reduce(
                    out=junk, in0=slot.ap, in1=h[:, c, :], scale=1.0, scalar=0.0, op0=ALU.mult, op1=ALU.add,
                    accum_out=aa[:, c * P + s:c * P + s + 1]), (slot.ready,)))

            def sums(c, s, slot):
                slot.free(stt(accs[:, c, :], slot.ap, wgt[:, c * P + s:c * P + s + 1], accs[:, c, :],
                              ALU.mult, ALU.add, (slot.ready,)))

            for table, use in (("peer_u", dots), ("peer_v", sums)):
                for c in range(2):
                    if use is sums:
                        tt(V, wgt[:, c * P:(c + 1) * P], wgt[:, c * P:(c + 1) * P], gs[:, c * P:(c + 1) * P],
                           ALU.mult, (A,))
                    for s in range(P):
                        use(c, s, gather(table, c, s))
                    if use is dots:
                        act(wgt[:, c * P:(c + 1) * P], aa[:, c * P:(c + 1) * P], ACT.Gelu, (V,))
            for c in range(2):
                stt(h[:, c, :], h[:, c, :], ALPHA, accs[:, c, :], ALU.mult, ALU.add)
            g2, b2 = load_row("rows", 5 + 5 * l), load_row("rows", 6 + 5 * l)
            layer_norm(g2, b2, scr)

        def topk(groups, n, vals, ids, src, alt):
            for i in range(groups):
                x, y = src[:, i * n:(i + 1) * n], alt[:, i * n:(i + 1) * n]
                a, b = vals[:, i * 16:i * 16 + 8], vals[:, i * 16 + 8:i * 16 + 16]
                ia, ib = ids[:, i * 16:i * 16 + 8], ids[:, i * 16 + 8:i * 16 + 16]
                V.op(lambda e, a=a, x=x: e.max(out=a, in_=x))
                V.op(lambda e, a=a, x=x, ia=ia: e.max_index(ia, a, x))
                V.op(lambda e, a=a, x=x, y=y: e.match_replace(out=y, in_to_replace=a, in_values=x, imm_value=-3e38),
                     chain=False)
                V.op(lambda e, b=b, y=y: e.max(out=b, in_=y))
                V.op(lambda e, b=b, y=y, ib=ib: e.max_index(ib, b, y))

        def second():
            Rk = ar(0, 1024).rearrange("p (c n) -> p c n", c=2)
            Rv = ar(1024, 1024).rearrange("p (c n) -> p c n", c=2)
            Rq = ar(2048, 1024).rearrange("p (c n) -> p c n", c=2)
            RkT = ar(3072, 1024).rearrange("p (k t) -> p k t", k=4)
            RqT = ar(4096, 1024).rearrange("p (k t) -> p k t", k=4)
            GG = ar(5120, 3072).rearrange("p (a c n) -> p a c n", a=3, c=2)
            GkT = ar(8192, 1024).rearrange("p (k t) -> p k t", k=4)
            GqT = ar(9216, 1024).rearrange("p (k t) -> p k t", k=4)
            Oret = ar(10240, 1024).rearrange("p (c n) -> p c n", c=2)
            Ogdn = ar(11264, 1024).rearrange("p (c n) -> p c n", c=2)
            S4 = ar(12288, 2048).rearrange("p (s n) -> p s n", s=4)
            Tm = lambda i: ar(14336 + 512 * i, 512)
            sc8 = {n: sm(8) for n in ("lasp", "e1", "e2", "ea", "eg", "ekt")}
            la = sm(16).rearrange("p (c n) -> p c n", c=2)
            be = sm(16).rearrange("p (c n) -> p c n", c=2)
            gc = sm(4)
            dec = sm(8)
            cd = sm(8)
            modT, cmT = sm(48), sm(16)
            gsx, gsc, gs2 = sm(8), sm(8), sm(8)
            t16 = sm(16)
            cs = sm(16)

            def silu_small(o, x, tmp):
                act(tmp, x, ACT.Sigmoid, (V,))
                tt(V, o, x, tmp, ALU.mult, (A,))

            silu_small(cs, smalls["cvec"], t16)
            csv = cs.rearrange("p (k s) -> p k s", k=8)
            b = bank()
            for i in range(12):
                w = load(d["w_mod"][i])
                for m in range(4):
                    j = 4 * i + m
                    for k in range(8):
                        mm(b, b.ap[:, 2 * j:2 * j + 2], w.ap[:, k * 512 + m * P:k * 512 + (m + 1) * P],
                           csv[:, k, :], k == 0, k == 7, (w.ready, V), last=(k == 7))
                w.free(PE.now)
            pv = b.ap[:, 0:96].rearrange("p (j s) -> p j s", s=2)
            tt(V, modT, pv[:, :, 0], smalls["b_mod"], ALU.add, (PE,))
            b.free(tt(V, cmT, pv[:, 0:16, 1], smalls["b_mod"][:, 0:16], ALU.add))
            nm = smalls["norm_cols"]
            for o, s, g in ((gsx, modT[:, 8:16], nm[:, 0:8]), (gsc, cmT[:, 8:16], nm[:, 0:8]),
                            (gs2, modT[:, 32:40], nm[:, 8:16])):
                stt(o, s, 1.0, g, ALU.add, ALU.mult)
            ea = sc8["ea"]
            act(ea, smalls["a_log"], ACT.Exp, (V,))
            rd = smalls["ret_decay"]
            act(cd, rd, ACT.Exp, (V,), scale=128.0)
            rel, col = C("rel"), C("col")
            Dret = Tm(15)
            cst_f = sm(8)
            for hd in range(4):
                o = Dret[:, hd * P:(hd + 1) * P]
                t1, t2 = Tm(0)[:, 0:P], Tm(0)[:, P:2 * P]
                ts(V, t1, rel, 0.0, None, ALU.max, None, (A, PE))
                ts(V, t2, rel, -1.0, 0.0, ALU.mult, ALU.max)
                act(t1, t1, ACT.Exp, (V,), scale=rd[:, hd:hd + 1])
                act(t2, t2, ACT.Exp, (V,), scale=rd[:, 4 + hd:5 + hd])
                tt(V, t1, t1, C("triF"), ALU.mult, (A,))
                tt(V, t2, t2, C("triB"), ALU.mult)
                tt(V, o, t1, t2, ALU.add)
            ts(V, cst_f[:, 0:1], col, -1.0, 127.0, ALU.mult, ALU.add)
            ts(V, dec[:, 0:4], rd[:, 0:4], cst_f[:, 0:1], None, ALU.mult, None)
            ts(V, dec[:, 4:8], rd[:, 4:8], col, None, ALU.mult, None)
            act(dec, dec, ACT.Exp, (V,))
            V.hold_for(A)

            def rms_rows(dst, src, n, after=()):
                for c in range(2):
                    act(dst[:, c, :], src[:, c, :], ACT.Square, (V, PE, *after), accum_out=st["ss"][:, c:c + 1])
                rsqrt(st["rs"][:, 0:2], st["ss"][:, 0:2], 1.0 / n, 1e-6, (A,))

            def normed(src, gcol, shift, xn):
                rms_rows(xn, src, D)
                for c in range(2):
                    ts(V, xn[:, c, :], src[:, c, :], st["rs"][:, c:c + 1], None, ALU.mult, None)
                transpose_to(hT, lambda c, k: xn[:, c, k * P:(k + 1) * P], 8, (V, PE),
                             affine=lambda k: (gcol[:, k:k + 1], shift[:, k:k + 1]))

            def features(x_side):
                n_conv = 3 if x_side else 2
                raw, cv = ar(14336, 1024), ar(15360, 1024)
                scr2 = ar(16384, 1024)
                if x_side:
                    for dst, i, s in ((Rk, 0, P ** -0.5), (Rv, 1, 1.0), (Rq, 4, 1.0)):
                        w = load(d["w_in2"][i])

                        def out(c, ps, dst=dst, s=s):
                            return ts(V, dst[:, c, :], ps, s, None, ALU.mult, None, (PE,))
                        token_mm(hT, w, 512, out, (V, A))
                        w.free(PE.now)
                    cos, sin = C("cos2"), C("sin2")
                    for R in (Rk, Rq):
                        for c in range(2):
                            xv = R[:, c, :].rearrange("p (h w f) -> p h w f", h=4, w=2)
                            cc, sn = bc(cos[:, c * 64:(c + 1) * 64], 1, 4), bc(sin[:, c * 64:(c + 1) * 64], 1, 4)
                            q = [scr2[:, 256 * j:256 * (j + 1)].rearrange("p (h f) -> p h f", h=4) for j in range(4)]
                            tt(V, q[0], xv[:, :, 0, :], cc, ALU.mult, (A, PE))
                            tt(V, q[1], xv[:, :, 1, :], sn, ALU.mult)
                            tt(V, q[2], xv[:, :, 0, :], sn, ALU.mult)
                            tt(V, q[3], xv[:, :, 1, :], cc, ALU.mult)
                            tt(V, xv[:, :, 0, :], q[0], q[1], ALU.subtract)
                            tt(V, xv[:, :, 1, :], q[2], q[3], ALU.add)
                    transpose_to(RkT, lambda c, k: Rk[:, c, k * P:(k + 1) * P], 4, (V,))
                    transpose_to(RqT, lambda c, k: Rq[:, c, k * P:(k + 1) * P], 4, (V,))
                else:
                    for dst, i, s in ((Rk, 0, P ** -0.5), (Rv, 1, 1.0)):
                        w = load(d["w_in2"][i])

                        def out(c, ps, dst=dst, s=s):
                            return ts(V, dst[:, c, :], ps, s, None, ALU.mult, None, (PE,))
                        token_mm(hT, w, 512, out, (V, A))
                        w.free(PE.now)
                w = load(d["w_gab"], 1)
                dtb = smalls["dt_bias"]

                def out(c, ps):
                    e1, e2 = sc8["e1"], sc8["e2"]
                    tt(V, e1, ps[:, 0:8], dtb, ALU.add, (PE, A))
                    u = cp(V, be[:, c, :], ps[:, 8:16])
                    act(be[:, c, :], be[:, c, :], ACT.Sigmoid, (V,))
                    act(e2, e1, ACT.Abs)
                    act(e2, e2, ACT.Exp, scale=-1.0)
                    act(e2, e2, ACT.Ln, bias=1.0)
                    stt(e1, e1, 0.0, e2, ALU.max, ALU.add, (A,))
                    stt(la[:, c, :], e1, -1.0, ea, ALU.mult, ALU.mult)
                    return u
                token_mm(hT, w, 16, out, (V, A), wstride=16)
                w.free(PE.now)
                cw = smalls["conv"].rearrange("p (j f) -> p j f", j=3)
                for a, i, f0 in ((0, 2, 4), (1, 3, 8), (2, 6, 0))[:n_conv]:
                    w = load(d["w_in2"][i])
                    rw = raw.rearrange("p (m t) -> p m t", m=4)
                    cvv = cv.rearrange("p (m t) -> p m t", m=4)
                    for m0 in (0, 2):
                        b = bank()
                        for m in (m0, m0 + 1):
                            feat_mm(hT, w, m, b.ap[:, (m - m0) * 256:(m - m0) * 256 + 256], b, (V, A))
                        b.free(cp(V, rw[:, m0:m0 + 2, :], b.ap[:, :].rearrange("p (m t) -> p m t", m=2), (PE,)))
                    w.free(PE.now)
                    for m in range(4):
                        x, y = rw[:, m, :], cvv[:, m, :]
                        f = f0 + m
                        ts(V, y, x, cw[:, 1, f:f + 1], None, ALU.mult, None, (PE,))
                        stt(y[:, 1:256], x[:, 0:255], cw[:, 0, f:f + 1], y[:, 1:256], ALU.mult, ALU.add)
                        stt(y[:, 0:255], x[:, 1:256], cw[:, 2, f:f + 1], y[:, 0:255], ALU.mult, ALU.add)
                    act(raw, cv, ACT.Sigmoid, (V,))
                    tt(V, cv, cv, raw, ALU.mult, (A,))
                    for c in range(2):
                        b = bank()
                        for m in range(4):
                            tr(b, b.ap[:, m * P:(m + 1) * P], cvv[:, m, c * P:(c + 1) * P], (V,), last=(m == 3))
                        b.free(cp(V, GG[:, a, c, :], b.ap[:, :], (PE,)))
                        if a != 1:
                            x = GG[:, a, c, :]
                            tt(V, scr2[:, 0:512], x, x, ALU.mult)
                            red(st["ss"][:, 0:4], heads(scr2[:, 0:512], 4))
                            rsqrt(st["rs"][:, 0:4], st["ss"][:, 0:4], 1.0, 1e-6)
                            if a == 2:
                                ts(V, st["rs"][:, 0:4], st["rs"][:, 0:4], P ** -0.5, None, ALU.mult, None)
                            tt(V, heads(x, 4), heads(x, 4), bc(st["rs"][:, 0:4], 2, P), ALU.mult)
                    if a != 1:
                        transpose_to(GkT if a == 0 else GqT, lambda c, k, a=a: GG[:, a, c, k * P:(k + 1) * P], 4, (V,))

            def gdn_matrices(c):
                kk = bank()
                for hd in range(4):
                    mm(kk, kk.ap[:, hd * P:(hd + 1) * P], GkT[:, hd, c * P:(c + 1) * P],
                       GkT[:, hd, c * P:(c + 1) * P], after=(V, A), last=(hd == 3))
                kk.free(cp(V, Tm(10), kk.ap[:, :], (PE,)))

            def gdn_chunk(dr, c, x_side):
                tri = C("triF") if dr == 0 else C("triB")
                strict = C("low") if dr == 0 else C("up")
                end = P - 1 if dr == 0 else 0
                GR, Dm, DT, Am, AT, Xm, XT, Pm = (Tm(i) for i in range(8))
                lac = la[:, c, dr * 4:dr * 4 + 4]
                bec = be[:, c, dr * 4:dr * 4 + 4]
                b = bank()
                for hd in range(4):
                    t = cp(V, Pm[:, hd * P:(hd + 1) * P], lac[:, hd:hd + 1].to_broadcast([P, P]), (PE, A))
                for hd in range(4):
                    mm(b, b.ap[:, hd * P:(hd + 1) * P], Pm[:, hd * P:(hd + 1) * P], tri, after=(V, A), last=(hd == 3))
                b.free(cp(V, GR, b.ap[:, :], (PE,)))
                b = bank()
                mm(b, b.ap[:, 0:4], tri, lac, after=(V, A), last=True)
                b.free(cp(V, gc, b.ap[:, 0:4], (PE,)))
                for hd in range(4):
                    s = slice(hd * P, (hd + 1) * P)
                    ts(V, Dm[:, s], GR[:, s], gc[:, hd:hd + 1], 0.0, ALU.subtract, ALU.max)
                    ts(V, DT[:, s], GR[:, s], gc[:, hd:hd + 1], 0.0, ALU.subtract, ALU.min)
                act(Dm, Dm, ACT.Exp, (V,), scale=-1.0)
                act(DT, DT, ACT.Exp)
                ekt, eg = sc8["ekt"][:, 0:4], sc8["eg"][:, 0:4]
                last = heads(GR, 4)[:, :, end:end + 1].rearrange("p h x -> p (h x)")
                tt(V, ekt, last, gc, ALU.subtract)
                act(ekt, ekt, ACT.Exp, (V,))
                act(eg, last, ACT.Exp)
                act(gc, gc, ACT.Exp)
                tt(V, heads(Dm, 4), heads(Dm, 4), bc(strict, 1, 4), ALU.mult, (A,))
                tt(V, heads(DT, 4), heads(DT, 4), bc(tri, 1, 4), ALU.mult)
                tt(V, Am, Tm(10), Dm, ALU.mult)
                tt(V, heads(Am, 4), heads(Am, 4), bc(bec, 2, P), ALU.mult)
                b = bank()
                for hd in range(4):
                    tr(b, b.ap[:, hd * P:(hd + 1) * P], Am[:, hd * P:(hd + 1) * P], (V,), last=(hd == 3))
                b.free(cp(V, AT, b.ap[:, :], (PE,)))
                I4 = bc(ident, 1, 4)
                for Y, Z in ((Xm, Am), (XT, AT)):
                    tt(V, heads(Y, 4), heads(Z, 4), bc(C("lvl0"), 1, 4), ALU.mult)
                    tt(V, heads(Y, 4), I4, heads(Y, 4), ALU.subtract)
                Bm = Dm
                for lv in range(1, 7):
                    tt(V, heads(Bm, 4), heads(AT, 4), bc(C(f"lvl{lv}"), 1, 4), ALU.mult, (PE,))
                    b = bank()
                    for hd in range(4):
                        s = slice(hd * P, (hd + 1) * P)
                        mm(b, b.ap[:, s], Bm[:, s], Xm[:, s], after=(V,), last=(hd == 3))
                    b.free(cp(V, Pm, b.ap[:, :], (PE,)))
                    b2 = bank()
                    for hd in range(4):
                        s = slice(hd * P, (hd + 1) * P)
                        mm(b2, b2.ap[:, s], Pm[:, s], XT[:, s], after=(V,), last=(hd == 3))
                    if lv < 6:
                        b = bank()
                        for hd in range(4):
                            s = slice(hd * P, (hd + 1) * P)
                            mm(b, b.ap[:, s], XT[:, s], Pm[:, s], last=(hd == 3))
                        b.free(tt(V, Xm, Xm, b.ap[:, :], ALU.subtract, (PE,)))
                    b2.free(tt(V, XT, XT, b2.ap[:, :], ALU.subtract, (PE,)))
                Gk, Gv = GG[:, 0, c, :], GG[:, 1, c, :]
                rv, rk, U, WT, vn, kt, qe = Dm, Am, Tm(8), Tm(9), Tm(11), Xm, Tm(12)
                tt(V, heads(rv, 4), heads(Gv, 4), bc(bec, 2, P), ALU.mult, (PE,))
                tt(V, heads(rk, 4), heads(Gk, 4), bc(bec, 2, P), ALU.mult)
                tt(V, heads(rk, 4), heads(rk, 4), bc(gc, 2, P), ALU.mult)
                tt(V, heads(kt, 4), heads(Gk, 4), bc(ekt, 2, P), ALU.mult)
                b = bank()
                for hd in range(4):
                    s = slice(hd * P, (hd + 1) * P)
                    mm(b, b.ap[:, s], XT[:, s], rv[:, s], after=(V,), last=(hd == 3))
                b.free(cp(V, U, b.ap[:, :], (PE,)))
                b = bank()
                for hd in range(4):
                    s = slice(hd * P, (hd + 1) * P)
                    mm(b, b.ap[:, s], rk[:, s], XT[:, s], after=(V,), last=(hd == 3))
                b.free(cp(V, WT, b.ap[:, :], (PE,)))
                S = S4[:, 2 + dr, :]
                b = bank()
                for hd in range(4):
                    s = slice(hd * P, (hd + 1) * P)
                    mm(b, b.ap[:, s], WT[:, s], S[:, s], after=(V,), last=(hd == 3))
                b.free(tt(V, vn, U, b.ap[:, :], ALU.subtract, (PE,)))
                if x_side:
                    kq = bank()
                    for hd in range(4):
                        s = slice(hd * P, (hd + 1) * P)
                        mm(kq, kq.ap[:, s], GkT[:, hd, c * P:(c + 1) * P], GqT[:, hd, c * P:(c + 1) * P],
                           after=(V, A), last=(hd == 3))
                    kq.free(tt(V, DT, DT, kq.ap[:, :], ALU.mult, (PE,)))
                    act(qe, GR, ACT.Exp, (PE, V))
                    tt(V, heads(qe, 4), heads(qe, 4), GqT[:, :, c * P:(c + 1) * P], ALU.mult, (A,))
                    b = bank()
                    for hd in range(4):
                        s = slice(hd * P, (hd + 1) * P)
                        mm(b, b.ap[:, s], DT[:, s], vn[:, s], True, False, (V,))
                        mm(b, b.ap[:, s], qe[:, s], S[:, s], False, True, (V,), last=(hd == 3))
                    b.free(tt(V, Ogdn[:, c, :], Ogdn[:, c, :], b.ap[:, :], ALU.add, (PE,)))
                b = bank()
                for hd in range(4):
                    s = slice(hd * P, (hd + 1) * P)
                    mm(b, b.ap[:, s], kt[:, s], vn[:, s], after=(V,), last=(hd == 3))
                tt(V, heads(S, 4), heads(S, 4), bc(eg, 2, P), ALU.mult, (PE,))
                b.free(tt(V, S, S, b.ap[:, :], ALU.add))

            def ret_chunk(dr, c, x_side):
                S = S4[:, dr, :]
                kd, qe = Tm(13), Tm(14)
                if x_side:
                    for hd in range(4):
                        act(qe[:, hd * P:(hd + 1) * P], C("up1") if dr == 0 else C("down"), ACT.Exp, (PE, V),
                            scale=rd[:, 4 * dr + hd:4 * dr + hd + 1])
                    tt(V, heads(qe, 4), heads(qe, 4), RqT[:, :, c * P:(c + 1) * P], ALU.mult, (A,))
                    b = bank()
                    for hd in range(4):
                        s = slice(hd * P, (hd + 1) * P)
                        mm(b, b.ap[:, s], qe[:, s], S[:, s], after=(V,), last=(hd == 3))
                    b.free(tt(V, Oret[:, c, :], Oret[:, c, :], b.ap[:, :], ALU.add, (PE,)))
                    if dr == 0:
                        b = bank()
                        for hd in range(4):
                            s = slice(hd * P, (hd + 1) * P)
                            mm(b, b.ap[:, s], RkT[:, hd, c * P:(c + 1) * P], RqT[:, hd, c * P:(c + 1) * P],
                               after=(V, A), last=(hd == 3))
                        b.free(tt(V, kd, Dret, b.ap[:, :], ALU.mult, (PE,)))
                        b = bank()
                        for hd in range(4):
                            s = slice(hd * P, (hd + 1) * P)
                            mm(b, b.ap[:, s], kd[:, s], Rv[:, c, s], after=(V,), last=(hd == 3))
                        b.free(tt(V, Oret[:, c, :], Oret[:, c, :], b.ap[:, :], ALU.add, (PE,)))
                tt(V, heads(kd, 4), heads(Rk[:, c, :], 4), bc(dec[:, 4 * dr:4 * dr + 4], 2, P), ALU.mult, (PE,))
                b = bank()
                for hd in range(4):
                    s = slice(hd * P, (hd + 1) * P)
                    mm(b, b.ap[:, s], kd[:, s], Rv[:, c, s], after=(V,), last=(hd == 3))
                tt(V, heads(S, 4), heads(S, 4), bc(cd[:, 4 * dr:4 * dr + 4], 2, P), ALU.mult, (PE,))
                b.free(tt(V, S, S, b.ap[:, :], ALU.add))

            def mixers(x_side):
                for c in range(2):
                    gdn_matrices(c)
                    gdn_chunk(0, c, x_side)
                    ret_chunk(0, c, x_side)
                for c in (1, 0):
                    gdn_matrices(c)
                    gdn_chunk(1, c, x_side)
                    ret_chunk(1, c, x_side)

            V.op(lambda e: e.memset(ar(10240, 4096), 0.0), (A, PE))
            ctx_sb = ar(16384, 2048).rearrange("p (c n) -> p c n", c=2)
            cslot, before = take(2)
            SP.dma(lambda e: e.dma_start(cslot.ap.rearrange("p (c n) -> p c n", c=2),
                                         d["ctx"].rearrange("(c p) n -> p c n", p=P)), before, ring_sems[cslot.first])
            cx = cslot.ap.rearrange("p (c n) -> p c n", c=2)
            A.hold_for(cslot.ready)
            V.hold_for(cslot.ready)
            normed(cx, gsc, cmT[:, 0:8], ctx_sb)
            cslot.free(V.now)
            show("hc", hT_sb[:, :], (V, A))
            features(False)
            mixers(False)
            for i in range(4):
                show(f"init{i}", S4[:, i, :], (V,))
            normed(h, gsx, modT[:, 0:8], ctx_sb)
            show("hx", hT_sb[:, :], (V, A))
            features(True)
            show("rk", Rk, (V,))
            show("gk", GG[:, 0, :, :], (V,))
            show("gq", GG[:, 2, :, :], (V,))
            show("log_a", la, (V,))
            show("beta", be, (A,))
            mixers(True)
            show("ret_x", Oret, (V,))
            show("gdn_x", Ogdn, (V,))

            gt = ar(14336, 4096).rearrange("p (c n) -> p c n", c=2)
            rg = ar(0, 1024).rearrange("p (c n) -> p c n", c=2)
            gz = ar(1024, 1024).rearrange("p (c n) -> p c n", c=2)
            t5 = ar(2048, 512)
            yT = ar(3072, 2048).rearrange("p (k t) -> p k t", k=8)
            mg = ar(5120, 2048).rearrange("p (c n) -> p c n", c=2)
            for dst, i in ((rg, 5), (gz, 7)):
                w = load(d["w_in2"][i])

                def out(c, ps, dst=dst):
                    act(dst[:, c, :], ps, ACT.Sigmoid, (PE, V))
                    return tt(V, dst[:, c, :], dst[:, c, :], ps, ALU.mult, (A,))
                token_mm(hT, w, 512, out, (V, A))
                w.free(PE.now)
            for i in range(4):
                w = load(d["w_in2"][8 + i])

                def out(c, ps, i=i):
                    return act(gt[:, c, i * 512:(i + 1) * 512], ps, ACT.Sigmoid, (PE, V))
                token_mm(hT, w, 512, out, (V, A))
                w.free(PE.now)
            nw = load_row("rows", 12)
            for c in range(2):
                y = Oret[:, c, :]
                red(st["sum"][:, 0:4], heads(y, 4))
                ts(V, st["sum"][:, 0:4], st["sum"][:, 0:4], -1.0 / P, None, ALU.mult, None)
                tt(V, heads(y, 4), heads(y, 4), bc(st["sum"][:, 0:4], 2, P), ALU.add)
                for y, g, o in ((Oret[:, c, :], rg, 0), (Ogdn[:, c, :], gz, 512)):
                    tt(V, t5, y, y, ALU.mult)
                    red(st["ss"][:, 0:4], heads(t5, 4))
                    rsqrt(st["rs"][:, 0:4], st["ss"][:, 0:4], 1.0 / P, 1e-6)
                    tt(V, heads(y, 4), heads(y, 4), bc(st["rs"][:, 0:4], 2, P), ALU.mult)
                    tt(V, y, y, nw.ap[:, o:o + 512], ALU.mult, (nw.ready,))
                    tt(V, y, y, g[:, c, :], ALU.mult)
            nw.free(V.now)
            transpose_to(yT[:, 0:4, :], lambda c, k: Oret[:, c, k * P:(k + 1) * P], 4, (V,))
            transpose_to(yT[:, 4:8, :], lambda c, k: Ogdn[:, c, k * P:(k + 1) * P], 4, (V,))
            for s, name in ((0, "w_ret_out"), (1, "w_gdn_out")):
                w = load(d[name])
                for i in range(2):
                    def out(c, ps, i=i, s=s):
                        g = gt[:, c, s * 1024 + i * 512:s * 1024 + i * 512 + 512]
                        m = mg[:, c, i * 512:(i + 1) * 512]
                        if s == 0:
                            return tt(V, m, g, ps, ALU.mult, (PE, A))
                        u = tt(V, g, g, ps, ALU.mult, (PE, A))
                        tt(V, m, m, g, ALU.add)
                        return u
                    token_mm(yT[:, s * 4:s * 4 + 4, :], w, 512, out, (V, A), nk=4, woff=i * 512, wstride=1024)
                w.free(PE.now)
            transpose_to(hT, lambda c, k: mg[:, c, k * P:(k + 1) * P], 8, (V, PE))
            mo = gt[:, :, 0:1024]
            for i in range(2):
                w = load(d["w_o2"][i])

                def out(c, ps, i=i):
                    return cp(V, mo[:, c, i * 512:(i + 1) * 512], ps, (PE,))
                token_mm(hT, w, 512, out, (V, A))
                w.free(PE.now)

            def add_gated(y, row, gate, gb, scr):
                for i in range(2):
                    b = bank()
                    for j in range(4):
                        k = 4 * i + j
                        cp(V, scr[:, 0, j * P:(j + 1) * P], gate[:, k:k + 1].to_broadcast([P, P]), (PE, A))
                    for j in range(4):
                        mm(b, b.ap[:, j * P:(j + 1) * P], scr[:, 0, j * P:(j + 1) * P], ident, after=(V,), last=(j == 3))
                    b.free(cp(V, gb[:, i * 512:(i + 1) * 512], b.ap[:, :], (PE,)))
                w = load_row("rows", row)
                tt(V, gb, gb, w.ap, ALU.mult, (w.ready,))
                w.free(V.now)
                rms_rows(scr, y, D)
                for c in range(2):
                    stt(y[:, c, :], y[:, c, :], st["rs"][:, c:c + 1], gb, ALU.mult, ALU.mult, (A,))
                    tt(V, h[:, c, :], h[:, c, :], y[:, c, :], ALU.add)

            add_gated(mo, 13, modT[:, 16:24], ar(7168, 1024), ar(8192, 2048).rearrange("p (c n) -> p c n", c=2))
            show("xmix", h_sb[:, :], (V,))
            normed(h, gs2, modT[:, 24:32], ctx_sb)
            moe(ctx_sb, modT, add_gated)

        def moe(scr, modT, add_gated):
            Wt = ar(0, 128).rearrange("p (c n) -> p c n", c=2)
            sg = ar(128, 128).rearrange("p (c n) -> p c n", c=2)
            bi = ar(256, 128).rearrange("p (c n) -> p c n", c=2)
            cb = ar(384, 64)
            g8, m8, kp, srt = ar(448, 64), ar(512, 8), ar(520, 8), ar(528, 8)
            gsum, ssum, rb = ar(536, 8), ar(544, 8), ar(552, 64)
            WT_ = ar(616, 256)
            sel = ar(872, 512)
            WB = ar(1536, 16384).rearrange("p (e t) -> p e t", e=64)
            act_b = [ar(17920 + 1536 * i, 512) for i in range(2)]
            t_b = [ar(17920 + 1536 * i + 512, 512) for i in range(2)]
            hid = [ar(17920 + 1536 * i + 1024, 512) for i in range(2)]
            rbs = load(d["router_bias"].to_broadcast([P, 64]), 1)
            w = load(d["w_router"], 1)

            def out(c, ps):
                act(sg[:, c, :], ps, ACT.Exp, (PE, V), scale=-1.0)
                u = A.now
                ts(V, sg[:, c, :], sg[:, c, :], 1.0, None, ALU.add, None, (A,))
                V.op(lambda e: e.reciprocal(sg[:, c, :], sg[:, c, :]))
                tt(V, bi[:, c, :], sg[:, c, :], rbs.ap[:, 0:64], ALU.add, (rbs.ready,))
                return u
            token_mm(hT, w, 64, out, (V, A), wstride=64)
            w.free(PE.now)
            rbs.free(V.now)
            for c in range(2):
                for g in range(8):
                    V.op(lambda e, g=g, c=c: e.max(out=g8[:, 8 * g:8 * g + 8], in_=bi[:, c, 8 * g:8 * g + 8]))
                gv = heads(g8, 8)
                tt(V, gsum, gv[:, :, 0:1].rearrange("p a b -> p (a b)"), gv[:, :, 1:2].rearrange("p a b -> p (a b)"), ALU.add)
                V.op(lambda e: e.max(out=m8, in_=gsum))
                V.op(lambda e: e.memset(m8[:, 4:8], 3e38))
                V.op(lambda e: e.match_replace(out=kp, in_to_replace=m8, in_values=gsum, imm_value=-2e38))
                ts(V, kp, kp, -1e38, -1e30, ALU.is_gt, ALU.mult)
                tt(V, heads(cb, 8), heads(bi[:, c, :], 8), bc(kp, 2, 8), ALU.add)
                V.op(lambda e: e.max(out=m8, in_=cb))
                V.op(lambda e: e.match_replace(out=cb, in_to_replace=m8, in_values=cb, imm_value=-2e38))
                ts(V, cb, cb, -1e38, None, ALU.is_lt, None)
                tt(V, Wt[:, c, :], sg[:, c, :], cb, ALU.mult)
                red(ssum[:, 0:1], Wt[:, c, :])
                V.op(lambda e: e.reciprocal(ssum[:, 0:1], ssum[:, 0:1]))
                ts(V, Wt[:, c, :], Wt[:, c, :], ssum[:, 0:1], 2.5, ALU.mult, ALU.mult)
            b = bank()
            for c in range(2):
                tr(b, b.ap[0:64, c * P:(c + 1) * P], Wt[:, c, :], (V,), last=(c == 1))
            b.free(cp(V, WT_[0:64, :], b.ap[0:64, 0:256], (PE,)))
            for e0 in range(0, 64, 4):
                for j in range(4):
                    cp(V, sel[0:64, j * P:(j + 1) * P], ident[0:64, e0 + j:e0 + j + 1].to_broadcast([64, P]), (PE,))
                for jj in (0, 2):
                    b = bank()
                    for j in (jj, jj + 1):
                        mm(b, b.ap[:, (j - jj) * 256:(j - jj) * 256 + 256], sel[0:64, j * P:(j + 1) * P], WT_[0:64, :],
                           after=(V,), last=(j == jj + 1))
                    b.free(cp(A, WB[:, e0 + jj:e0 + jj + 2, :], b.ap[:, :].rearrange("p (e t) -> p e t", e=2), (PE, V)))
            acc = []
            for i in range(4):
                bpos[0] += (-bpos[0]) % 8 if i == 0 else 0
                acc.append(bank())
            held.update(x.first for x in acc)
            ready_hid = [None, None]
            done_hid = [None, None]

            def down(e, wd):
                hv = hid[e % 2].rearrange("p (f t) -> p f t", f=2)
                for c in range(2):
                    for n in range(2):
                        b = acc[2 * c + n]
                        for f in range(2):
                            mm(b, b.ap[:, :], hv[:, f, c * P:(c + 1) * P],
                               wd.ap[:, f * 1024 + n * 512:f * 1024 + n * 512 + 512],
                               e == 0 and f == 0, e == 64 and f == 1, (wd.ready, ready_hid[e % 2]),
                               last=(c == 1 and n == 1 and f == 1))
                done_hid[e % 2] = PE.now
                wd.free(PE.now)

            prev = None
            for e in range(65):
                wg = load(d["w_gu"][e] if e < 64 else d["w_gu_sh"])
                wd = load(d["w_down"][e] if e < 64 else d["w_down_sh"])
                bg, bu = bank(), bank()
                for f in range(2):
                    feat_mm(hT, wg, f, bg.ap[:, f * 256:(f + 1) * 256], bg, (V, A) if e == 0 else ())
                tg = PE.now
                for f in range(2):
                    feat_mm(hT, wg, 2 + f, bu.ap[:, f * 256:(f + 1) * 256], bu, ())
                wg.free(PE.now)
                i = e % 2
                t1 = act(act_b[i], bg.ap[:, :], ACT.Sigmoid, (tg, V) if ready_hid[i] is None else (tg, ready_hid[i]))
                tt(V, t_b[i], act_b[i], bg.ap[:, :], ALU.mult, (t1,))
                bg.free(V.now)
                if e < 64:
                    u = tt(V, t_b[i], t_b[i], bu.ap[:, :], ALU.mult, (PE,))
                    tt(V, hid[i].rearrange("p (f t) -> p f t", f=2), t_b[i].rearrange("p (f t) -> p f t", f=2),
                       bc(WB[:, e, :], 1, 2), ALU.mult, (A,) if done_hid[i] is None else (done_hid[i],))
                else:
                    u = tt(V, hid[i], t_b[i], bu.ap[:, :], ALU.mult, (PE, done_hid[i]))
                bu.free(u)
                ready_hid[i] = V.now
                if prev is not None:
                    down(*prev)
                prev = (e, wd)
            down(*prev)
            y = ar(1536, 2048).rearrange("p (c n) -> p c n", c=2)
            for c in range(2):
                for n in range(2):
                    acc[2 * c + n].free(cp(V, y[:, c, n * 512:(n + 1) * 512], acc[2 * c + n].ap[:, :], (PE,)))
            held.clear()
            add_gated(y, 14, modT[:, 40:48], ar(3584, 1024), ar(4608, 2048).rearrange("p (c n) -> p c n", c=2))
            SP.dma(lambda e: e.dma_start(y_dram, h), [V.now], s_out)
            n_out[0] += 16

        asm = {n: sm(k) for n, k in (("ss", 16), ("rs", 16), ("mx", 8), ("den", 8), ("snk", 8))}
        iu = sb("iu", 512, U32)
        show("h0", h_sb[:, :], (V,))
        for l in range(LAYERS):
            attention(l)
            show(f"hattn{l}", h_sb[:, :], (V,))
            if stop == f"attn{l}":
                break
            peer(l)
            show(f"h{l + 1}", h_sb[:, :], (V,))
            if stop == f"peer{l}":
                break
        if stop is None:
            second()
        else:
            SP.dma(lambda e: e.dma_start(y_dram, h), [V.now], s_out)
            n_out[0] += 16

        block = ctx.enter_context(nc.Block())

        @block.sync
        def _(e):
            SP.play(e)
            e.wait_ge(s_out, n_out[0])

        @block.gpsimd
        def _(e):
            G.play(e)

        @block.scalar
        def _(e):
            A.play(e)

        @block.vector
        def _(e):
            V.play(e)

        @block.tensor
        def _(e):
            PE.play(e)


def constants():
    import numpy as np
    f = np.float32
    t = {}
    i = np.arange(P)
    t["ident"] = np.eye(P)
    t["triF"] = (i[:, None] <= i[None, :])
    t["triB"] = (i[:, None] >= i[None, :])
    t["low"] = (i[:, None] > i[None, :])
    t["up"] = (i[:, None] < i[None, :])
    tok = np.arange(T).reshape(2, P)
    dist = np.abs(tok[:, :, None] - np.arange(T)[None, None, :])
    t["dist"] = dist.transpose(1, 0, 2).reshape(P, -1)
    t["mask"] = np.where(dist <= 128, 0.0, -1e30).transpose(1, 0, 2).reshape(P, -1)
    t["iota16"] = np.tile(np.arange(16), (P, 1))
    pos = np.stack([np.arange(T) // 64, np.arange(T) % 64], -1).astype(f)
    inv = (f(10000.0) ** (-np.arange(16, dtype=f) / f(16))).astype(f)
    ang = (pos[:, :, None] * inv).astype(f).reshape(2, P, 32).transpose(1, 0, 2).reshape(P, 64)
    t["cos1"], t["sin1"] = np.cos(ang), np.sin(ang)
    inv = (f(10000.0) ** (-np.arange(32, dtype=f) / f(32))).astype(f)
    ang = np.concatenate([pos[:, 0:1] * inv, pos[:, 1:2] * inv], -1).astype(f)
    ang = ang.reshape(2, P, 64).transpose(1, 0, 2).reshape(P, 128)
    t["cos2"], t["sin2"] = np.cos(ang), np.sin(ang)
    for l in range(7):
        same = (i[:, None] >> (l + 1)) == (i[None, :] >> (l + 1))
        t[f"lvl{l}"] = same & ((i[:, None] >> l) != (i[None, :] >> l))
    t["up1"] = np.tile(i + 1, (P, 1))
    t["down"] = np.tile(P - i, (P, 1))
    t["col"] = i[:, None]
    t["mhalf"] = np.full((P, 16), -0.5)
    t["rel"] = i[None, :] - i[:, None]
    at, o = {}, 0
    for k, v in t.items():
        at[k] = (o, v.shape[1])
        o += v.shape[1]
    return at, o, np.ascontiguousarray(np.concatenate([v.astype(f) for v in t.values()], 1))


CONST_AT, CONST_COLS, CONSTS = constants()


def tiles(w, n=512):
    import numpy as np
    k, m = w.shape[-2:]
    lead = w.shape[:-2]
    v = w.reshape(*lead, k // P, P, m // n, n)
    r = len(lead)
    v = np.moveaxis(v, r + 2, r)
    v = np.moveaxis(v, r + 2, r + 1)
    return np.ascontiguousarray(v).reshape(*lead, m // n, P, k // P * n)


def arrays_of(i):
    import numpy as np
    a = {k: np.asarray(v) for k, v in i.items()}
    r = {"consts": CONSTS, "x": a["x"][0]}
    rows = [a["ln_in_g"], a["ln_in_b"]]
    for l in range(LAYERS):
        rows += [np.concatenate([a["gn_a_g"][l], a["gn_b_g"][l]]), a["ln1_g"][l], a["ln1_b"][l],
                 a["ln2_g"][l], a["ln2_b"][l]]
    rows += [np.concatenate([a["ret_gn_w_2"][0], a["gdn_norm_w_2"][0]]), a["norm_mix_post_2"][0],
             a["norm_ffn_post_2"][0]]
    r["rows"] = np.stack(rows)
    r["qn_g"] = a["qn_g"].reshape(1, -1)
    r["kn_g"] = a["kn_g"].reshape(1, -1)
    r["sink"] = a["sink"].reshape(1, -1)
    r["a_log"] = a["gdn_a_log_2"].reshape(1, -1)
    r["dt_bias"] = a["gdn_dt_bias_2"].reshape(1, -1)
    r["ret_decay"] = a["ret_log_decay_2"].reshape(1, -1)
    cols = lambda v: v.reshape(-1, P).T
    r["b_mod"] = cols(a["b_mod_2"][0])
    r["cvec"] = np.stack([cols(a["c_2"][0]), cols(a["c_ctx_2"])], -1).reshape(P, -1)
    r["conv"] = a["gdn_conv_2"][0].reshape(3, 12, P).transpose(2, 0, 1).reshape(P, -1)
    r["norm_cols"] = np.concatenate([cols(a["norm_mix_pre_2"][0]), cols(a["norm_ffn_pre_2"][0])], 1)
    r["w_in"] = tiles(a["w_in"])
    r["w_o"] = tiles(a["w_o"])
    r["peer_wq"] = tiles(a["peer_wq"])
    r["peer_keys"] = a["peer_keys"].transpose(0, 4, 1, 2, 3).reshape(LAYERS, P, 2048)
    r["peer_u"] = a["peer_u"].reshape(-1, D)
    r["peer_v"] = a["peer_v"].reshape(-1, D)
    r["ctx"] = a["ctx_2"][0]
    r["w_mod"] = tiles(a["w_mod_2"][0])
    w = a["w_in_2"][0]
    r["w_in2"] = tiles(np.concatenate([w[:, 0:2048], w[:, 2064:]], 1))
    r["w_gab"] = tiles(w[:, 2048:2064], 16)[0]
    r["w_ret_out"] = tiles(a["w_ret_out_2"][0], 1024)[0]
    r["w_gdn_out"] = tiles(a["w_gdn_out_2"][0], 1024)[0]
    r["w_o2"] = tiles(a["w_o_2"][0])
    r["w_router"] = tiles(a["w_router_2"][0], 64)[0]
    r["router_bias"] = a["router_bias_2"].reshape(1, -1)
    r["w_gu"] = tiles(np.concatenate([a["w_gate_2"][0], a["w_up_2"][0]], -1))[:, 0]
    r["w_down"] = tiles(a["w_down_2"][0], 1024)[:, 0]
    r["w_gu_sh"] = tiles(np.concatenate([a["w_sh_gate_2"][0], a["w_sh_up_2"][0]], -1))[0]
    r["w_down_sh"] = tiles(a["w_sh_down_2"][0], 1024)[0]
    return {k: np.ascontiguousarray(v) for k, v in r.items()}


def kernel(**inputs):
    import concourse.bacc as _bacc
    from concourse import mybir as _mybir
    from concourse.bass_utils import run_bass_kernel_spmd as _run

    nc = _bacc.Bacc("TRN2", target_bir_lowering=False, num_devices=1)
    arrays, d = {}, {}
    for name, a in arrays_of(inputs).items():
        arrays[f"in_{name}"] = a
        d[name] = nc.dram_tensor(f"in_{name}", a.shape, _mybir.dt.from_np(a.dtype), kind="ExternalInput").ap()
    out = nc.dram_tensor("out_0", (T, D), F32, kind="ExternalOutput").ap()
    build(nc, d, out)
    r = _run(nc, [arrays], core_ids=[0])
    return r.results[0]["out_0"].reshape(1, T, D)
```

```python
import concourse.bass as bass
from concourse import mybir
from contextlib import ExitStack

P = 128
ALU = mybir.AluOpType
ACT = mybir.ActivationFunctionType
F32 = mybir.dt.float32
U32 = mybir.dt.uint32
AX = mybir.AxisListType.X

T, D, NC_ = 256, 1024, 2
LAYERS = 2
NEXP = 16384
ALPHA = (2.0 * LAYERS) ** 0.25
RING = 20
ARENA = 22528


class Queue:

    def __init__(self, name, sem, chained):
        self.name, self.sem, self.chained = name, sem, chained
        self.items, self.n, self.pending = [], 0, []

    @property
    def now(self):
        return (self.sem, self.n)

    def op(self, emit, after=(), inc=True, chain=True):
        waits = [a.now if isinstance(a, Queue) else a for a in after] + self.pending
        self.pending = []
        if self.chained and chain and self.n:
            waits.append(self.now)
        if inc:
            self.n += 1
        self.items.append((emit, waits, self.sem if inc else None, 1))
        return self.now

    def hold_for(self, *producers):
        self.pending += [a.now if isinstance(a, Queue) else a for a in producers]

    def dma(self, emit, after, sem):
        self.items.append((emit, after, sem, 16))

    def begin_if(self, flag, *after):
        self.items.append(("if", (flag, after), self.n, 0))

    def end_if(self):
        self.items.append(("end", None, self.n, 0))

    def play(self, eng):
        seen = {}

        def wait(w):
            if isinstance(w, Slot):
                for x in w.released:
                    wait(x)
                return
            s, v = w
            if v and seen.get(s.num, 0) < v:
                seen[s.num] = v
                eng.wait_ge(s, v)

        def run(items):
            for emit, waits, sem, by in items:
                for w in waits:
                    wait(w)
                ins = emit(eng)
                if sem is not None:
                    ins.then_inc(sem, by)

        marks = [i for i, it in enumerate(self.items) if it[0] in ("if", "end")]
        if not marks:
            return run(self.items)
        a, b = marks
        run(self.items[:a])
        flag, after = self.items[a][1]
        for w in after:
            wait(w)
        value = eng.value_load(flag[0:1, 0:1], min_val=0, max_val=1)
        before = dict(seen)
        with eng.If(value > 0):
            run(self.items[a + 1:b])
        n = self.items[b][2] - self.items[a][2]
        if n:
            with eng.Else():
                eng.sem_inc(self.sem, n)
        seen.clear()
        seen.update(before)
        run(self.items[b + 1:])


class Slot:

    def __init__(self, ap, first):
        self.ap, self.first, self.ready, self.released = ap, first, None, []

    def free(self, *tokens):
        self.released.extend(tokens)


def build(nc, d, out, dump=None, stop=None):
    import numpy as np
    ctx = ExitStack()
    with ctx:
        def sb(name, n, dt=F32):
            return ctx.enter_context(nc.sbuf_tensor(name, [P, n], dt))

        def sem(name):
            return ctx.enter_context(nc.semaphore(name))

        y_dram = out.rearrange("(c p) n -> p c n", p=P)
        PE = Queue("pe", sem("s_pe"), False)
        V = Queue("v", sem("s_v"), True)
        A = Queue("a", sem("s_a"), True)
        G = Queue("g", sem("s_g"), True)
        SP = Queue("sp", sem("s_sp"), False)
        s_small = sem("s_small")
        s_out = sem("s_out")
        ring_sems = [sem(f"s_r{i}") for i in range(RING)]
        gath_sems = [sem(f"s_g{i}") for i in range(RING)]
        ring_count, gath_count = [0] * RING, [0] * RING

        ring2_sems = ([sem(f"s_b{i}") for i in range(RING)], [0] * RING)
        xg_sems = [sem(f"s_xg{i}") for i in range(4)]
        xg2_sems = [sem(f"s_xh{i}") for i in range(4)]
        s_tab, s_y, s_y2, s_yin = sem("s_tab"), sem("s_y"), sem("s_y2"), sem("s_yin")
        x_tab, y_tab = d["x_tab"], d["y_tab"]
        flag = ctx.enter_context(nc.sbuf_tensor("flag", [P, 1], U32))
        h_sb = sb("h", 2048)
        hT_sb = sb("hT", 2048)
        ring = sb("ring", RING * 1024)
        arena = sb("arena", ARENA)
        cst = sb("cst", CONST_COLS)
        small = sb("small", 1000)
        idx_u = sb("idx_u", 256, U32)
        banks = [ctx.enter_context(nc.psum_tensor(f"ps{i}", [P, 512], F32)) for i in range(8)]

        h = h_sb[:, :].rearrange("p (c n) -> p c n", c=2)
        hT = hT_sb[:, :].rearrange("p (k t) -> p k t", k=8)

        def C(name):
            o, n = CONST_AT[name]
            return cst[:, o:o + n]

        ident = C("ident")

        small_at = [0]

        def sm(n):
            o = small_at[0]
            small_at[0] += n
            assert small_at[0] <= 1000
            return small[:, o:o + n]

        owners = [None] * RING
        rpos = [0]

        def take(k, sems=None, count=None):
            sems, count = sems or ring_sems, count or ring_count
            if rpos[0] % RING + k > RING:
                rpos[0] += RING - rpos[0] % RING
            s = rpos[0] % RING
            rpos[0] += k
            slot = Slot(ring[:, s * 1024:(s + k) * 1024], s)
            before = []
            for i in range(s, s + k):
                if owners[i] is not None and owners[i] not in before:
                    before.append(owners[i])
                owners[i] = slot
            count[s] += 16
            slot.ready = (sems[s], count[s])
            return slot, before

        def load(src, k=None, sems=None):
            n = src.shape[-1]
            k = k or -(-n // 1024)
            sems, count = sems or (ring_sems, ring_count)
            slot, before = take(k, sems, count)
            dst = slot.ap[:, 0:n]
            SP.dma(lambda e: e.dma_start(dst, src), before, sems[slot.first])
            return slot

        def load_row(name, row):
            src = d[name][row:row + 1, :].to_broadcast([P, d[name].shape[1]])
            return load(src)

        bank_slots = [Slot(b, i) for i, b in enumerate(banks)]
        bpos = [0]
        held = set()

        def bank():
            while bpos[0] % 8 in held:
                bpos[0] += 1
            i = bpos[0] % 8
            bpos[0] += 1
            new = Slot(banks[i], i)
            new.before = bank_slots[i]
            bank_slots[i] = new
            return new

        def mm(b, o, lhsT, rhs, start=True, stop=True, after=(), last=False):
            return PE.op(lambda e: e.matmul(o, lhsT, rhs, start=start, stop=stop, skip_group_check=True),
                         (b.before, *after), inc=last)

        def tr(b, o, src, after=(), last=False):
            return PE.op(lambda e: e.transpose(o, src, ident), (b.before, *after), inc=last)

        def tt(q, o, a, b, op, after=(), **k):
            return q.op(lambda e: e.tensor_tensor(o, a, b, op), after, **k)

        def ts(q, o, a, s1, s2, op0, op1, after=(), **k):
            if op1 is None:
                return q.op(lambda e: e.tensor_scalar(o, a, s1, None, op0), after, **k)
            return q.op(lambda e: e.tensor_scalar(o, a, s1, s2, op0, op1), after, **k)

        def stt(o, a, s, b, op0, op1, after=(), **k):
            return V.op(lambda e: e.scalar_tensor_tensor(out=o, in0=a, scalar=s, in1=b, op0=op0, op1=op1), after, **k)

        def rsqrt(o, a, scale, eps, after=()):
            ts(V, o, a, scale, eps, ALU.mult, ALU.add, after)
            n = o.shape[-1]
            t = tt(G, o, o, C("mhalf")[:, 0:n], ALU.pow, (V,))
            V.hold_for(t)
            return t

        def red(o, a, op=ALU.add, after=()):
            return V.op(lambda e: e.tensor_reduce(o, a, AX, op), after)

        def act(o, a, f, after=(), **k):
            return A.op(lambda e: e.activation(o, a, f, **k), after)

        def cp(q, o, a, after=()):
            if q is A:
                return A.op(lambda e: e.activation(o, a, ACT.Copy), after)
            return q.op(lambda e: e.tensor_copy(o, a), after)

        def bc(a, axis, n):
            u = a.unsqueeze(axis)
            s = list(u.shape)
            s[axis] = n
            return u.to_broadcast(s)

        def heads(a, n):
            return a.rearrange("p (h x) -> p h x", h=n)

        def show(name, ap, after):
            if dump is not None:
                n = 1
                for x in ap.shape[1:]:
                    n *= x
                o = dump(name, [P] + list(ap.shape[1:]))
                SP.dma(lambda e: e.dma_start(o, ap), [a.now if isinstance(a, Queue) else a for a in after], s_out)
                n_out[0] += 16

        n_out = [0]

        SP.dma(lambda e: e.dma_start(cst[:, :], d["consts"]), [], s_small)
        SP.dma(lambda e: e.dma_start(h, d["x"].rearrange("(c p) n -> p c n", p=P)), [], s_small)
        smalls = {}
        n_small = 32
        for name in ("qn_g", "kn_g", "sink", "a_log", "dt_bias", "ret_decay"):
            n = d[name].shape[1]
            smalls[name] = sm(n)
            SP.dma(lambda e, o=smalls[name], s=d[name].to_broadcast([P, n]): e.dma_start(o, s), [], s_small)
            n_small += 16
        for name in ("b_mod", "cvec", "conv", "norm_cols", "router_bias"):
            if name == "router_bias":
                continue
            n = d[name].shape[1]
            smalls[name] = sm(n)
            SP.dma(lambda e, o=smalls[name], s=d[name]: e.dma_start(o, s), [], s_small)
            n_small += 16
        loaded = (s_small, n_small)

        st = {n: sm(8) for n in ("sum", "ss", "rs")}
        first = [loaded]

        def transpose_to(dst, src_of, nk, after, affine=None):
            for c in range(2):
                for k0 in range(0, nk, 4):
                    b = bank()
                    for j in range(4):
                        t = tr(b, b.ap[:, j * P:(j + 1) * P], src_of(c, k0 + j), after, last=(j == 3))
                    if affine is None:
                        q = (V, A)[(k0 // 4) % 2]
                        b.free(cp(q, dst[:, k0:k0 + 4, c * P:(c + 1) * P], b.ap[:, :].rearrange("p (k t) -> p k t", k=4),
                                  (PE,)))
                    else:
                        for j in range(4):
                            s1, s2 = affine(k0 + j)
                            u = ts(V, dst[:, k0 + j, c * P:(c + 1) * P], b.ap[:, j * P:(j + 1) * P], s1, s2,
                                   ALU.mult, ALU.add, (PE,))
                        b.free(u)

        def token_mm(xT, w, n, take_out, after, nk=8, woff=0, wstride=512):
            wv = w.ap
            for c in range(2):
                b = bank()
                for k in range(nk):
                    mm(b, b.ap[:, 0:n], xT[:, k, c * P:(c + 1) * P], wv[:, woff + k * wstride:woff + k * wstride + n],
                       k == 0, k == nk - 1, (w.ready, *after), last=(k == nk - 1))
                b.free(take_out(c, b.ap[:, 0:n]))

        def feat_mm(xT, w, m, o, b, after):
            for k in range(8):
                t = mm(b, o, w.ap[:, k * 512 + m * P:k * 512 + (m + 1) * P], xT[:, k, :],
                       k == 0, k == 7, (w.ready, *after), last=(k == 7))
            return t

        def layer_norm(g, b, scratch, after=()):
            for c in range(2):
                x, y = h[:, c, :], scratch[:, c, :]
                red(st["sum"][:, c:c + 1], x, after=(A, G, *after))
                ts(V, st["sum"][:, c:c + 1], st["sum"][:, c:c + 1], -1.0 / D, None, ALU.mult, None)
                ts(V, x, x, st["sum"][:, c:c + 1], None, ALU.add, None)
                act(y, x, ACT.Square, (V,), accum_out=st["ss"][:, c:c + 1])
                rsqrt(st["rs"][:, c:c + 1], st["ss"][:, c:c + 1], 1.0 / D, 1e-5, (A,))
                stt(x, x, st["rs"][:, c:c + 1], g.ap, ALU.mult, ALU.mult, (g.ready,))
                tt(V, x, x, b.ap, ALU.add, (b.ready,))
            g.free(V.now)
            b.free(V.now)

        def ar(o, n):
            assert o + n <= ARENA
            return arena[:, o:o + n]

        V.op(lambda e: e.memset(st["sum"], 0.0), (loaded,))
        PE.op(lambda e: e.transpose(banks[0][:, 0:P], ident, ident), (loaded,), inc=True)
        A.op(lambda e: e.activation(st["ss"], st["sum"], ACT.Copy), (loaded, V))
        G.op(lambda e: e.memset(st["rs"], 0.0), (loaded,))
        bank_slots[0].free(PE.now)
        lnscr = ar(0, 2048).rearrange("p (c n) -> p c n", c=2)
        g0, b0 = load_row("rows", 0), load_row("rows", 1)
        layer_norm(g0, b0, lnscr)

        def attention(l):
            proj = ar(0, 3072).rearrange("p (c n) -> p c n", c=2)
            qkT = ar(3072, 5120).rearrange("p (i t) -> p i t", i=20)
            S = ar(8192, 2048)
            PT = ar(10240, 2048)
            mix = ar(12288, 2048).rearrange("p (c n) -> p c n", c=2)
            rot = ar(14336, 1280).rearrange("p (c n) -> p c n", c=2)
            tmp = ar(15616, 2048)
            scr = ar(17664, 2048).rearrange("p (c n) -> p c n", c=2)
            ss, rs, mx, den, snk = (asm[n] for n in ("ss", "rs", "mx", "den", "snk"))
            w = [load(d["w_in"][l, i]) for i in range(3)]
            transpose_to(hT, lambda c, k: h[:, c, k * P:(k + 1) * P], 8, (V, A, G))
            for i in range(3):
                def out(c, ps, i=i):
                    return cp((V, A)[(i + c) % 2], proj[:, c, i * 512:(i + 1) * 512], ps, (PE,))
                token_mm(hT, w[i], 512, out, (V, A))
                w[i].free(PE.now)
            cos, sin = C("cos1"), C("sin1")
            for c in range(2):
                x, r = proj[:, c, 0:640], rot[:, c, :]
                tt(V, tmp[:, 0:640], x, x, ALU.mult, (A, PE))
                red(ss[:, 0:10], heads(tmp[:, 0:640], 10))
                rsqrt(rs[:, 0:10], ss[:, 0:10], 1.0 / 64, 1e-6)
                tt(V, heads(x, 10), heads(x, 10), bc(rs[:, 0:10], 2, 64), ALU.mult)
                tt(V, heads(x[:, 0:512], 8), heads(x[:, 0:512], 8),
                   bc(smalls["qn_g"][:, l * 64:(l + 1) * 64], 1, 8), ALU.mult)
                tt(V, heads(x[:, 512:640], 2), heads(x[:, 512:640], 2),
                   bc(smalls["kn_g"][:, l * 64:(l + 1) * 64], 1, 2), ALU.mult)
                xv = x.rearrange("p (h a w f) -> p h a w f", h=10, a=2, w=2)
                rv = r.rearrange("p (h a w f) -> p h a w f", h=10, a=2, w=2)
                tv = tmp[:, 0:320].rearrange("p (h a f) -> p h a f", h=10, a=2)
                tg = tmp[:, 1024:1344].rearrange("p (h a f) -> p h a f", h=10, a=2)
                cc = bc(cos[:, c * 32:(c + 1) * 32].rearrange("p (a f) -> p a f", a=2), 1, 10)
                sn = bc(sin[:, c * 32:(c + 1) * 32].rearrange("p (a f) -> p a f", a=2), 1, 10)
                x1, x2 = xv[:, :, :, 0, :], xv[:, :, :, 1, :]
                tt(V, rv[:, :, :, 0, :], x1, cc, ALU.mult)
                tt(G, tg, x1, sn, ALU.mult, (V,))
                tt(V, tv, x2, sn, ALU.mult)
                tt(G, rv[:, :, :, 1, :], x2, cc, ALU.mult)
                tt(V, rv[:, :, :, 0, :], rv[:, :, :, 0, :], tv, ALU.subtract)
                tt(G, rv[:, :, :, 1, :], rv[:, :, :, 1, :], tg, ALU.add)
                V.hold_for(G)
            for c in range(2):
                for i0 in range(0, 20, 4):
                    b = bank()
                    for j in range(4):
                        i = i0 + j
                        src = rot[:, c, i * 64:(i + 1) * 64] if i < 10 else proj[:, c, 128 + i * 64:192 + i * 64]
                        tr(b, b.ap[0:64, j * P:(j + 1) * P], src, (V, G, A), last=(j == 3))
                    b.free(cp((V, A)[(i0 // 4) % 2], qkT[0:64, i0:i0 + 4, c * P:(c + 1) * P],
                              b.ap[0:64, :].rearrange("p (k t) -> p k t", k=4), (PE,)))
            for br in range(2):
                voff = 640 if br == 0 else 1408
                for c in range(2):
                    dist, mask = C("dist")[:, c * 256:(c + 1) * 256], C("mask")[:, c * 256:(c + 1) * 256]
                    for k in range(4):
                        b = bank()
                        for hd in (2 * k, 2 * k + 1):
                            mm(b, b.ap[:, (hd % 2) * 256:(hd % 2) * 256 + 256],
                               qkT[0:64, br * 10 + hd, c * P:(c + 1) * P],
                               qkT[0:64, br * 10 + 8 + hd // 4, :], after=(V, A), last=(hd % 2 == 1))
                        if br == 0:
                            u = ts(V, S[:, k * 512:(k + 1) * 512], b.ap[:, :], 0.125, None, ALU.mult, None, (PE,))
                        else:
                            for hd in (2 * k, 2 * k + 1):
                                tm = tmp[:, hd * 256:hd * 256 + 256]
                                slope = float(np.float32(2.0 ** (-(hd + 1.0))))
                                stt(tm, dist, -slope, mask, ALU.mult, ALU.add, (A,))
                                u = stt(S[:, hd * 256:hd * 256 + 256], b.ap[:, (hd % 2) * 256:(hd % 2) * 256 + 256],
                                        0.125, tm, ALU.mult, ALU.add, (PE,))
                        b.free(u)
                    Sv = heads(S, 8)
                    red(mx, Sv, ALU.max)
                    if br == 1:
                        tt(V, mx, mx, smalls["sink"][:, l * 8:(l + 1) * 8], ALU.max)
                        tt(V, snk, smalls["sink"][:, l * 8:(l + 1) * 8], mx, ALU.subtract)
                    tt(V, Sv, Sv, bc(mx, 2, 256), ALU.subtract)
                    act(S, S, ACT.Exp, (V,))
                    if br == 1:
                        act(snk, snk, ACT.Exp)
                    red(den, Sv, after=(A,))
                    if br == 1:
                        tt(V, den, den, snk, ALU.add)
                    V.op(lambda e: e.reciprocal(den, den))
                    for i0 in range(0, 16, 4):
                        b = bank()
                        for j in range(4):
                            i = i0 + j
                            tr(b, b.ap[:, j * P:(j + 1) * P], S[:, i * P:(i + 1) * P], (A, V), last=(j == 3))
                        b.free(cp((V, A)[(i0 // 4) % 2], PT[:, i0 * P:(i0 + 4) * P], b.ap[:, :], (PE,)))
                    b = bank()
                    for hd in range(8):
                        g = hd // 4
                        for s in range(2):
                            mm(b, b.ap[:, hd * 64:(hd + 1) * 64], PT[:, (hd * 2 + s) * P:(hd * 2 + s + 1) * P],
                               proj[:, s, voff + g * 64:voff + (g + 1) * 64], s == 0, s == 1, (V, A),
                               last=(hd == 7 and s == 1))
                    b.free(tt(V, heads(mix[:, c, br * 512:(br + 1) * 512], 8), heads(b.ap[:, :], 8),
                              bc(den, 2, 64), ALU.mult, (PE,)))
            w = [load(d["w_o"][l, i]) for i in range(2)]
            gn = load_row("rows", 2 + 5 * l)
            for c in range(2):
                m = mix[:, c, :]
                tt(V, tmp[:, 0:1024], m, m, ALU.mult, (PE,))
                red(ss, heads(tmp[:, 0:1024], 16))
                rsqrt(rs, ss, 1.0 / 64, 1e-6)
                tt(V, heads(m, 16), heads(m, 16), bc(rs, 2, 64), ALU.mult)
                tt(V, m, m, gn.ap, ALU.mult, (gn.ready,))
            gn.free(V.now)
            transpose_to(hT, lambda c, k: mix[:, c, k * P:(k + 1) * P], 8, (V, PE))
            for i in range(2):
                def out(c, ps, i=i):
                    x = h[:, c, i * 512:(i + 1) * 512]
                    return stt(x, x, ALPHA, ps, ALU.mult, ALU.add, (PE,))
                token_mm(hT, w[i], 512, out, (V, A))
                w[i].free(PE.now)
            g1, b1 = load_row("rows", 3 + 5 * l), load_row("rows", 4 + 5 * l)
            layer_norm(g1, b1, scr)

        def peer(l):
            qT = ar(0, 4096).rearrange("p (m t) -> p m t", m=16)
            SC = ar(4096, 2048)
            SC2 = ar(6144, 2048)
            OH = ar(8192, 2048)
            junk = ar(10240, 1024)
            accs = ar(11264, 2048).rearrange("p (c n) -> p c n", c=2)
            v16 = ar(13312, 256)
            i16u = iu[:, 0:256]
            i16 = ar(13568, 256)
            tsv = ar(13824, 128)
            pf1 = ar(13952, 128)
            pf2 = ar(14080, 128)
            e1 = ar(14208, 128)
            e2 = ar(14336, 128)
            gs = ar(14464, 256)
            aa = ar(14720, 256)
            wgt = ar(14976, 256)
            scr = ar(17664, 2048).rearrange("p (c n) -> p c n", c=2)
            w = [load(d["peer_wq"][l, i]) for i in range(4)]
            kt = load(d["peer_keys"][l])
            transpose_to(hT, lambda c, k: h[:, c, k * P:(k + 1) * P], 8, (V, A, G))
            for i in range(4):
                for m0 in range(0, 4, 2):
                    b = bank()
                    for m in (m0, m0 + 1):
                        feat_mm(hT, w[i], m, b.ap[:, (m - m0) * 256:(m - m0) * 256 + 256], b, (V, A))
                    b.free(cp((V, A)[(m0 // 2) % 2], qT[:, i * 4 + m0:i * 4 + m0 + 2, :],
                              b.ap[:, :].rearrange("p (m t) -> p m t", m=2), (PE,)))
                w[i].free(PE.now)
            i_ready = []
            for c in range(2):
                for j in range(4):
                    b = bank()
                    for m in range(4):
                        hp = 4 * j + m
                        mm(b, b.ap[:, m * P:(m + 1) * P], qT[:, hp, c * P:(c + 1) * P],
                           kt.ap[:, hp * P:(hp + 1) * P], after=(kt.ready, V, A), last=(m == 3))
                    b.free(cp((V, A)[j % 2], SC[:, j * 512:(j + 1) * 512], b.ap[:, :], (PE, V)))
                V.hold_for(A, G)
                for grp, n, vals, ids, src, alt in ((16, P, v16, i16u, SC, SC2),):
                    topk(grp, n, vals, ids, src, alt)
                cp(V, i16, i16u)
                v4 = v16.rearrange("p (h s k) -> p h s k", h=8, s=2)
                i4 = i16.rearrange("p (h s k) -> p h s k", h=8, s=2)
                cand = SC.rearrange("p (h a b) -> p h a b", h=8, a=16)
                tt(V, cand, bc(v4[:, :, 0, :], 3, 16), bc(v4[:, :, 1, :], 2, 16), ALU.add)
                pos = iu[:, 256:384]
                topk(8, 256, tsv, pos, SC, SC2)
                pu = iu[:, 384:512]
                ts(V, pu, pos, 4, None, ALU.logical_shift_right, None)
                cp(V, pf1, pu)
                ts(V, pu, pos, 15, None, ALU.bitwise_and, None)
                cp(V, pf2, pu)
                for s, pf, ee in ((0, pf1, e1), (1, pf2, e2)):
                    tt(V, OH.rearrange("p (s k) -> p s k", k=16), bc(C("iota16"), 1, 128), bc(pf, 2, 16), ALU.is_equal)
                    o4 = OH.rearrange("p (h s k) -> p h s k", h=8, s=16)
                    tt(V, o4, o4, bc(i4[:, :, s, :], 2, 16), ALU.mult)
                    red(ee, OH.rearrange("p (s k) -> p s k", k=16))
                stt(e1, e1, 128.0, e2, ALU.mult, ALU.add)
                ts(V, e1, e1, float(l * NEXP), None, ALU.add, None)
                i_ready.append(cp(V, idx_u[:, c * P:(c + 1) * P], e1, (G,)))
                g = gs[:, c * P:(c + 1) * P]
                t3 = heads(tsv, 8)
                tt(V, heads(g, 8), t3, t3[:, :, 0:1].to_broadcast([P, 8, 16]), ALU.subtract)
                act(g, g, ACT.Exp, (V,))
                red(st["sum"], heads(g, 8), after=(A,))
                V.op(lambda e: e.reciprocal(st["sum"], st["sum"]))
                tt(V, heads(g, 8), heads(g, 8), bc(st["sum"], 2, 16), ALU.mult)
            kt.free(PE.now)
            if dump is not None:
                show(f"eidx{l}", idx_u[:, :], (V,))

            def gather(table, c, s):
                slot, before = take(1, gath_sems, gath_count)
                G.dma(lambda e: e.indirect_dma_start(
                    out=slot.ap, out_offset=None, in_=d[table],
                    in_offset=bass.IndirectOffsetOnAxis(ap=idx_u[:, c * P + s:c * P + s + 1], axis=0)),
                    [i_ready[c], *before], gath_sems[slot.first])
                return slot

            V.op(lambda e: e.memset(accs, 0.0), (A,))
            pend = []

            def dots(c, s, slot):
                slot.free(V.op(lambda e: e.tensor_tensor_reduce(
                    out=junk, in0=slot.ap, in1=h[:, c, :], scale=1.0, scalar=0.0, op0=ALU.mult, op1=ALU.add,
                    accum_out=aa[:, c * P + s:c * P + s + 1]), (slot.ready,)))

            def sums(c, s, slot):
                slot.free(stt(accs[:, c, :], slot.ap, wgt[:, c * P + s:c * P + s + 1], accs[:, c, :],
                              ALU.mult, ALU.add, (slot.ready,)))

            for table, use in (("peer_u", dots), ("peer_v", sums)):
                for c in range(2):
                    if use is sums:
                        tt(V, wgt[:, c * P:(c + 1) * P], wgt[:, c * P:(c + 1) * P], gs[:, c * P:(c + 1) * P],
                           ALU.mult, (A,))
                    for s in range(P):
                        use(c, s, gather(table, c, s))
                    if use is dots:
                        act(wgt[:, c * P:(c + 1) * P], aa[:, c * P:(c + 1) * P], ACT.Gelu, (V,))
            for c in range(2):
                stt(h[:, c, :], h[:, c, :], ALPHA, accs[:, c, :], ALU.mult, ALU.add)
            g2, b2 = load_row("rows", 5 + 5 * l), load_row("rows", 6 + 5 * l)
            layer_norm(g2, b2, scr)

        def topk(groups, n, vals, ids, src, alt):
            for i in range(groups):
                x, y = src[:, i * n:(i + 1) * n], alt[:, i * n:(i + 1) * n]
                a, b = vals[:, i * 16:i * 16 + 8], vals[:, i * 16 + 8:i * 16 + 16]
                ia, ib = ids[:, i * 16:i * 16 + 8], ids[:, i * 16 + 8:i * 16 + 16]
                V.op(lambda e, a=a, x=x: e.max(out=a, in_=x))
                V.op(lambda e, a=a, x=x, ia=ia: e.max_index(ia, a, x))
                V.op(lambda e, a=a, x=x, y=y: e.match_replace(out=y, in_to_replace=a, in_values=x, imm_value=-3e38),
                     chain=False)
                V.op(lambda e, b=b, y=y: e.max(out=b, in_=y))
                V.op(lambda e, b=b, y=y, ib=ib: e.max_index(ib, b, y))

        def second():
            Rk = ar(0, 1024).rearrange("p (c n) -> p c n", c=2)
            Rv = ar(1024, 1024).rearrange("p (c n) -> p c n", c=2)
            Rq = ar(2048, 1024).rearrange("p (c n) -> p c n", c=2)
            RkT = ar(3072, 1024).rearrange("p (k t) -> p k t", k=4)
            RqT = ar(4096, 1024).rearrange("p (k t) -> p k t", k=4)
            GG = ar(5120, 3072).rearrange("p (a c n) -> p a c n", a=3, c=2)
            GkT = ar(8192, 1024).rearrange("p (k t) -> p k t", k=4)
            GqT = ar(9216, 1024).rearrange("p (k t) -> p k t", k=4)
            Oret = ar(10240, 1024).rearrange("p (c n) -> p c n", c=2)
            Ogdn = ar(11264, 1024).rearrange("p (c n) -> p c n", c=2)
            S4 = ar(12288, 2048).rearrange("p (s n) -> p s n", s=4)
            Tm = lambda i: ar(14336 + 512 * i, 512)
            sc8 = {n: sm(8) for n in ("lasp", "e1", "e2", "ea", "eg", "ekt")}
            la = sm(16).rearrange("p (c n) -> p c n", c=2)
            be = sm(16).rearrange("p (c n) -> p c n", c=2)
            gc = sm(4)
            dec = sm(8)
            cd = sm(8)
            modT, cmT = sm(48), sm(16)
            gsx, gsc, gs2 = sm(8), sm(8), sm(8)
            t16 = sm(16)
            cs = sm(16)

            def silu_small(o, x, tmp):
                act(tmp, x, ACT.Sigmoid, (V,))
                tt(V, o, x, tmp, ALU.mult, (A,))

            silu_small(cs, smalls["cvec"], t16)
            csv = cs.rearrange("p (k s) -> p k s", k=8)
            b = bank()
            for i in range(12):
                w = load(d["w_mod"][i])
                for m in range(4):
                    j = 4 * i + m
                    for k in range(8):
                        mm(b, b.ap[:, 2 * j:2 * j + 2], w.ap[:, k * 512 + m * P:k * 512 + (m + 1) * P],
                           csv[:, k, :], k == 0, k == 7, (w.ready, V), last=(k == 7))
                w.free(PE.now)
            pv = b.ap[:, 0:96].rearrange("p (j s) -> p j s", s=2)
            tt(V, modT, pv[:, :, 0], smalls["b_mod"], ALU.add, (PE,))
            b.free(tt(V, cmT, pv[:, 0:16, 1], smalls["b_mod"][:, 0:16], ALU.add))
            nm = smalls["norm_cols"]
            for o, s, g in ((gsx, modT[:, 8:16], nm[:, 0:8]), (gsc, cmT[:, 8:16], nm[:, 0:8]),
                            (gs2, modT[:, 32:40], nm[:, 8:16])):
                stt(o, s, 1.0, g, ALU.add, ALU.mult)
            ea = sc8["ea"]
            act(ea, smalls["a_log"], ACT.Exp, (V,))
            rd = smalls["ret_decay"]
            act(cd, rd, ACT.Exp, (V,), scale=128.0)
            rel, col = C("rel"), C("col")
            Dret = Tm(15)
            cst_f = sm(8)
            for hd in range(4):
                o = Dret[:, hd * P:(hd + 1) * P]
                t1, t2 = Tm(0)[:, 0:P], Tm(0)[:, P:2 * P]
                ts(V, t1, rel, 0.0, None, ALU.max, None, (A, PE))
                ts(V, t2, rel, -1.0, 0.0, ALU.mult, ALU.max)
                act(t1, t1, ACT.Exp, (V,), scale=rd[:, hd:hd + 1])
                act(t2, t2, ACT.Exp, (V,), scale=rd[:, 4 + hd:5 + hd])
                tt(V, t1, t1, C("triF"), ALU.mult, (A,))
                tt(V, t2, t2, C("triB"), ALU.mult)
                tt(V, o, t1, t2, ALU.add)
            ts(V, cst_f[:, 0:1], col, -1.0, 127.0, ALU.mult, ALU.add)
            ts(V, dec[:, 0:4], rd[:, 0:4], cst_f[:, 0:1], None, ALU.mult, None)
            ts(V, dec[:, 4:8], rd[:, 4:8], col, None, ALU.mult, None)
            act(dec, dec, ACT.Exp, (V,))
            V.hold_for(A)

            def rms_rows(dst, src, n, after=()):
                for c in range(2):
                    act(dst[:, c, :], src[:, c, :], ACT.Square, (V, PE, *after), accum_out=st["ss"][:, c:c + 1])
                rsqrt(st["rs"][:, 0:2], st["ss"][:, 0:2], 1.0 / n, 1e-6, (A,))

            def normed(src, gcol, shift, xn):
                rms_rows(xn, src, D)
                for c in range(2):
                    ts(V, xn[:, c, :], src[:, c, :], st["rs"][:, c:c + 1], None, ALU.mult, None)
                transpose_to(hT, lambda c, k: xn[:, c, k * P:(k + 1) * P], 8, (V, PE),
                             affine=lambda k: (gcol[:, k:k + 1], shift[:, k:k + 1]))

            def features(x_side):
                n_conv = 3 if x_side else 2
                raw, cv = ar(14336, 1024), ar(15360, 1024)
                scr2 = ar(16384, 1024)
                if x_side:
                    for dst, i, s in ((Rk, 0, P ** -0.5), (Rv, 1, 1.0), (Rq, 4, 1.0)):
                        w = load(d["w_in2"][i])

                        def out(c, ps, dst=dst, s=s):
                            return ts(V, dst[:, c, :], ps, s, None, ALU.mult, None, (PE,))
                        token_mm(hT, w, 512, out, (V, A))
                        w.free(PE.now)
                    cos, sin = C("cos2"), C("sin2")
                    for R in (Rk, Rq):
                        for c in range(2):
                            xv = R[:, c, :].rearrange("p (h w f) -> p h w f", h=4, w=2)
                            cc, sn = bc(cos[:, c * 64:(c + 1) * 64], 1, 4), bc(sin[:, c * 64:(c + 1) * 64], 1, 4)
                            q = [scr2[:, 256 * j:256 * (j + 1)].rearrange("p (h f) -> p h f", h=4) for j in range(4)]
                            tt(V, q[0], xv[:, :, 0, :], cc, ALU.mult, (A, PE))
                            tt(V, q[1], xv[:, :, 1, :], sn, ALU.mult)
                            tt(V, q[2], xv[:, :, 0, :], sn, ALU.mult)
                            tt(V, q[3], xv[:, :, 1, :], cc, ALU.mult)
                            tt(V, xv[:, :, 0, :], q[0], q[1], ALU.subtract)
                            tt(V, xv[:, :, 1, :], q[2], q[3], ALU.add)
                    transpose_to(RkT, lambda c, k: Rk[:, c, k * P:(k + 1) * P], 4, (V,))
                    transpose_to(RqT, lambda c, k: Rq[:, c, k * P:(k + 1) * P], 4, (V,))
                else:
                    for dst, i, s in ((Rk, 0, P ** -0.5), (Rv, 1, 1.0)):
                        w = load(d["w_in2"][i])

                        def out(c, ps, dst=dst, s=s):
                            return ts(V, dst[:, c, :], ps, s, None, ALU.mult, None, (PE,))
                        token_mm(hT, w, 512, out, (V, A))
                        w.free(PE.now)
                w = load(d["w_gab"], 1)
                dtb = smalls["dt_bias"]

                def out(c, ps):
                    e1, e2 = sc8["e1"], sc8["e2"]
                    tt(V, e1, ps[:, 0:8], dtb, ALU.add, (PE, A))
                    u = cp(V, be[:, c, :], ps[:, 8:16])
                    act(be[:, c, :], be[:, c, :], ACT.Sigmoid, (V,))
                    act(e2, e1, ACT.Abs)
                    act(e2, e2, ACT.Exp, scale=-1.0)
                    act(e2, e2, ACT.Ln, bias=1.0)
                    stt(e1, e1, 0.0, e2, ALU.max, ALU.add, (A,))
                    stt(la[:, c, :], e1, -1.0, ea, ALU.mult, ALU.mult)
                    return u
                token_mm(hT, w, 16, out, (V, A), wstride=16)
                w.free(PE.now)
                cw = smalls["conv"].rearrange("p (j f) -> p j f", j=3)
                for a, i, f0 in ((0, 2, 4), (1, 3, 8), (2, 6, 0))[:n_conv]:
                    w = load(d["w_in2"][i])
                    rw = raw.rearrange("p (m t) -> p m t", m=4)
                    cvv = cv.rearrange("p (m t) -> p m t", m=4)
                    for m0 in (0, 2):
                        b = bank()
                        for m in (m0, m0 + 1):
                            feat_mm(hT, w, m, b.ap[:, (m - m0) * 256:(m - m0) * 256 + 256], b, (V, A))
                        b.free(cp(V, rw[:, m0:m0 + 2, :], b.ap[:, :].rearrange("p (m t) -> p m t", m=2), (PE,)))
                    w.free(PE.now)
                    for m in range(4):
                        x, y = rw[:, m, :], cvv[:, m, :]
                        f = f0 + m
                        ts(V, y, x, cw[:, 1, f:f + 1], None, ALU.mult, None, (PE,))
                        stt(y[:, 1:256], x[:, 0:255], cw[:, 0, f:f + 1], y[:, 1:256], ALU.mult, ALU.add)
                        stt(y[:, 0:255], x[:, 1:256], cw[:, 2, f:f + 1], y[:, 0:255], ALU.mult, ALU.add)
                    act(raw, cv, ACT.Sigmoid, (V,))
                    tt(V, cv, cv, raw, ALU.mult, (A,))
                    for c in range(2):
                        b = bank()
                        for m in range(4):
                            tr(b, b.ap[:, m * P:(m + 1) * P], cvv[:, m, c * P:(c + 1) * P], (V,), last=(m == 3))
                        b.free(cp(V, GG[:, a, c, :], b.ap[:, :], (PE,)))
                        if a != 1:
                            x = GG[:, a, c, :]
                            tt(V, scr2[:, 0:512], x, x, ALU.mult)
                            red(st["ss"][:, 0:4], heads(scr2[:, 0:512], 4))
                            rsqrt(st["rs"][:, 0:4], st["ss"][:, 0:4], 1.0, 1e-6)
                            if a == 2:
                                ts(V, st["rs"][:, 0:4], st["rs"][:, 0:4], P ** -0.5, None, ALU.mult, None)
                            tt(V, heads(x, 4), heads(x, 4), bc(st["rs"][:, 0:4], 2, P), ALU.mult)
                    if a != 1:
                        transpose_to(GkT if a == 0 else GqT, lambda c, k, a=a: GG[:, a, c, k * P:(k + 1) * P], 4, (V,))

            def gdn_matrices(c):
                kk = bank()
                for hd in range(4):
                    mm(kk, kk.ap[:, hd * P:(hd + 1) * P], GkT[:, hd, c * P:(c + 1) * P],
                       GkT[:, hd, c * P:(c + 1) * P], after=(V, A), last=(hd == 3))
                kk.free(cp(V, Tm(10), kk.ap[:, :], (PE,)))

            def gdn_chunk(dr, c, x_side):
                tri = C("triF") if dr == 0 else C("triB")
                strict = C("low") if dr == 0 else C("up")
                end = P - 1 if dr == 0 else 0
                GR, Dm, DT, Am, AT, Xm, XT, Pm = (Tm(i) for i in range(8))
                lac = la[:, c, dr * 4:dr * 4 + 4]
                bec = be[:, c, dr * 4:dr * 4 + 4]
                b = bank()
                for hd in range(4):
                    t = cp(V, Pm[:, hd * P:(hd + 1) * P], lac[:, hd:hd + 1].to_broadcast([P, P]), (PE, A))
                for hd in range(4):
                    mm(b, b.ap[:, hd * P:(hd + 1) * P], Pm[:, hd * P:(hd + 1) * P], tri, after=(V, A), last=(hd == 3))
                b.free(cp(V, GR, b.ap[:, :], (PE,)))
                b = bank()
                mm(b, b.ap[:, 0:4], tri, lac, after=(V, A), last=True)
                b.free(cp(V, gc, b.ap[:, 0:4], (PE,)))
                for hd in range(4):
                    s = slice(hd * P, (hd + 1) * P)
                    ts(V, Dm[:, s], GR[:, s], gc[:, hd:hd + 1], 0.0, ALU.subtract, ALU.max)
                    ts(V, DT[:, s], GR[:, s], gc[:, hd:hd + 1], 0.0, ALU.subtract, ALU.min)
                act(Dm, Dm, ACT.Exp, (V,), scale=-1.0)
                act(DT, DT, ACT.Exp)
                ekt, eg = sc8["ekt"][:, 0:4], sc8["eg"][:, 0:4]
                last = heads(GR, 4)[:, :, end:end + 1].rearrange("p h x -> p (h x)")
                tt(V, ekt, last, gc, ALU.subtract)
                act(ekt, ekt, ACT.Exp, (V,))
                act(eg, last, ACT.Exp)
                act(gc, gc, ACT.Exp)
                tt(V, heads(Dm, 4), heads(Dm, 4), bc(strict, 1, 4), ALU.mult, (A,))
                tt(V, heads(DT, 4), heads(DT, 4), bc(tri, 1, 4), ALU.mult)
                tt(V, Am, Tm(10), Dm, ALU.mult)
                tt(V, heads(Am, 4), heads(Am, 4), bc(bec, 2, P), ALU.mult)
                b = bank()
                for hd in range(4):
                    tr(b, b.ap[:, hd * P:(hd + 1) * P], Am[:, hd * P:(hd + 1) * P], (V,), last=(hd == 3))
                b.free(cp(V, AT, b.ap[:, :], (PE,)))
                I4 = bc(ident, 1, 4)
                for Y, Z in ((Xm, Am), (XT, AT)):
                    tt(V, heads(Y, 4), heads(Z, 4), bc(C("lvl0"), 1, 4), ALU.mult)
                    tt(V, heads(Y, 4), I4, heads(Y, 4), ALU.subtract)
                Bm = Dm
                for lv in range(1, 7):
                    tt(V, heads(Bm, 4), heads(AT, 4), bc(C(f"lvl{lv}"), 1, 4), ALU.mult, (PE,))
                    b = bank()
                    for hd in range(4):
                        s = slice(hd * P, (hd + 1) * P)
                        mm(b, b.ap[:, s], Bm[:, s], Xm[:, s], after=(V,), last=(hd == 3))
                    b.free(cp(V, Pm, b.ap[:, :], (PE,)))
                    b2 = bank()
                    for hd in range(4):
                        s = slice(hd * P, (hd + 1) * P)
                        mm(b2, b2.ap[:, s], Pm[:, s], XT[:, s], after=(V,), last=(hd == 3))
                    if lv < 6:
                        b = bank()
                        for hd in range(4):
                            s = slice(hd * P, (hd + 1) * P)
                            mm(b, b.ap[:, s], XT[:, s], Pm[:, s], last=(hd == 3))
                        b.free(tt(V, Xm, Xm, b.ap[:, :], ALU.subtract, (PE,)))
                    b2.free(tt(V, XT, XT, b2.ap[:, :], ALU.subtract, (PE,)))
                Gk, Gv = GG[:, 0, c, :], GG[:, 1, c, :]
                rv, rk, U, WT, vn, kt, qe = Dm, Am, Tm(8), Tm(9), Tm(11), Xm, Tm(12)
                tt(V, heads(rv, 4), heads(Gv, 4), bc(bec, 2, P), ALU.mult, (PE,))
                tt(V, heads(rk, 4), heads(Gk, 4), bc(bec, 2, P), ALU.mult)
                tt(V, heads(rk, 4), heads(rk, 4), bc(gc, 2, P), ALU.mult)
                tt(V, heads(kt, 4), heads(Gk, 4), bc(ekt, 2, P), ALU.mult)
                b = bank()
                for hd in range(4):
                    s = slice(hd * P, (hd + 1) * P)
                    mm(b, b.ap[:, s], XT[:, s], rv[:, s], after=(V,), last=(hd == 3))
                b.free(cp(V, U, b.ap[:, :], (PE,)))
                b = bank()
                for hd in range(4):
                    s = slice(hd * P, (hd + 1) * P)
                    mm(b, b.ap[:, s], rk[:, s], XT[:, s], after=(V,), last=(hd == 3))
                b.free(cp(V, WT, b.ap[:, :], (PE,)))
                S = S4[:, 2 + dr, :]
                b = bank()
                for hd in range(4):
                    s = slice(hd * P, (hd + 1) * P)
                    mm(b, b.ap[:, s], WT[:, s], S[:, s], after=(V,), last=(hd == 3))
                b.free(tt(V, vn, U, b.ap[:, :], ALU.subtract, (PE,)))
                if x_side:
                    kq = bank()
                    for hd in range(4):
                        s = slice(hd * P, (hd + 1) * P)
                        mm(kq, kq.ap[:, s], GkT[:, hd, c * P:(c + 1) * P], GqT[:, hd, c * P:(c + 1) * P],
                           after=(V, A), last=(hd == 3))
                    kq.free(tt(V, DT, DT, kq.ap[:, :], ALU.mult, (PE,)))
                    act(qe, GR, ACT.Exp, (PE, V))
                    tt(V, heads(qe, 4), heads(qe, 4), GqT[:, :, c * P:(c + 1) * P], ALU.mult, (A,))
                    b = bank()
                    for hd in range(4):
                        s = slice(hd * P, (hd + 1) * P)
                        mm(b, b.ap[:, s], DT[:, s], vn[:, s], True, False, (V,))
                        mm(b, b.ap[:, s], qe[:, s], S[:, s], False, True, (V,), last=(hd == 3))
                    b.free(tt(V, Ogdn[:, c, :], Ogdn[:, c, :], b.ap[:, :], ALU.add, (PE,)))
                b = bank()
                for hd in range(4):
                    s = slice(hd * P, (hd + 1) * P)
                    mm(b, b.ap[:, s], kt[:, s], vn[:, s], after=(V,), last=(hd == 3))
                tt(V, heads(S, 4), heads(S, 4), bc(eg, 2, P), ALU.mult, (PE,))
                b.free(tt(V, S, S, b.ap[:, :], ALU.add))

            def ret_chunk(dr, c, x_side):
                S = S4[:, dr, :]
                kd, qe = Tm(13), Tm(14)
                if x_side:
                    for hd in range(4):
                        act(qe[:, hd * P:(hd + 1) * P], C("up1") if dr == 0 else C("down"), ACT.Exp, (PE, V),
                            scale=rd[:, 4 * dr + hd:4 * dr + hd + 1])
                    tt(V, heads(qe, 4), heads(qe, 4), RqT[:, :, c * P:(c + 1) * P], ALU.mult, (A,))
                    b = bank()
                    for hd in range(4):
                        s = slice(hd * P, (hd + 1) * P)
                        mm(b, b.ap[:, s], qe[:, s], S[:, s], after=(V,), last=(hd == 3))
                    b.free(tt(V, Oret[:, c, :], Oret[:, c, :], b.ap[:, :], ALU.add, (PE,)))
                    if dr == 0:
                        b = bank()
                        for hd in range(4):
                            s = slice(hd * P, (hd + 1) * P)
                            mm(b, b.ap[:, s], RkT[:, hd, c * P:(c + 1) * P], RqT[:, hd, c * P:(c + 1) * P],
                               after=(V, A), last=(hd == 3))
                        b.free(tt(V, kd, Dret, b.ap[:, :], ALU.mult, (PE,)))
                        b = bank()
                        for hd in range(4):
                            s = slice(hd * P, (hd + 1) * P)
                            mm(b, b.ap[:, s], kd[:, s], Rv[:, c, s], after=(V,), last=(hd == 3))
                        b.free(tt(V, Oret[:, c, :], Oret[:, c, :], b.ap[:, :], ALU.add, (PE,)))
                tt(V, heads(kd, 4), heads(Rk[:, c, :], 4), bc(dec[:, 4 * dr:4 * dr + 4], 2, P), ALU.mult, (PE,))
                b = bank()
                for hd in range(4):
                    s = slice(hd * P, (hd + 1) * P)
                    mm(b, b.ap[:, s], kd[:, s], Rv[:, c, s], after=(V,), last=(hd == 3))
                tt(V, heads(S, 4), heads(S, 4), bc(cd[:, 4 * dr:4 * dr + 4], 2, P), ALU.mult, (PE,))
                b.free(tt(V, S, S, b.ap[:, :], ALU.add))

            def mixers(x_side):
                for c in range(2):
                    gdn_matrices(c)
                    gdn_chunk(0, c, x_side)
                    ret_chunk(0, c, x_side)
                for c in (1, 0):
                    gdn_matrices(c)
                    gdn_chunk(1, c, x_side)
                    ret_chunk(1, c, x_side)

            V.op(lambda e: e.memset(ar(10240, 4096), 0.0), (A, PE))
            ctx_sb = ar(16384, 2048).rearrange("p (c n) -> p c n", c=2)
            cslot, before = take(2)
            SP.dma(lambda e: e.dma_start(cslot.ap.rearrange("p (c n) -> p c n", c=2),
                                         d["ctx"].rearrange("(c p) n -> p c n", p=P)), before, ring_sems[cslot.first])
            cx = cslot.ap.rearrange("p (c n) -> p c n", c=2)
            A.hold_for(cslot.ready)
            V.hold_for(cslot.ready)
            normed(cx, gsc, cmT[:, 0:8], ctx_sb)
            cslot.free(V.now)
            show("hc", hT_sb[:, :], (V, A))
            features(False)
            mixers(False)
            for i in range(4):
                show(f"init{i}", S4[:, i, :], (V,))
            normed(h, gsx, modT[:, 0:8], ctx_sb)
            show("hx", hT_sb[:, :], (V, A))
            features(True)
            show("rk", Rk, (V,))
            show("gk", GG[:, 0, :, :], (V,))
            show("gq", GG[:, 2, :, :], (V,))
            show("log_a", la, (V,))
            show("beta", be, (A,))
            mixers(True)
            show("ret_x", Oret, (V,))
            show("gdn_x", Ogdn, (V,))

            gt = ar(14336, 4096).rearrange("p (c n) -> p c n", c=2)
            rg = ar(0, 1024).rearrange("p (c n) -> p c n", c=2)
            gz = ar(1024, 1024).rearrange("p (c n) -> p c n", c=2)
            t5 = ar(2048, 512)
            yT = ar(3072, 2048).rearrange("p (k t) -> p k t", k=8)
            mg = ar(5120, 2048).rearrange("p (c n) -> p c n", c=2)
            for dst, i in ((rg, 5), (gz, 7)):
                w = load(d["w_in2"][i])

                def out(c, ps, dst=dst):
                    act(dst[:, c, :], ps, ACT.Sigmoid, (PE, V))
                    return tt(V, dst[:, c, :], dst[:, c, :], ps, ALU.mult, (A,))
                token_mm(hT, w, 512, out, (V, A))
                w.free(PE.now)
            for i in range(4):
                w = load(d["w_in2"][8 + i])

                def out(c, ps, i=i):
                    return act(gt[:, c, i * 512:(i + 1) * 512], ps, ACT.Sigmoid, (PE, V))
                token_mm(hT, w, 512, out, (V, A))
                w.free(PE.now)
            nw = load_row("rows", 12)
            for c in range(2):
                y = Oret[:, c, :]
                red(st["sum"][:, 0:4], heads(y, 4))
                ts(V, st["sum"][:, 0:4], st["sum"][:, 0:4], -1.0 / P, None, ALU.mult, None)
                tt(V, heads(y, 4), heads(y, 4), bc(st["sum"][:, 0:4], 2, P), ALU.add)
                for y, g, o in ((Oret[:, c, :], rg, 0), (Ogdn[:, c, :], gz, 512)):
                    tt(V, t5, y, y, ALU.mult)
                    red(st["ss"][:, 0:4], heads(t5, 4))
                    rsqrt(st["rs"][:, 0:4], st["ss"][:, 0:4], 1.0 / P, 1e-6)
                    tt(V, heads(y, 4), heads(y, 4), bc(st["rs"][:, 0:4], 2, P), ALU.mult)
                    tt(V, y, y, nw.ap[:, o:o + 512], ALU.mult, (nw.ready,))
                    tt(V, y, y, g[:, c, :], ALU.mult)
            nw.free(V.now)
            transpose_to(yT[:, 0:4, :], lambda c, k: Oret[:, c, k * P:(k + 1) * P], 4, (V,))
            transpose_to(yT[:, 4:8, :], lambda c, k: Ogdn[:, c, k * P:(k + 1) * P], 4, (V,))
            for s, name in ((0, "w_ret_out"), (1, "w_gdn_out")):
                w = load(d[name])
                for i in range(2):
                    def out(c, ps, i=i, s=s):
                        g = gt[:, c, s * 1024 + i * 512:s * 1024 + i * 512 + 512]
                        m = mg[:, c, i * 512:(i + 1) * 512]
                        if s == 0:
                            return tt(V, m, g, ps, ALU.mult, (PE, A))
                        u = tt(V, g, g, ps, ALU.mult, (PE, A))
                        tt(V, m, m, g, ALU.add)
                        return u
                    token_mm(yT[:, s * 4:s * 4 + 4, :], w, 512, out, (V, A), nk=4, woff=i * 512, wstride=1024)
                w.free(PE.now)
            transpose_to(hT, lambda c, k: mg[:, c, k * P:(k + 1) * P], 8, (V, PE))
            mo = gt[:, :, 0:1024]
            for i in range(2):
                w = load(d["w_o2"][i])

                def out(c, ps, i=i):
                    return cp(V, mo[:, c, i * 512:(i + 1) * 512], ps, (PE,))
                token_mm(hT, w, 512, out, (V, A))
                w.free(PE.now)

            def add_gated(y, row, gate, gb, scr):
                for i in range(2):
                    b = bank()
                    for j in range(4):
                        k = 4 * i + j
                        cp(V, scr[:, 0, j * P:(j + 1) * P], gate[:, k:k + 1].to_broadcast([P, P]), (PE, A))
                    for j in range(4):
                        mm(b, b.ap[:, j * P:(j + 1) * P], scr[:, 0, j * P:(j + 1) * P], ident, after=(V,), last=(j == 3))
                    b.free(cp(V, gb[:, i * 512:(i + 1) * 512], b.ap[:, :], (PE,)))
                w = load_row("rows", row)
                tt(V, gb, gb, w.ap, ALU.mult, (w.ready,))
                w.free(V.now)
                rms_rows(scr, y, D)
                for c in range(2):
                    stt(y[:, c, :], y[:, c, :], st["rs"][:, c:c + 1], gb, ALU.mult, ALU.mult, (A,))
                    tt(V, h[:, c, :], h[:, c, :], y[:, c, :], ALU.add)

            add_gated(mo, 13, modT[:, 16:24], ar(7168, 1024), ar(8192, 2048).rearrange("p (c n) -> p c n", c=2))
            show("xmix", h_sb[:, :], (V,))
            normed(h, gs2, modT[:, 24:32], ctx_sb)
            moe(ctx_sb, modT, add_gated, gs2)

        def moe(xn, modT, add_gated, gs2):
            Wt = ar(0, 128).rearrange("p (c n) -> p c n", c=2)
            sg = ar(128, 128).rearrange("p (c n) -> p c n", c=2)
            bi = ar(256, 128).rearrange("p (c n) -> p c n", c=2)
            Mk = ar(384, 128).rearrange("p (c n) -> p c n", c=2)
            g8, m8, kp = ar(512, 64), ar(576, 8), ar(584, 8)
            gsum, ssum, big = ar(592, 8), ar(600, 8), ar(608, 64)
            TW = ar(672, 256).rearrange("p (c e x) -> p c e x", c=2, x=2)
            rk = ar(928, 128).rearrange("p (c n) -> p c n", c=2)
            ST = ar(1056, 256).rearrange("p (w e x) -> p w e x", w=2, x=2)
            ig, isc = ar(1312, 128), ar(1440, 128)
            OH = ar(1568, 2048).rearrange("p (c e s) -> p c e s", c=2, e=8)
            ysh = ar(3616, 2048).rearrange("p (c n) -> p c n", c=2)
            xg = [ar(5664 + 1024 * i, 1024) for i in range(4)]
            XT = [ar(9760 + 1024 * i, 1024) for i in range(2)]
            yb = [ar(11808 + 1024 * i, 1024) for i in range(2)]
            sgm = [ar(13856 + 512 * i, 512) for i in range(2)]
            hid = [ar(14880 + 512 * i, 512) for i in range(2)]
            yin = ar(18432, 2048).rearrange("p (c n) -> p c n", c=2)
            sh2 = modT[:, 24:32]

            SP.dma(lambda e: e.dma_start(x_tab.rearrange("(c p) n -> p c n", p=P), xn), [V.now], s_tab)
            V.op(lambda e: e.memset(yin, 0.0), (PE, A))
            V.op(lambda e: e.memset(yb[0], 0.0))
            SP.dma(lambda e: e.dma_start(y_tab[0:T, :].rearrange("(c p) n -> p c n", p=P), yin), [V.now], s_tab)
            SP.dma(lambda e: e.dma_start(y_tab[T:T + P, :], yb[0]), [V.now], s_tab)
            tab_ready = (s_tab, 48)

            rbs = load(d["router_bias"].to_broadcast([P, 64]), 1)
            w = load(d["w_router"], 1)

            def router_out(c, ps):
                act(sg[:, c, :], ps, ACT.Exp, (PE, V), scale=-1.0)
                u = A.now
                ts(V, sg[:, c, :], sg[:, c, :], 1.0, None, ALU.add, None, (A,))
                V.op(lambda e: e.reciprocal(sg[:, c, :], sg[:, c, :]))
                tt(V, bi[:, c, :], sg[:, c, :], rbs.ap[:, 0:64], ALU.add, (rbs.ready,))
                return u
            token_mm(hT, w, 64, router_out, (V, A), wstride=64)
            w.free(PE.now)
            rbs.free(V.now)
            for c in range(2):
                for g in range(8):
                    V.op(lambda e, g=g, c=c: e.max(out=g8[:, 8 * g:8 * g + 8], in_=bi[:, c, 8 * g:8 * g + 8]))
                gv = heads(g8, 8)
                tt(V, gsum, gv[:, :, 0:1].rearrange("p a b -> p (a b)"), gv[:, :, 1:2].rearrange("p a b -> p (a b)"),
                   ALU.add)
                V.op(lambda e: e.max(out=m8, in_=gsum))
                V.op(lambda e: e.memset(m8[:, 4:8], 3e38))
                V.op(lambda e: e.match_replace(out=kp, in_to_replace=m8, in_values=gsum, imm_value=-2e38))
                ts(V, kp, kp, -1e38, -1e30, ALU.is_gt, ALU.mult)
                cb = Mk[:, c, :]
                tt(V, heads(cb, 8), heads(bi[:, c, :], 8), bc(kp, 2, 8), ALU.add)
                topm(m8, cb)
                ts(V, cb, cb, -1e38, None, ALU.is_lt, None)
                tt(V, Wt[:, c, :], sg[:, c, :], cb, ALU.mult)
                red(ssum[:, 0:1], Wt[:, c, :])
                V.op(lambda e: e.reciprocal(ssum[:, 0:1], ssum[:, 0:1]))
                ts(V, Wt[:, c, :], Wt[:, c, :], ssum[:, 0:1], 2.5, ALU.mult, ALU.mult)
                cp(V, TW[:, c, :, 1], Wt[:, c, :])
                ts(V, big, C("ones")[:, 0:64], C("col"), float(1 + c * P), ALU.mult, ALU.add)
                cp(V, TW[:, c, :, 0], big)
            for c in range(2):
                b = bank()
                if c == 1:
                    mm(b, b.ap[:, 0:64], C("ones"), Mk[:, 0, :], True, False, (V,))
                mm(b, b.ap[:, 0:64], C("up"), Mk[:, c, :], c == 0, True, (V,), last=True)
                b.free(cp(V, rk[:, c, :], b.ap[:, 0:64], (PE,)))
                stt(rk[:, c, :], Mk[:, c, :], -1000.0, rk[:, c, :], ALU.mult, ALU.add)
                ts(V, rk[:, c, :], rk[:, c, :], 1000.0, None, ALU.add, None)
            b = bank()
            for c in range(2):
                mm(b, b.ap[:, 0:64], C("ones"), Mk[:, c, :], c == 0, c == 1, (V,), last=(c == 1))
            b.free(red(ssum[:, 0:1], b.ap[:, 0:64], ALU.max, (PE,)))
            ts(V, ssum[:, 0:1], ssum[:, 0:1], float(P), None, ALU.is_gt, None)
            over = cp(V, flag[:, 0:1], ssum[:, 0:1])
            b = bank()
            for wave in range(2):
                for e0 in range(0, 64, 8):
                    for c in range(2):
                        tt(V, OH[:, c, :, :], bc(C("iota")[:, wave * P:(wave + 1) * P], 1, 8),
                           bc(rk[:, c, e0:e0 + 8], 2, P), ALU.is_equal, (PE,))
                    for j in range(8):
                        for c in range(2):
                            o = (wave * 64 + e0 + j) * 2
                            mm(b, b.ap[:, o:o + 2], OH[:, c, j, :], TW[:, c, e0 + j, :], c == 0, c == 1, (V,),
                               last=(j == 7 and c == 1))
            b.free(cp(V, ST, b.ap[:, 0:256].rearrange("p (w e x) -> p w e x", w=2, x=2), (PE,)))
            v = ST[:, :, :, 0]
            igv, isv = ig.rearrange("p (w e) -> p w e", w=2), isc.rearrange("p (w e) -> p w e", w=2)
            ts(V, igv, v, -1.0, 0.0, ALU.add, ALU.max)
            cp(V, iu[:, 0:128], ig, (G,))
            ts(V, isv, v, 0.0, None, ALU.is_equal, None)
            ts(V, isc, isc, C("col257"), None, ALU.mult, None)
            tt(V, isv, isv, v, ALU.add)
            ts(V, isc, isc, -1.0, None, ALU.add, None)
            i_ready = cp(V, iu[:, 128:256], isc)

            wg, wd = load(d["w_gu_sh"]), load(d["w_down_sh"])
            bg, bu = bank(), bank()
            for f in range(4):
                bb = bg if f < 2 else bu
                feat_mm(hT, wg, f, bb.ap[:, (f % 2) * 256:(f % 2 + 1) * 256], bb, (V, A))
            wg.free(PE.now)
            act(sgm[0], bg.ap[:, :], ACT.Sigmoid, (PE, V))
            tt(V, sgm[0], sgm[0], bg.ap[:, :], ALU.mult, (A,))
            bg.free(V.now)
            bu.free(tt(V, hid[0], sgm[0], bu.ap[:, :], ALU.mult))
            hv = hid[0].rearrange("p (f t) -> p f t", f=2)
            for c in range(2):
                for n in range(2):
                    b = bank()
                    for f in range(2):
                        mm(b, b.ap[:, :], hv[:, f, c * P:(c + 1) * P],
                           wd.ap[:, f * 1024 + n * 512:f * 1024 + n * 512 + 512], f == 0, f == 1, (wd.ready, V),
                           last=(f == 1))
                    b.free(cp((V, A)[n], ysh[:, c, n * 512:(n + 1) * 512], b.ap[:, :], (PE,)))
            wd.free(PE.now)

            def experts(wave, sems, x_sems, base):
                got, xt_done, hid_done, y_done, xt_ev, used_y = {}, {}, {}, {}, {}, {}
                h_done, w_of, banks_of = {}, {}, {}
                start = (V.now, A.now, PE.now)

                def fetch(e):
                    after = [i_ready, tab_ready, *start]
                    if e >= 4:
                        after.append(xt_done[e - 4])
                    n = e % 4
                    G.dma(lambda g: g.indirect_dma_start(
                        out=xg[n], out_offset=None, in_=x_tab,
                        in_offset=bass.IndirectOffsetOnAxis(ap=iu[:, wave * 64 + e:wave * 64 + e + 1], axis=0)),
                        after, x_sems[n])
                    got[e] = (x_sems[n], 16 * (e // 4 + 1))

                def turn(e):
                    w_of[e] = (load(d["w_gu"][e], sems=sems), load(d["w_down"][e], sems=sems))
                    x, o = xg[e % 4], XT[e % 2]
                    after_x = [h_done[e - 2]] if e >= 2 else []
                    marks = []
                    for k0 in (0, 4):
                        b = bank()
                        for j in range(4):
                            tr(b, b.ap[:, j * P:(j + 1) * P], x[:, (k0 + j) * P:(k0 + j + 1) * P], (got[e],),
                               last=(j == 3))
                        for j in range(4):
                            k = k0 + j
                            a, r = o[:, k * P:(k + 1) * P], b.ap[:, j * P:(j + 1) * P]
                            if k0 == 0:
                                u = ts(V, a, r, gs2[:, k:k + 1], sh2[:, k:k + 1], ALU.mult, ALU.add,
                                       (PE, *after_x), chain=False)
                            else:
                                u = A.op(lambda q, a=a, r=r, k=k: q.activation(
                                    a, r, ACT.Identity, bias=sh2[:, k:k + 1], scale=gs2[:, k:k + 1]),
                                    (PE, *after_x), chain=False)
                        b.free(u)
                        marks.append(u)
                    xt_done[e] = PE.now
                    xt_ev[e] = marks

                def up(e):
                    wg, wd = w_of[e]
                    o = XT[e % 2]
                    b, b2 = bank(), bank()
                    for f in range(4):
                        bb = b if f < 2 else b2
                        for k in range(8):
                            mm(bb, bb.ap[:, (f % 2) * P:(f % 2 + 1) * P], wg.ap[:, k * 512 + f * P:k * 512 + (f + 1) * P],
                               o[:, k * P:(k + 1) * P], k == 0, k == 7, (wg.ready, *xt_ev[e]), last=(k == 7 and f % 2 == 1))
                        if f == 1:
                            tg = PE.now
                    wg.free(PE.now)
                    h_done[e] = PE.now
                    s, hd = sgm[e % 2][:, 0:256], hid[e % 2][:, 0:256]
                    prior = [used_y[e - 2][0]] if e >= 2 else []
                    t = act(s, b.ap[:, 0:256], ACT.Sigmoid, (tg, *prior, *([hid_done[e - 2]] if e >= 2 else [])))
                    b.free(tt(V, s, s, b.ap[:, 0:256], ALU.mult, (t,)))
                    hid_done[e] = tt(V, hd, s, b2.ap[:, 0:256], ALU.mult, (h_done[e], *prior))
                    b2.free(hid_done[e])

                def down(e):
                    wg, wd = w_of[e]
                    hd = hid[e % 2][:, 0:256].rearrange("p (f t) -> p f t", f=2)
                    y = yb[e % 2]
                    wcol = ST[:, wave, e, 1:2]
                    ev = []
                    for n in range(2):
                        b = bank()
                        for f in range(2):
                            mm(b, b.ap[:, :], hd[:, f, :], wd.ap[:, f * 1024 + n * 512:f * 1024 + n * 512 + 512],
                               f == 0, f == 1, (wd.ready, hid_done[e]), last=(f == 1))
                        o = y[:, n * 512:(n + 1) * 512]
                        free = [y_done[e - 2]] if e >= 2 else []
                        if n == 0:
                            u = ts(V, o, b.ap[:, :], wcol, None, ALU.mult, None, (PE, *free))
                        else:
                            u = A.op(lambda q, o=o, b=b: q.activation(o, b.ap[:, :], ACT.Copy, scale=wcol),
                                     (PE, *free))
                        b.free(u)
                        ev.append(u)
                    used_y[e] = (PE.now,)
                    wd.free(PE.now)
                    n_y[0] += 16
                    G.dma(lambda g: g.indirect_dma_start(
                        out=y_tab, out_offset=bass.IndirectOffsetOnAxis(
                            ap=iu[:, 128 + wave * 64 + e:128 + wave * 64 + e + 1], axis=0),
                        in_=y, in_offset=None, compute_op=ALU.add), [*ev, (base, n_y[0] - 16)], base)
                    y_done[e] = (base, n_y[0])

                n_y = [0]
                for e in range(3):
                    fetch(e)
                turn(0)
                for e in range(65):
                    if e + 1 < 64:
                        turn(e + 1)
                    if e < 64:
                        up(e)
                        if e + 3 < 64:
                            fetch(e + 3)
                    if e >= 1:
                        down(e - 1)
                return (base, n_y[0])

            done = experts(0, None, xg_sems, s_y)
            for q in (PE, V, A, G, SP):
                q.begin_if(flag, over, done)
            second_done = experts(1, ring2_sems, xg2_sems, s_y2)
            V.op(lambda e: e.memset(m8, 0.0), (second_done, PE, A))
            for q in (PE, V, A, G, SP):
                q.end_if()
            y = yin
            SP.dma(lambda e: e.dma_start(yin, y_tab[0:T, :].rearrange("(c p) n -> p c n", p=P)), [done, V.now], s_yin)
            for c in range(2):
                tt(V, yin[:, c, :], yin[:, c, :], ysh[:, c, :], ALU.add, ((s_yin, 16), A))
            add_gated(y, 14, modT[:, 40:48], ar(5664, 1024), ar(7712, 2048).rearrange("p (c n) -> p c n", c=2))
            SP.dma(lambda e: e.dma_start(y_dram, h), [V.now], s_out)
            n_out[0] += 16

        def topm(m, x):
            V.op(lambda e: e.max(out=m, in_=x))
            V.op(lambda e: e.match_replace(out=x, in_to_replace=m, in_values=x, imm_value=-2e38))

        asm = {n: sm(k) for n, k in (("ss", 16), ("rs", 16), ("mx", 8), ("den", 8), ("snk", 8))}
        iu = sb("iu", 512, U32)
        show("h0", h_sb[:, :], (V,))
        for l in range(LAYERS):
            attention(l)
            show(f"hattn{l}", h_sb[:, :], (V,))
            if stop == f"attn{l}":
                break
            peer(l)
            show(f"h{l + 1}", h_sb[:, :], (V,))
            if stop == f"peer{l}":
                break
        if stop is None:
            second()
        else:
            SP.dma(lambda e: e.dma_start(y_dram, h), [V.now], s_out)
            n_out[0] += 16

        block = ctx.enter_context(nc.Block())

        @block.sync
        def _(e):
            SP.play(e)
            e.wait_ge(s_out, n_out[0])

        @block.gpsimd
        def _(e):
            G.play(e)

        @block.scalar
        def _(e):
            A.play(e)

        @block.vector
        def _(e):
            V.play(e)

        @block.tensor
        def _(e):
            PE.play(e)


TABLES = {"x_tab": T, "y_tab": T + P}


def constants():
    import numpy as np
    f = np.float32
    t = {}
    i = np.arange(P)
    t["ident"] = np.eye(P)
    t["triF"] = (i[:, None] <= i[None, :])
    t["triB"] = (i[:, None] >= i[None, :])
    t["low"] = (i[:, None] > i[None, :])
    t["up"] = (i[:, None] < i[None, :])
    tok = np.arange(T).reshape(2, P)
    dist = np.abs(tok[:, :, None] - np.arange(T)[None, None, :])
    t["dist"] = dist.transpose(1, 0, 2).reshape(P, -1)
    t["mask"] = np.where(dist <= 128, 0.0, -1e30).transpose(1, 0, 2).reshape(P, -1)
    t["iota16"] = np.tile(np.arange(16), (P, 1))
    pos = np.stack([np.arange(T) // 64, np.arange(T) % 64], -1).astype(f)
    inv = (f(10000.0) ** (-np.arange(16, dtype=f) / f(16))).astype(f)
    ang = (pos[:, :, None] * inv).astype(f).reshape(2, P, 32).transpose(1, 0, 2).reshape(P, 64)
    t["cos1"], t["sin1"] = np.cos(ang), np.sin(ang)
    inv = (f(10000.0) ** (-np.arange(32, dtype=f) / f(32))).astype(f)
    ang = np.concatenate([pos[:, 0:1] * inv, pos[:, 1:2] * inv], -1).astype(f)
    ang = ang.reshape(2, P, 64).transpose(1, 0, 2).reshape(P, 128)
    t["cos2"], t["sin2"] = np.cos(ang), np.sin(ang)
    for l in range(7):
        same = (i[:, None] >> (l + 1)) == (i[None, :] >> (l + 1))
        t[f"lvl{l}"] = same & ((i[:, None] >> l) != (i[None, :] >> l))
    t["up1"] = np.tile(i + 1, (P, 1))
    t["down"] = np.tile(P - i, (P, 1))
    t["col"] = i[:, None]
    t["ones"] = np.ones((P, P))
    t["iota"] = np.tile(np.arange(256), (P, 1))
    t["col257"] = i[:, None] + 257
    t["mhalf"] = np.full((P, 16), -0.5)
    t["rel"] = i[None, :] - i[:, None]
    at, o = {}, 0
    for k, v in t.items():
        at[k] = (o, v.shape[1])
        o += v.shape[1]
    return at, o, np.ascontiguousarray(np.concatenate([v.astype(f) for v in t.values()], 1))


CONST_AT, CONST_COLS, CONSTS = constants()


def tiles(w, n=512):
    import numpy as np
    k, m = w.shape[-2:]
    lead = w.shape[:-2]
    v = w.reshape(*lead, k // P, P, m // n, n)
    r = len(lead)
    v = np.moveaxis(v, r + 2, r)
    v = np.moveaxis(v, r + 2, r + 1)
    return np.ascontiguousarray(v).reshape(*lead, m // n, P, k // P * n)


def arrays_of(i):
    import numpy as np
    a = {k: np.asarray(v) for k, v in i.items()}
    r = {"consts": CONSTS, "x": a["x"][0]}
    rows = [a["ln_in_g"], a["ln_in_b"]]
    for l in range(LAYERS):
        rows += [np.concatenate([a["gn_a_g"][l], a["gn_b_g"][l]]), a["ln1_g"][l], a["ln1_b"][l],
                 a["ln2_g"][l], a["ln2_b"][l]]
    rows += [np.concatenate([a["ret_gn_w_2"][0], a["gdn_norm_w_2"][0]]), a["norm_mix_post_2"][0],
             a["norm_ffn_post_2"][0]]
    r["rows"] = np.stack(rows)
    r["qn_g"] = a["qn_g"].reshape(1, -1)
    r["kn_g"] = a["kn_g"].reshape(1, -1)
    r["sink"] = a["sink"].reshape(1, -1)
    r["a_log"] = a["gdn_a_log_2"].reshape(1, -1)
    r["dt_bias"] = a["gdn_dt_bias_2"].reshape(1, -1)
    r["ret_decay"] = a["ret_log_decay_2"].reshape(1, -1)
    cols = lambda v: v.reshape(-1, P).T
    r["b_mod"] = cols(a["b_mod_2"][0])
    r["cvec"] = np.stack([cols(a["c_2"][0]), cols(a["c_ctx_2"])], -1).reshape(P, -1)
    r["conv"] = a["gdn_conv_2"][0].reshape(3, 12, P).transpose(2, 0, 1).reshape(P, -1)
    r["norm_cols"] = np.concatenate([cols(a["norm_mix_pre_2"][0]), cols(a["norm_ffn_pre_2"][0])], 1)
    r["w_in"] = tiles(a["w_in"])
    r["w_o"] = tiles(a["w_o"])
    r["peer_wq"] = tiles(a["peer_wq"])
    r["peer_keys"] = a["peer_keys"].transpose(0, 4, 1, 2, 3).reshape(LAYERS, P, 2048)
    r["peer_u"] = a["peer_u"].reshape(-1, D)
    r["peer_v"] = a["peer_v"].reshape(-1, D)
    r["ctx"] = a["ctx_2"][0]
    r["w_mod"] = tiles(a["w_mod_2"][0])
    w = a["w_in_2"][0]
    r["w_in2"] = tiles(np.concatenate([w[:, 0:2048], w[:, 2064:]], 1))
    r["w_gab"] = tiles(w[:, 2048:2064], 16)[0]
    r["w_ret_out"] = tiles(a["w_ret_out_2"][0], 1024)[0]
    r["w_gdn_out"] = tiles(a["w_gdn_out_2"][0], 1024)[0]
    r["w_o2"] = tiles(a["w_o_2"][0])
    r["w_router"] = tiles(a["w_router_2"][0], 64)[0]
    r["router_bias"] = a["router_bias_2"].reshape(1, -1)
    r["w_gu"] = tiles(np.concatenate([a["w_gate_2"][0], a["w_up_2"][0]], -1))[:, 0]
    r["w_down"] = tiles(a["w_down_2"][0], 1024)[:, 0]
    r["w_gu_sh"] = tiles(np.concatenate([a["w_sh_gate_2"][0], a["w_sh_up_2"][0]], -1))[0]
    r["w_down_sh"] = tiles(a["w_sh_down_2"][0], 1024)[0]
    return {k: np.ascontiguousarray(v) for k, v in r.items()}


def kernel(**inputs):
    import concourse.bacc as _bacc
    from concourse import mybir as _mybir
    from concourse.bass_utils import run_bass_kernel_spmd as _run

    nc = _bacc.Bacc("TRN2", target_bir_lowering=False, num_devices=1)
    arrays, d = {}, {}
    for name, a in arrays_of(inputs).items():
        arrays[f"in_{name}"] = a
        d[name] = nc.dram_tensor(f"in_{name}", a.shape, _mybir.dt.from_np(a.dtype), kind="ExternalInput").ap()
    out = nc.dram_tensor("out_0", (T, D), F32, kind="ExternalOutput").ap()
    for name, rows in TABLES.items():
        d[name] = nc.dram_tensor(name, (rows, D), F32).ap()
    build(nc, d, out)
    r = _run(nc, [arrays], core_ids=[0])
    return r.results[0]["out_0"].reshape(1, T, D)
```

```python
import concourse.bass as bass
from concourse import mybir
from contextlib import ExitStack

P = 128
ALU = mybir.AluOpType
ACT = mybir.ActivationFunctionType
F32 = mybir.dt.float32
U32 = mybir.dt.uint32
AX = mybir.AxisListType.X

T, D, NC_ = 256, 1024, 2
LAYERS = 2
NEXP = 16384
ALPHA = (2.0 * LAYERS) ** 0.25
RING = 20
ARENA = 22528
RATE_U = ((0.6, 0.0), (0.9, 0.9))
RATE_V = (0.6, 0.5)
PE_OF = (1, 2)
GRAIN = 3
AHEAD = 8


class Queue:

    def __init__(self, name, sem, chained):
        self.name, self.sem, self.chained = name, sem, chained
        self.items, self.n, self.pending = [], 0, []

    @property
    def now(self):
        return (self.sem, self.n)

    def op(self, emit, after=(), inc=True, chain=True):
        waits = [a.now if isinstance(a, Queue) else a for a in after] + self.pending
        self.pending = []
        if self.chained and chain and self.n:
            waits.append(self.now)
        if inc:
            self.n += 1
        self.items.append((emit, waits, self.sem if inc else None, 1))
        return self.now

    def hold_for(self, *producers):
        self.pending += [a.now if isinstance(a, Queue) else a for a in producers]

    def dma(self, emit, after, sem):
        self.items.append((emit, after, sem, 16))

    def begin_if(self, flag, *after):
        self.items.append(("if", (flag, after), self.n, 0))

    def end_if(self):
        self.items.append(("end", None, self.n, 0))

    def play(self, eng):
        seen = {}

        def wait(w):
            if isinstance(w, Slot):
                for x in w.released:
                    wait(x)
                return
            s, v = w
            if v and seen.get(s.num, 0) < v:
                seen[s.num] = v
                eng.wait_ge(s, v)

        def run(items):
            for emit, waits, sem, by in items:
                for w in waits:
                    wait(w)
                ins = emit(eng)
                if sem is not None:
                    ins.then_inc(sem, by)

        marks = [i for i, it in enumerate(self.items) if it[0] in ("if", "end")]
        if not marks:
            return run(self.items)
        a, b = marks
        run(self.items[:a])
        flag, after = self.items[a][1]
        for w in after:
            wait(w)
        value = eng.value_load(flag[0:1, 0:1], min_val=0, max_val=1)
        before = dict(seen)
        with eng.If(value > 0):
            run(self.items[a + 1:b])
        n = self.items[b][2] - self.items[a][2]
        if n:
            with eng.Else():
                eng.sem_inc(self.sem, n)
        seen.clear()
        seen.update(before)
        run(self.items[b + 1:])


class Slot:

    def __init__(self, ap, first):
        self.ap, self.first, self.ready, self.released = ap, first, None, []

    def free(self, *tokens):
        self.released.extend(tokens)


def build(nc, d, out, dump=None, stop=None):
    import numpy as np
    ctx = ExitStack()
    with ctx:
        def sb(name, n, dt=F32):
            return ctx.enter_context(nc.sbuf_tensor(name, [P, n], dt))

        def sem(name):
            return ctx.enter_context(nc.semaphore(name))

        y_dram = out.rearrange("(c p) n -> p c n", p=P)
        PE = Queue("pe", sem("s_pe"), False)
        V = Queue("v", sem("s_v"), True)
        A = Queue("a", sem("s_a"), True)
        G = Queue("g", sem("s_g"), True)
        SP = Queue("sp", sem("s_sp"), False)
        s_small = sem("s_small")
        s_out = sem("s_out")
        ring_sems = [sem(f"s_r{i}") for i in range(RING)]
        gath_sems = [sem(f"s_g{i}") for i in range(RING)]
        ring_count, gath_count = [0] * RING, [0] * RING

        ring2_sems = ([sem(f"s_b{i}") for i in range(RING)], [0] * RING)
        xg_sems = [sem(f"s_xg{i}") for i in range(4)]
        xg2_sems = [sem(f"s_xh{i}") for i in range(4)]
        s_tab, s_y, s_y2, s_yin = sem("s_tab"), sem("s_y"), sem("s_y2"), sem("s_yin")
        x_tab, y_tab = d["x_tab"], d["y_tab"]
        flag = ctx.enter_context(nc.sbuf_tensor("flag", [P, 1], U32))
        h_sb = sb("h", 2048)
        hT_sb = sb("hT", 2048)
        ring = sb("ring", RING * 1024)
        arena = sb("arena", ARENA)
        cst = sb("cst", CONST_COLS)
        small = sb("small", 1000)
        idx_u = sb("idx_u", 256, U32)
        banks = [ctx.enter_context(nc.psum_tensor(f"ps{i}", [P, 512], F32)) for i in range(8)]

        h = h_sb[:, :].rearrange("p (c n) -> p c n", c=2)
        hT = hT_sb[:, :].rearrange("p (k t) -> p k t", k=8)

        def C(name):
            o, n = CONST_AT[name]
            return cst[:, o:o + n]

        ident = C("ident")

        small_at = [0]

        def sm(n):
            o = small_at[0]
            small_at[0] += n
            assert small_at[0] <= 1000
            return small[:, o:o + n]

        owners = [None] * RING
        rpos = [0]

        def free_at(i):
            return owners[i] is None or owners[i].released

        def take(k, sems=None, count=None):
            if sems is None:
                sems, count = ring_sems, ring_count if count is None else count
            for _ in range(2 * RING):
                s = rpos[0] % RING
                if s + k <= RING and all(free_at(i) for i in range(s, s + k)):
                    break
                rpos[0] += 1
            else:
                raise ValueError("the ring is full")
            rpos[0] += k
            slot = Slot(ring[:, s * 1024:(s + k) * 1024], s)
            before = []
            for i in range(s, s + k):
                if owners[i] is not None and owners[i] not in before:
                    before.append(owners[i])
                owners[i] = slot
            if count is not False:
                count[s] += 16
                slot.ready = (sems[s], count[s])
            return slot, before

        def load(src, k=None, sems=None):
            n = src.shape[-1]
            k = k or -(-n // 1024)
            sems, count = sems or (ring_sems, ring_count)
            slot, before = take(k, sems, count)
            dst = slot.ap[:, 0:n]
            SP.dma(lambda e: e.dma_start(dst, src), before, sems[slot.first])
            return slot

        def load_row(name, row):
            src = d[name][row:row + 1, :].to_broadcast([P, d[name].shape[1]])
            return load(src)

        free_banks = [Slot(b, i) for i, b in enumerate(banks)]

        def bank():
            old = free_banks.pop(0)
            new = Slot(banks[old.first], old.first)
            new.before = old
            return new

        def need(n):
            while len(free_banks) < n:
                yield

        def release(b, *tokens):
            b.free(*tokens)
            free_banks.append(b)

        def mm(b, o, lhsT, rhs, start=True, stop=True, after=(), last=False):
            t = PE.op(lambda e: e.matmul(o, lhsT, rhs, start=start, stop=stop, skip_group_check=True),
                      (b.before, *after), inc=last)
            if last:
                b.done = t
            return t

        def tr(b, o, src, after=(), last=False):
            t = PE.op(lambda e: e.transpose(o, src, ident), (b.before, *after), inc=last)
            if last:
                b.done = t
            return t

        def run(*gens):
            gens = list(gens)
            while gens:
                for g in list(gens):
                    if next(g, run) is run:
                        gens.remove(g)

        work, credit = [], [0.0]

        def step(rate):
            credit[0] = credit[0] + 2 * rate if work else 0.0
            while credit[0] > 0 and work:
                n = next(work[0], run)
                if n is run:
                    work.pop(0)
                else:
                    credit[0] -= n or 2

        def tt(q, o, a, b, op, after=(), **k):
            return q.op(lambda e: e.tensor_tensor(o, a, b, op), after, **k)

        def ts(q, o, a, s1, s2, op0, op1, after=(), **k):
            if op1 is None:
                return q.op(lambda e: e.tensor_scalar(o, a, s1, None, op0), after, **k)
            return q.op(lambda e: e.tensor_scalar(o, a, s1, s2, op0, op1), after, **k)

        def stt(o, a, s, b, op0, op1, after=(), **k):
            return V.op(lambda e: e.scalar_tensor_tensor(out=o, in0=a, scalar=s, in1=b, op0=op0, op1=op1), after, **k)

        def rsqrt(o, a, scale, eps, after=()):
            ts(V, o, a, scale, eps, ALU.mult, ALU.add, after)
            n = o.shape[-1]
            t = tt(G, o, o, C("mhalf")[:, 0:n], ALU.pow, (V,))
            V.hold_for(t)
            return t

        def red(o, a, op=ALU.add, after=()):
            return V.op(lambda e: e.tensor_reduce(o, a, AX, op), after)

        def act(o, a, f, after=(), **k):
            return A.op(lambda e: e.activation(o, a, f, **k), after)

        def cp(q, o, a, after=()):
            if q is A:
                return A.op(lambda e: e.activation(o, a, ACT.Copy), after)
            return q.op(lambda e: e.tensor_copy(o, a), after)

        def bc(a, axis, n):
            u = a.unsqueeze(axis)
            s = list(u.shape)
            s[axis] = n
            return u.to_broadcast(s)

        def heads(a, n):
            return a.rearrange("p (h x) -> p h x", h=n)

        def show(name, ap, after):
            if dump is not None and not name.startswith("mid"):
                n = 1
                for x in ap.shape[1:]:
                    n *= x
                o = dump(name, [P] + list(ap.shape[1:]))
                SP.dma(lambda e: e.dma_start(o, ap), [V.now, A.now, G.now], dump_sem(name))
                for q in (V, A, G, PE):
                    q.hold_for((dump_sems[-1], 16))

        n_out = [0]
        dump_sems = []

        def dump_sem(name):
            dump_sems.append(sem(f"s_d_{name}"))
            return dump_sems[-1]

        SP.dma(lambda e: e.dma_start(cst[:, :], d["consts"]), [], s_small)
        SP.dma(lambda e: e.dma_start(h, d["x"].rearrange("(c p) n -> p c n", p=P)), [], s_small)
        smalls = {}
        n_small = 32
        for name in ("qn_g", "kn_g", "sink", "a_log", "dt_bias", "ret_decay"):
            n = d[name].shape[1]
            smalls[name] = sm(n)
            SP.dma(lambda e, o=smalls[name], s=d[name].to_broadcast([P, n]): e.dma_start(o, s), [], s_small)
            n_small += 16
        for name in ("b_mod", "cvec", "conv", "norm_cols", "router_bias"):
            if name == "router_bias":
                continue
            n = d[name].shape[1]
            smalls[name] = sm(n)
            SP.dma(lambda e, o=smalls[name], s=d[name]: e.dma_start(o, s), [], s_small)
            n_small += 16
        loaded = (s_small, n_small)

        asm = {n: sm(k) for n, k in (("ss", 16), ("rs", 16), ("s8", 8))}
        for i in range(2):
            asm |= {f"{n}{i}": sm(k) for n, k in (("ms", 16), ("mr", 16))}
        iu = sb("iu", 512, U32)

        st = {n: sm(8) for n in ("sum", "ss", "rs")}

        def transpose_to(dst, src_of, nk, after, affine=None, chunks=(0, 1)):
            todo = []
            for c in chunks:
                for k0 in range(0, nk, 4):
                    yield from need(1)
                    b = bank()
                    for j in range(4):
                        tr(b, b.ap[:, j * P:(j + 1) * P], src_of(c, k0 + j), after, last=(j == 3))
                    todo.append((b, c, k0))
                    if len(todo) == 2:
                        yield
                        while todo:
                            turned(dst, *todo.pop(0), affine)

        def turned(dst, b, c, k0, affine):
            if affine is None:
                q = (V, A)[(k0 // 4 + c) % 2]
                release(b, cp(q, dst[:, k0:k0 + 4, c * P:(c + 1) * P], b.ap[:, :].rearrange("p (k t) -> p k t", k=4),
                              (b.done,)))
                return
            for j in range(4):
                s1, s2 = affine(k0 + j)
                o, r = dst[:, k0 + j, c * P:(c + 1) * P], b.ap[:, j * P:(j + 1) * P]
                if k0 == 0:
                    u = ts(V, o, r, s1, s2, ALU.mult, ALU.add, (b.done,))
                else:
                    u = A.op(lambda e, o=o, r=r, s1=s1, s2=s2: e.activation(o, r, ACT.Identity, bias=s2, scale=s1),
                             (b.done, V))
            release(b, u)

        def token_mm(xT, w, n, take_out, after, nk=8, woff=0, wstride=512, grain=8):
            wv = w.ap
            yield 12 if nk == 8 and n > 64 else 2
            yield from need(2)
            bs = [bank(), bank()]
            for c in range(2):
                b = bs[c]
                for k in range(nk):
                    mm(b, b.ap[:, 0:n], xT[:, k, c * P:(c + 1) * P], wv[:, woff + k * wstride:woff + k * wstride + n],
                       k == 0, k == nk - 1, (w.ready, *after), last=(k == nk - 1))
                    if k % grain == grain - 1 and k < nk - 1:
                        yield
                yield 7 if n > 64 else 2
            for i in range(2):
                release(bs[i], take_out(i, bs[i], bs[i].ap[:, 0:n]))

        def feat_mm(xT, w, m, o, b, after):
            for k in range(8):
                mm(b, o, w.ap[:, k * 512 + m * P:k * 512 + (m + 1) * P], xT[:, k, :],
                   k == 0, k == 7, (w.ready, *after), last=(k == 7))

        def layer_norm(g, b, scratch, chunks=(0, 1)):
            s, q, r = st["sum"], st["ss"], st["rs"]
            for c in chunks:
                red(s[:, c:c + 1], h[:, c, :], after=(A, G))
            for c in chunks:
                ts(V, s[:, c:c + 1], s[:, c:c + 1], -1.0 / D, None, ALU.mult, None)
                x = h[:, c, :]
                u = ts(V, x, x, s[:, c:c + 1], None, ALU.add, None)
                act(scratch, x, ACT.Square, (u,), accum_out=q[:, c:c + 1])
            part = slice(chunks[0], chunks[-1] + 1)
            rsqrt(r[:, part], q[:, part], 1.0 / D, 1e-5, (A,))
            for c in chunks:
                x = h[:, c, :]
                stt(x, x, r[:, c:c + 1], g.ap, ALU.mult, ALU.mult, (g.ready,))
                tt(V, x, x, b.ap, ALU.add, (b.ready,))
            g.free(V.now)
            b.free(V.now)

        def ar(o, n):
            assert o + n <= ARENA
            return arena[:, o:o + n]

        V.op(lambda e: e.memset(st["sum"], 0.0), (loaded,))
        PE.op(lambda e: e.transpose(banks[0][:, 0:P], ident, ident), (loaded,), inc=True)
        A.op(lambda e: e.activation(st["ss"], st["sum"], ACT.Copy), (loaded, V))
        G.op(lambda e: e.memset(st["rs"], 0.0), (loaded,))
        free_banks[0].free(PE.now)
        lnscr = ar(0, 1024)
        g0, b0 = load_row("rows", 0), load_row("rows", 1)
        layer_norm(g0, b0, lnscr)

        def attention(l):
            proj = ar(0, 3072).rearrange("p (c n) -> p c n", c=2)
            qkT = ar(3072, 5120).rearrange("p (i t) -> p i t", i=20)
            mix = ar(16384, 2048).rearrange("p (c n) -> p c n", c=2)
            rot = ar(18432, 1280).rearrange("p (c n) -> p c n", c=2)
            w = [load(d["w_in"][l, i]) for i in range(3)]

            def project(i, split):
                def out(c, b, ps):
                    return cp((V, A)[(i + c) % 2], proj[:, c, i * 512:(i + 1) * 512], ps, (b.done,))
                yield from token_mm(hT, w[i], 512, out, (V, A))
                w[i].free(PE.now)

            run(transpose_to(hT, lambda c, k: h[:, c, k * P:(k + 1) * P], 8, (V, A, G)))
            run(project(0, 0))
            run(project(1, 0))

            def rope(c):
                cos, sin = C("cos1"), C("sin1")
                ss, rs = asm["ss"][:, 0:10], asm["rs"][:, 0:10]
                tmp = ar(8192 + 2048 * c, 2048)
                x, r = proj[:, c, 0:640], rot[:, c, :]
                tt(V, tmp[:, 0:640], x, x, ALU.mult, (A,))
                red(ss, heads(tmp[:, 0:640], 10))
                rsqrt(rs, ss, 1.0 / 64, 1e-6)
                tt(V, heads(x, 10), heads(x, 10), bc(rs, 2, 64), ALU.mult)
                tt(V, heads(x[:, 0:512], 8), heads(x[:, 0:512], 8),
                   bc(smalls["qn_g"][:, l * 64:(l + 1) * 64], 1, 8), ALU.mult)
                tt(V, heads(x[:, 512:640], 2), heads(x[:, 512:640], 2),
                   bc(smalls["kn_g"][:, l * 64:(l + 1) * 64], 1, 2), ALU.mult)
                yield
                xv = x.rearrange("p (h a w f) -> p h a w f", h=10, a=2, w=2)
                rv = r.rearrange("p (h a w f) -> p h a w f", h=10, a=2, w=2)
                tv = tmp[:, 0:320].rearrange("p (h a f) -> p h a f", h=10, a=2)
                tg = tmp[:, 1024:1344].rearrange("p (h a f) -> p h a f", h=10, a=2)
                cc = bc(cos[:, c * 32:(c + 1) * 32].rearrange("p (a f) -> p a f", a=2), 1, 10)
                sn = bc(sin[:, c * 32:(c + 1) * 32].rearrange("p (a f) -> p a f", a=2), 1, 10)
                x1, x2 = xv[:, :, :, 0, :], xv[:, :, :, 1, :]
                u = V.now
                tt(V, rv[:, :, :, 0, :], x1, cc, ALU.mult)
                tt(G, tg, x1, sn, ALU.mult, (u,))
                tt(V, tv, x2, sn, ALU.mult)
                tt(G, rv[:, :, :, 1, :], x2, cc, ALU.mult)
                tt(V, rv[:, :, :, 0, :], rv[:, :, :, 0, :], tv, ALU.subtract)
                tt(G, rv[:, :, :, 1, :], rv[:, :, :, 1, :], tg, ALU.add)

            def turn_heads(i0, n):
                todo = []
                for c in range(2):
                    for i in range(i0, i0 + n, 4):
                        b = bank()
                        m = min(4, i0 + n - i)
                        for j in range(m):
                            q = i + j
                            src = rot[:, c, q * 64:(q + 1) * 64] if q < 10 else proj[:, c, 128 + q * 64:192 + q * 64]
                            tr(b, b.ap[0:64, j * P:(j + 1) * P], src, (V, G, A), last=(j == m - 1))
                        todo.append((b, i, c, m))
                        if len(todo) == 2:
                            yield
                            for b, i_, c_, m_ in todo:
                                release(b, cp((V, A)[(i_ // 4) % 2], qkT[0:64, i_:i_ + m_, c_ * P:(c_ + 1) * P],
                                              b.ap[0:64, 0:m_ * P].rearrange("p (k t) -> p k t", k=m_), (b.done,)))
                            todo = []
                for b, i_, c_, m_ in todo:
                    release(b, cp(V, qkT[0:64, i_:i_ + m_, c_ * P:(c_ + 1) * P],
                                  b.ap[0:64, 0:m_ * P].rearrange("p (k t) -> p k t", k=m_), (b.done,)))

            run(project(2, 0), rope(0), rope(1))
            run(turn_heads(10, 10), turn_heads(0, 10))

            def softmax(br, c, lane):
                S = PT = ar(8192 + 2048 * lane, 2048)
                mx, den, snk = (ar(19712 + 24 * lane + 8 * i, 8) for i in range(3))
                voff = 640 if br == 0 else 1408
                dist, mask = C("dist")[:, c * 256:(c + 1) * 256], C("mask")[:, c * 256:(c + 1) * 256]
                if br == 1:
                    for hd in range(8):
                        slope = float(np.float32(2.0 ** (-(hd + 1.0))))
                        stt(S[:, hd * 256:hd * 256 + 256], dist, -slope, mask, ALU.mult, ALU.add, (PE, A))
                Sv = heads(S, 8)
                for k in range(4):
                    b = bank()
                    for hd in (2 * k, 2 * k + 1):
                        mm(b, b.ap[:, (hd % 2) * 256:(hd % 2) * 256 + 256],
                           qkT[0:64, br * 10 + hd, c * P:(c + 1) * P],
                           qkT[0:64, br * 10 + 8 + hd // 4, :], after=(V, A), last=(hd % 2 == 1))
                    yield
                    x = S[:, k * 512:(k + 1) * 512]
                    if br == 0:
                        u = A.op(lambda e, x=x, b=b: e.activation(x, b.ap[:, :], ACT.Copy, scale=0.125), (b.done, V))
                    else:
                        u = stt(x, b.ap[:, :], 0.125, x, ALU.mult, ALU.add, (b.done,))
                    release(b, u)
                red(mx, Sv, ALU.max, (A,))
                if br == 1:
                    tt(V, mx, mx, smalls["sink"][:, l * 8:(l + 1) * 8], ALU.max)
                    tt(V, snk, smalls["sink"][:, l * 8:(l + 1) * 8], mx, ALU.subtract)
                ts(V, mx, mx, -1.0, None, ALU.mult, None)
                for hd in range(8):
                    x = S[:, hd * 256:(hd + 1) * 256]
                    t = act(x, x, ACT.Exp, (V,), bias=mx[:, hd:hd + 1], accum_out=den[:, hd:hd + 1])
                if br == 1:
                    t = act(snk, snk, ACT.Exp)
                yield
                for i0 in range(0, 16, 4):
                    b = bank()
                    for j in range(4):
                        i = i0 + j
                        tr(b, b.ap[:, j * P:(j + 1) * P], S[:, i * P:(i + 1) * P], (t,), last=(j == 3))
                    if i0 == 0:
                        V.hold_for(t)
                        if br == 1:
                            tt(V, den, den, snk, ALU.add)
                        V.op(lambda e: e.reciprocal(den, den))
                    yield
                    release(b, cp((V, A)[(i0 // 4) % 2], PT[:, i0 * P:(i0 + 4) * P], b.ap[:, :], (b.done,)))
                b = bank()
                for hd in range(8):
                    g = hd // 4
                    for s in range(2):
                        mm(b, b.ap[:, hd * 64:(hd + 1) * 64], PT[:, (hd * 2 + s) * P:(hd * 2 + s + 1) * P],
                           proj[:, s, voff + g * 64:voff + (g + 1) * 64], s == 0, s == 1, (V, A),
                           last=(hd == 7 and s == 1))
                yield
                release(b, tt(V, heads(mix[:, c, br * 512:(br + 1) * 512], 8), heads(b.ap[:, :], 8),
                              bc(den, 2, 64), ALU.mult, (b.done,)))

            def lane(i):
                both = [softmax(1, i, 2 * i), softmax(0, i, 2 * i + 1)]
                while both:
                    for g in list(both):
                        if next(g, run) is run:
                            both.remove(g)
                    yield
                m, tmp = mix[:, i, :], ar(8192 + 4096 * i, 1024)
                ss, rs = asm[f"ms{i}"], asm[f"mr{i}"]
                tt(V, tmp, m, m, ALU.mult, (A, PE))
                red(ss, heads(tmp, 16))
                rsqrt(rs, ss, 1.0 / 64, 1e-6)
                tt(V, heads(m, 16), heads(m, 16), bc(rs, 2, 64), ALU.mult)
                tt(V, m, m, gn.ap, ALU.mult, (gn.ready,))
                yield
                yield from transpose_to(hT, lambda c, k: mix[:, c, k * P:(k + 1) * P], 8, (V,), chunks=(i,))

            w = [load(d["w_o"][l, i]) for i in range(2)]
            gn = load_row("rows", 2 + 5 * l)
            g1, b1 = load_row("rows", 3 + 5 * l), load_row("rows", 4 + 5 * l)
            pairs = []
            run(lane(0), lane(1))
            gn.free(V.now)
            for c in range(2):
                for i in range(2):
                    b = bank()
                    for k in range(8):
                        mm(b, b.ap[:, :], hT[:, k, c * P:(c + 1) * P], w[i].ap[:, k * 512:(k + 1) * 512],
                           k == 0, k == 7, (w[i].ready, V, A), last=(k == 7))
                    if c == 1:
                        w[i].free(PE.now)
                    pairs.append((b, c, i))
            for c in range(2):
                for b, _, i in pairs[2 * c:2 * c + 2]:
                    x = h[:, c, i * 512:(i + 1) * 512]
                    release(b, stt(x, x, ALPHA, b.ap[:, :], ALU.mult, ALU.add, (b.done,)))
                layer_norm(g1, b1, ar(8192 + 1024 * c, 1024), (c,))

        def peer(l, background):
            qT = ar(0, 4096).rearrange("p (m t) -> p m t", m=16)
            SC = ar(4096, 2048)
            SC2 = ar(6144, 2048)
            OH = ar(8192, 2048)
            o = [13312]

            def keep(n):
                o[0] += n
                assert o[0] <= 20480
                return ar(o[0] - n, n)

            junk = keep(1024)
            accs = keep(2048).rearrange("p (c n) -> p c n", c=2)
            dg = keep(512)
            v16, i16, tsv = keep(256), keep(256), keep(128)
            pf1, pf2, e1, e2 = (keep(128) for _ in range(4))
            gs, aa, wgt = (keep(256) for _ in range(3))
            i16u = iu[:, 0:256]
            w = [load(d["peer_wq"][l, i]) for i in range(2)]
            kt = load(d["peer_keys"][l])
            for c in range(2):
                run(transpose_to(hT, lambda c, k: h[:, c, k * P:(k + 1) * P], 8, (V, A, G), chunks=(c,)))
            hT_done = (V.now, A.now)
            s8 = asm["s8"]
            i_ready, routed, sc_done = {}, {}, {}

            def queries(i, c):
                b = bank()
                for m in range(4):
                    for k in range(8):
                        mm(b, b.ap[:, m * P:(m + 1) * P], w[i].ap[:, k * 512 + m * P:k * 512 + (m + 1) * P],
                           hT[:, k, c * P:(c + 1) * P], k == 0, k == 7, (w[i].ready, *hT_done),
                           last=(m == 3 and k == 7))
                if c == 1:
                    w[i].free(PE.now)
                release(b, cp(A, qT[:, 4 * i:4 * i + 4, c * P:(c + 1) * P],
                              b.ap[:, :].rearrange("p (m t) -> p m t", m=4), (b.done,)))
                return A.now

            def scores(c, hf, ready):
                for j in range(2 * hf, 2 * hf + 2):
                    b = bank()
                    for m in range(4):
                        hp = 4 * j + m
                        mm(b, b.ap[:, m * P:(m + 1) * P], qT[:, hp, c * P:(c + 1) * P],
                           kt.ap[:, hp * P:(hp + 1) * P], after=(kt.ready, *ready), last=(m == 3))
                    yield
                    release(b, cp(A, SC[:, j * 512:(j + 1) * 512], b.ap[:, :], (b.done, V)))
                sc_done[c, hf] = A.now

            def route(c, hf):
                V.hold_for(sc_done[c, hf], G)
                half, quarter = slice(1024 * hf, 1024 * hf + 1024), slice(64 * hf, 64 * hf + 64)
                sc, sc2, oh = SC[:, half], SC2[:, half], OH[:, 0:1024]
                vv, ii, iif = (x[:, 128 * hf:128 * hf + 128] for x in (v16, i16u, i16))
                yield from topk(8, P, vv, ii, sc, sc2)
                cp(V, iif, ii)
                v4 = vv.rearrange("p (h s k) -> p h s k", h=4, s=2)
                i4 = iif.rearrange("p (h s k) -> p h s k", h=4, s=2)
                cand = sc.rearrange("p (h a b) -> p h a b", h=4, a=16)
                tt(V, cand, bc(v4[:, :, 0, :], 3, 16), bc(v4[:, :, 1, :], 2, 16), ALU.add)
                yield
                pos, pu = iu[:, 256:384][:, quarter], iu[:, 384:512][:, quarter]
                tv, f1, f2, x1, x2 = (x[:, quarter] for x in (tsv, pf1, pf2, e1, e2))
                yield from topk(4, 256, tv, pos, sc, sc2)
                ts(V, pu, pos, 4, None, ALU.logical_shift_right, None)
                cp(V, f1, pu)
                ts(V, pu, pos, 15, None, ALU.bitwise_and, None)
                cp(V, f2, pu)
                for s, pf, ee in ((0, f1, x1), (1, f2, x2)):
                    tt(V, oh.rearrange("p (s k) -> p s k", k=16), bc(C("iota16"), 1, 64), bc(pf, 2, 16), ALU.is_equal)
                    yield
                    o4 = oh.rearrange("p (h s k) -> p h s k", h=4, s=16)
                    tt(V, o4, o4, bc(i4[:, :, s, :], 2, 16), ALU.mult)
                    yield
                    red(ee, oh.rearrange("p (s k) -> p s k", k=16))
                    yield
                stt(x1, x1, 128.0, x2, ALU.mult, ALU.add)
                ts(V, x1, x1, float(l * NEXP), None, ALU.add, None)
                i_ready[c, hf] = cp(V, idx_u[:, c * P + 64 * hf:c * P + 64 * hf + 64], x1)
                yield
                g = gs[:, c * P + 64 * hf:c * P + 64 * hf + 64]
                t3 = heads(tv, 4)
                t = tt(V, heads(g, 4), t3, t3[:, :, 0:1].to_broadcast([P, 4, 16]), ALU.subtract)
                t = act(g, g, ACT.Exp, (t,))
                yield
                red(s8[:, 0:4], heads(g, 4), after=(t,))
                V.op(lambda e: e.reciprocal(s8[:, 0:4], s8[:, 0:4]))
                tt(V, heads(g, 4), heads(g, 4), bc(s8[:, 0:4], 2, 16), ALU.mult)
                routed[c, hf] = True

            def unit(c, hf):
                yield from scores(c, hf, (A.now,))
                if (c, hf) == (1, 1):
                    kt.free(PE.now)
                yield from route(c, hf)

            queries(0, 0)
            t = queries(1, 0)
            queries(0, 1)
            w.append(load(d["peer_wq"][l, 2]))
            run(scores(0, 0, (t,)))
            first = route(0, 0)
            next(first)
            for i, c in ((1, 1), (2, 0), (3, 0), (2, 1), (3, 1)):
                queries(i, c)
                if i == 1:
                    w.append(load(d["peer_wq"][l, 3]))
                next(first)
            run(first)

            def gather(table, c, s):
                slot, before = take(1, gath_sems, gath_count)
                G.dma(lambda e: e.indirect_dma_start(
                    out=slot.ap, out_offset=None, in_=d[table],
                    in_offset=bass.IndirectOffsetOnAxis(ap=idx_u[:, c * P + s:c * P + s + 1], axis=0)),
                    [i_ready[c, s // 64], *before], gath_sems[slot.first])
                return slot

            def dots(c, s, slot):
                slot.free(V.op(lambda e: e.tensor_tensor_reduce(
                    out=junk, in0=slot.ap, in1=h[:, c, :], scale=1.0, scalar=0.0, op0=ALU.mult, op1=ALU.add,
                    accum_out=aa[:, c * P + s:c * P + s + 1]), (slot.ready,)))

            def sums(c, s, slot):
                slot.free(stt(accs[:, c, :], slot.ap, wgt[:, c * P + s:c * P + s + 1], accs[:, c, :],
                              ALU.mult, ALU.add, (slot.ready,)))

            diag_used = [None] * 4

            def pe_sums(c, s, slot, two, first, last, n):
                i = n % 4
                x = dg[:, i * P:(i + 1) * P]
                wcol = wgt[:, c * P + s:c * P + s + 1]
                t = A.op(lambda e: e.activation(x, ident, ACT.Copy, scale=wcol),
                         (w_ready[c], *([diag_used[i]] if diag_used[i] else [])))
                for k in range(2):
                    mm(two[k], two[k].ap[:, :], x, slot.ap[:, k * 512:(k + 1) * 512], first, last,
                       (t, slot.ready), last=(k == 1 or last))
                diag_used[i] = PE.now
                slot.free(PE.now)

            V.op(lambda e: e.memset(accs, 0.0), (A,))
            w_ready = [None, None]
            work[:0] = [unit(0, 1), unit(1, 0), unit(1, 1)]
            work.extend(background)

            def weights(c):
                t = act(wgt[:, c * P:(c + 1) * P], aa[:, c * P:(c + 1) * P], ACT.Gelu, (V,))
                w_ready[c] = tt(V, wgt[:, c * P:(c + 1) * P], wgt[:, c * P:(c + 1) * P], gs[:, c * P:(c + 1) * P],
                                ALU.mult, (t,))

            order = [(t, c, s) for c in range(2) for t in ("peer_u", "peer_v") for s in range(P)]
            slots = []

            def rows(n):
                if n == len(slots):
                    while (order[n][1], order[n][2] // 64) not in i_ready:
                        step(1)
                while (len(slots) < min(n + 1 + AHEAD, len(order))
                       and (order[len(slots)][1], order[len(slots)][2] // 64) in i_ready):
                    slots.append(gather(*order[len(slots)]))
                return slots[n]

            for c in range(2):
                for s in range(P):
                    dots(c, s, rows(2 * P * c + s))
                    step(RATE_U[c][s // 64])
                two = (bank(), bank())
                on_pe = [s for s in range(P) if s % PE_OF[1] < PE_OF[0]]
                for s in range(P):
                    slot = rows(2 * P * c + P + s)
                    if s == 0:
                        while (c, 1) not in routed:
                            step(1)
                        weights(c)
                    if s in on_pe:
                        pe_sums(c, s, slot, two, s == on_pe[0], s == on_pe[-1], s)
                    else:
                        sums(c, s, slot)
                    step(RATE_V[c])
                for k in range(2):
                    a = accs[:, c, k * 512:(k + 1) * 512]
                    release(two[k], tt(V, a, a, two[k].ap[:, :], ALU.add, (two[k].done,)))
                stt(h[:, c, :], h[:, c, :], ALPHA, accs[:, c, :], ALU.mult, ALU.add)
                layer_norm(load_row("rows", 5 + 5 * l), load_row("rows", 6 + 5 * l), accs[:, c, :], (c,))
            show(f"mid{l}", h_sb[:, 0:1], (V,))
            while work:
                step(1)

        def topk(groups, n, vals, ids, src, alt):
            for i in range(groups):
                x, y = src[:, i * n:(i + 1) * n], alt[:, i * n:(i + 1) * n]
                a, b = vals[:, i * 16:i * 16 + 8], vals[:, i * 16 + 8:i * 16 + 16]
                ia, ib = ids[:, i * 16:i * 16 + 8], ids[:, i * 16 + 8:i * 16 + 16]
                V.op(lambda e, a=a, x=x: e.max(out=a, in_=x))
                V.op(lambda e, a=a, x=x, ia=ia: e.max_index(ia, a, x))
                V.op(lambda e, a=a, x=x, y=y: e.match_replace(out=y, in_to_replace=a, in_values=x, imm_value=-3e38),
                     chain=False)
                V.op(lambda e, b=b, y=y: e.max(out=b, in_=y))
                V.op(lambda e, b=b, y=y, ib=ib: e.max_index(ib, b, y))
                yield

        class Side:

            def __init__(self, x_side, o, t):
                self.x = x_side
                v = lambda a, n: ar(a, 1024 * n)
                self.Rk = v(o["Rk"], 1).rearrange("p (c n) -> p c n", c=2)
                self.Rv = v(o["Rv"], 1).rearrange("p (c n) -> p c n", c=2)
                n = 3 if x_side else 2
                self.GG = v(o["GG"], n).rearrange("p (a c n) -> p a c n", a=n, c=2)
                self.GkT = v(o["GkT"], 1).rearrange("p (k t) -> p k t", k=4)
                if x_side:
                    self.Rq = v(o["Rq"], 1).rearrange("p (c n) -> p c n", c=2)
                    self.RkT = v(o["RkT"], 1).rearrange("p (k t) -> p k t", k=4)
                    self.RqT = v(o["RqT"], 1).rearrange("p (k t) -> p k t", k=4)
                    self.GqT = v(o["GqT"], 1).rearrange("p (k t) -> p k t", k=4)
                    self.Oret = v(o["Oret"], 1).rearrange("p (c n) -> p c n", c=2)
                    self.Ogdn = v(o["Ogdn"], 1).rearrange("p (c n) -> p c n", c=2)
                self.t = t

            def T(self, i, n=1):
                return ar(self.t + 512 * i, 512 * n)

        ctx_side = Side(False, {"Rk": 0, "Rv": 1024, "GG": 2048, "GkT": 4096}, 5120)
        x_side = Side(True, {"Rk": 0, "Rv": 1024, "Rq": 2048, "RkT": 3072, "RqT": 4096, "GG": 5120, "GkT": 8192,
                             "GqT": 9216, "Oret": 10240, "Ogdn": 11264}, 12288)
        S4 = ar(20480, 2048).rearrange("p (s n) -> p s n", s=4)
        sc8 = {n: sm(8) for n in ("e1", "e2", "ea", "rq", "rs2", "css", "crs")}
        gsm = [[sm(4) for _ in range(3)] for _ in range(2)]
        la = sm(16).rearrange("p (c n) -> p c n", c=2)
        be = sm(16).rearrange("p (c n) -> p c n", c=2)
        dec, cd, dcol = sm(8), sm(8), sm(8)
        modT, cmT = sm(48), sm(16)
        gsx, gsc, gs2 = sm(8), sm(8), sm(8)
        t16, cs = sm(16), sm(16)
        csv = cs.rearrange("p (k s) -> p k s", k=8)
        nm = smalls["norm_cols"]
        rd = smalls["ret_decay"]

        def modulation(i0, i1):
            b = bank()
            for i in range(i0, i1):
                w = load(d["w_mod"][i])
                yield 12
                for m in range(4):
                    j = 4 * (i - i0) + m
                    for k in range(8):
                        mm(b, b.ap[:, 2 * j:2 * j + 2], w.ap[:, k * 512 + m * P:k * 512 + (m + 1) * P],
                           csv[:, k, :], k == 0, k == 7, (w.ready, cs_ready[0]), last=(k == 7))
                    if m < 3:
                        yield
                w.free(PE.now)
                yield
            n = 4 * (i1 - i0)
            pv = b.ap[:, 0:2 * n].rearrange("p (j s) -> p j s", s=2)
            u = tt(V, modT[:, 4 * i0:4 * i1], pv[:, :, 0], smalls["b_mod"][:, 4 * i0:4 * i1], ALU.add, (b.done,))
            if i0 == 0:
                u = tt(V, cmT, pv[:, :, 1], smalls["b_mod"][:, 0:16], ALU.add)
            release(b, u)

        cs_ready = [None]

        def decays():
            act(t16, smalls["cvec"], ACT.Sigmoid, (V,))
            cs_ready[0] = tt(V, cs, smalls["cvec"], t16, ALU.mult, (A,))
            act(sc8["ea"], smalls["a_log"], ACT.Exp, (V,))
            act(cd, rd, ACT.Exp, (V,), scale=128.0)
            col = C("col")
            ts(V, dcol[:, 0:1], col, -1.0, 127.0, ALU.mult, ALU.add)
            ts(V, dec[:, 0:4], rd[:, 0:4], dcol[:, 0:1], None, ALU.mult, None)
            ts(V, dec[:, 4:8], rd[:, 4:8], col, None, ALU.mult, None)
            act(dec, dec, ACT.Exp, (V,))
            V.hold_for(A)

        def ret_matrix(D_, t1, t2):
            rel = C("rel")
            for hd in range(4):
                o = D_[:, hd * P:(hd + 1) * P]
                u1 = ts(V, t1, rel, 0.0, None, ALU.max, None, (A, PE))
                u2 = ts(V, t2, rel, -1.0, 0.0, ALU.mult, ALU.max)
                act(t1, t1, ACT.Exp, (u1,), scale=rd[:, hd:hd + 1])
                u = act(t2, t2, ACT.Exp, (u2,), scale=rd[:, 4 + hd:5 + hd])
                yield
                tt(V, t1, t1, C("triF"), ALU.mult, (u,))
                tt(V, t2, t2, C("triB"), ALU.mult)
                tt(V, o, t1, t2, ALU.add)

        def rms_rows(dst, src, n, ss, rs, after=()):
            for c in range(2):
                act(dst[:, c, :], src[:, c, :], ACT.Square, (V, PE, *after), accum_out=ss[:, c:c + 1])
            rsqrt(rs[:, 0:2], ss[:, 0:2], 1.0 / n, 1e-6, (A,))

        def normed(src, gcol, shift, xn, dst, ss, rs, after=()):
            rms_rows(xn, src, D, ss, rs, after)
            for c in range(2):
                ts(V, xn[:, c, :], src[:, c, :], rs[:, c:c + 1], None, ALU.mult, None, after)
            yield
            yield from transpose_to(dst, lambda c, k: xn[:, c, k * P:(k + 1) * P], 8, (V,),
                                    affine=lambda k: (gcol[:, k:k + 1], shift[:, k:k + 1]))

        def row_features(s, xT):
            tiles_ = ((s.Rk, 0, P ** -0.5), (s.Rv, 1, 1.0)) + (((s.Rq, 4, 1.0),) if s.x else ())
            for dst, i, scale in tiles_:
                w = load(d["w_in2"][i])

                def out(c, b, ps, dst=dst, scale=scale):
                    return A.op(lambda e: e.activation(dst[:, c, :], ps, ACT.Copy, scale=scale), (b.done, V))
                yield from token_mm(xT, w, 512, out, (V, A))
                w.free(PE.now)
            if not s.x:
                return
            cos, sin = C("cos2"), C("sin2")
            scr2 = s.T(6, 2)
            q = [scr2[:, 256 * j:256 * (j + 1)].rearrange("p (h f) -> p h f", h=4) for j in range(4)]
            for R, RT in ((s.Rk, s.RkT), (s.Rq, s.RqT)):
                for c in range(2):
                    xv = R[:, c, :].rearrange("p (h w f) -> p h w f", h=4, w=2)
                    cc, sn = bc(cos[:, c * 64:(c + 1) * 64], 1, 4), bc(sin[:, c * 64:(c + 1) * 64], 1, 4)
                    u = V.now
                    tt(V, q[0], xv[:, :, 0, :], cc, ALU.mult, (A, G))
                    tt(G, q[2], xv[:, :, 0, :], sn, ALU.mult, (A, u))
                    tt(V, q[1], xv[:, :, 1, :], sn, ALU.mult)
                    tt(G, q[3], xv[:, :, 1, :], cc, ALU.mult)
                    tt(V, xv[:, :, 0, :], q[0], q[1], ALU.subtract, (G,))
                    tt(G, xv[:, :, 1, :], q[2], q[3], ALU.add, (V,))
                    yield
                yield from transpose_to(RT, lambda c, k, R=R: R[:, c, k * P:(k + 1) * P], 4, (V, G))

        def gate_columns(s, xT):
            w = load(d["w_gab"], 1)
            dtb = smalls["dt_bias"]

            def out(c, b, ps):
                e1, e2 = sc8["e1"], sc8["e2"]
                tt(V, e1, ps[:, 0:8], dtb, ALU.add, (b.done, A))
                u = cp(V, be[:, c, :], ps[:, 8:16])
                act(be[:, c, :], be[:, c, :], ACT.Sigmoid, (V,))
                act(e2, e1, ACT.Abs)
                act(e2, e2, ACT.Exp, scale=-1.0)
                act(e2, e2, ACT.Ln, bias=1.0)
                stt(e1, e1, 0.0, e2, ALU.max, ALU.add, (A,))
                stt(la[:, c, :], e1, -1.0, sc8["ea"], ALU.mult, ALU.mult)
                return u
            yield from token_mm(xT, w, 16, out, (V, A), wstride=16)
            w.free(PE.now)

        def conv_features(s, xT, kinds=((0, 2, 4), (1, 3, 8)), at=0):
            cw = smalls["conv"].rearrange("p (j f) -> p j f", j=3)
            raw, cv, scr2 = s.T(at, 2), s.T(at + 2, 2), s.T(at + 4, 1)
            ss, rs = sc8["css"][:, 0:4], sc8["crs"][:, 0:4]
            rw = raw.rearrange("p (m t) -> p m t", m=4)
            cvv = cv.rearrange("p (m t) -> p m t", m=4)
            for a, i, f0 in kinds:
                w = load(d["w_in2"][i])
                yield 12
                bs = []
                for m0 in (0, 2):
                    yield from need(1)
                    b = bank()
                    for m in (m0, m0 + 1):
                        feat_mm(xT, w, m, b.ap[:, (m - m0) * 256:(m - m0) * 256 + 256], b, (V, A) if m == 0 else ())
                    bs.append(b)
                    yield 7
                w.free(PE.now)
                for m0 in (0, 2):
                    b = bs[m0 // 2]
                    release(b, cp(A, rw[:, m0:m0 + 2, :], b.ap[:, :].rearrange("p (m t) -> p m t", m=2), (b.done, V)))
                for m in range(4):
                    x, y = rw[:, m, :], cvv[:, m, :]
                    f = f0 + m
                    ts(V, y, x, cw[:, 1, f:f + 1], None, ALU.mult, None, (A,))
                    stt(y[:, 1:256], x[:, 0:255], cw[:, 0, f:f + 1], y[:, 1:256], ALU.mult, ALU.add)
                    stt(y[:, 0:255], x[:, 1:256], cw[:, 2, f:f + 1], y[:, 0:255], ALU.mult, ALU.add)
                    if m % 2:
                        yield
                t = act(raw, cv, ACT.Sigmoid, (V,))
                yield
                tt(V, cv, cv, raw, ALU.mult, (t,))
                for c in range(2):
                    yield from need(1)
                    b = bank()
                    for m in range(4):
                        tr(b, b.ap[:, m * P:(m + 1) * P], cvv[:, m, c * P:(c + 1) * P], (V,), last=(m == 3))
                    yield
                    release(b, cp(V, s.GG[:, a, c, :], b.ap[:, :], (b.done,)))
                    if a != 1:
                        x = s.GG[:, a, c, :]
                        tt(V, scr2, x, x, ALU.mult)
                        red(ss, heads(scr2, 4))
                        rsqrt(rs, ss, 1.0, 1e-6)
                        if a == 2:
                            ts(V, rs, rs, P ** -0.5, None, ALU.mult, None)
                        tt(V, heads(x, 4), heads(x, 4), bc(rs, 2, P), ALU.mult)
                if a != 1:
                    yield from transpose_to(s.GkT if a == 0 else s.GqT,
                                            lambda c, k, a=a: s.GG[:, a, c, k * P:(k + 1) * P], 4, (V,))

        def by_head(pairs, b, after):
            for hd in range(4):
                sl = slice(hd * P, (hd + 1) * P)
                ps = pairs(sl, hd)
                for n, (l, r) in enumerate(ps):
                    mm(b, b.ap[:, sl], l, r, n == 0, n == len(ps) - 1, after,
                       last=(hd == 3 and n == len(ps) - 1))
            return b

        def gdn_chunk(s, dr, c, TT, smalls3, first):
            tri = C("triF") if dr == 0 else C("triB")
            strict = C("low") if dr == 0 else C("up")
            end = P - 1 if dr == 0 else 0
            GR, Dm, DT, Am, AT, Xm, XT, Pm, U, WT, kk, vn, qe = TT
            gc, eg, ekt = smalls3
            lac = la[:, c, dr * 4:dr * 4 + 4]
            bec = be[:, c, dr * 4:dr * 4 + 4]
            ck = slice(c * P, (c + 1) * P)
            yield from need(3)
            for hd in range(4):
                cp(V, Pm[:, hd * P:(hd + 1) * P], lac[:, hd:hd + 1].to_broadcast([P, P]), (PE, A, *first))
            b1 = by_head(lambda sl, hd: [(Pm[:, sl], tri)], bank(), (V, A))
            b2 = bank()
            mm(b2, b2.ap[:, 0:4], tri, lac, after=(V, A), last=True)
            b3 = by_head(lambda sl, hd: [(s.GkT[:, hd, ck], s.GkT[:, hd, ck])], bank(), (V, A))
            yield
            release(b1, cp(V, GR, b1.ap[:, :], (b1.done,)))
            release(b2, cp(V, gc, b2.ap[:, 0:4], (b2.done,)))
            release(b3, cp(A, kk, b3.ap[:, :], (b3.done, V)))
            for hd in range(4):
                sl = slice(hd * P, (hd + 1) * P)
                ts(V, Dm[:, sl], GR[:, sl], gc[:, hd:hd + 1], 0.0, ALU.subtract, ALU.max)
            t = act(Dm, Dm, ACT.Exp, (V,), scale=-1.0)
            for hd in range(4):
                sl = slice(hd * P, (hd + 1) * P)
                ts(V, DT[:, sl], GR[:, sl], gc[:, hd:hd + 1], 0.0, ALU.subtract, ALU.min)
            last = heads(GR, 4)[:, :, end:end + 1].rearrange("p h x -> p (h x)")
            tt(V, ekt, last, gc, ALU.subtract)
            act(DT, DT, ACT.Exp, (V,))
            act(ekt, ekt, ACT.Exp)
            act(eg, last, ACT.Exp)
            t2 = act(gc, gc, ACT.Exp)
            if s.x:
                t2 = act(qe, GR, ACT.Exp)
            yield
            tt(V, heads(Dm, 4), heads(Dm, 4), bc(strict, 1, 4), ALU.mult, (t,))
            tt(V, Am, kk, Dm, ALU.mult, (A,))
            tt(V, heads(Am, 4), heads(Am, 4), bc(bec, 2, P), ALU.mult)
            yield from need(1)
            b = bank()
            for hd in range(4):
                tr(b, b.ap[:, hd * P:(hd + 1) * P], Am[:, hd * P:(hd + 1) * P], (V,), last=(hd == 3))
            tt(V, heads(DT, 4), heads(DT, 4), bc(tri, 1, 4), ALU.mult, (t2,))
            I4 = bc(ident, 1, 4)
            tt(V, heads(Xm, 4), heads(Am, 4), bc(C("lvl0"), 1, 4), ALU.mult)
            tt(V, heads(Xm, 4), I4, heads(Xm, 4), ALU.subtract)
            yield
            release(b, cp(V, AT, b.ap[:, :], (b.done,)))
            tt(V, heads(XT, 4), heads(AT, 4), bc(C("lvl0"), 1, 4), ALU.mult)
            tt(V, heads(XT, 4), I4, heads(XT, 4), ALU.subtract)
            Bs = (Dm, U)
            g = tt(G, heads(Bs[1], 4), heads(AT, 4), bc(C("lvl1"), 1, 4), ALU.mult, (V, PE, A))
            for lv in range(1, 7):
                Bm = Bs[lv % 2]
                yield from need(1)
                b = by_head(lambda sl, hd: [(Bm[:, sl], Xm[:, sl])], bank(), (V, g))
                if lv < 6:
                    g = tt(G, heads(Bs[(lv + 1) % 2], 4), heads(AT, 4), bc(C(f"lvl{lv + 1}"), 1, 4), ALU.mult,
                           (V, prior_use[0]) if lv > 1 else (V,))
                prior = b.done
                yield
                release(b, cp(A, Pm, b.ap[:, :], (b.done, V)))
                yield from need(2)
                b2 = by_head(lambda sl, hd: [(Pm[:, sl], XT[:, sl])], bank(), (A, V))
                if lv < 6:
                    b = by_head(lambda sl, hd: [(XT[:, sl], Pm[:, sl])], bank(), ())
                prior_use[0] = prior
                yield
                if lv < 6:
                    release(b, tt(V, Xm, Xm, b.ap[:, :], ALU.subtract, (b.done,)))
                release(b2, tt(V, XT, XT, b2.ap[:, :], ALU.subtract, (b2.done,)))
            Gk, Gv = s.GG[:, 0, c, :], s.GG[:, 1, c, :]
            rv, rk, kt = Dm, Am, Xm
            tt(V, heads(rv, 4), heads(Gv, 4), bc(bec, 2, P), ALU.mult, (G,))
            tt(V, heads(rk, 4), heads(Gk, 4), bc(bec, 2, P), ALU.mult)
            tt(V, heads(rk, 4), heads(rk, 4), bc(gc, 2, P), ALU.mult)
            yield from need(3)
            b = by_head(lambda sl, hd: [(XT[:, sl], rv[:, sl])], bank(), (V,))
            b2 = by_head(lambda sl, hd: [(rk[:, sl], XT[:, sl])], bank(), (V,))
            tt(V, heads(kt, 4), heads(Gk, 4), bc(ekt, 2, P), ALU.mult, (A,))
            if s.x:
                kq = by_head(lambda sl, hd: [(s.GkT[:, hd, ck], s.GqT[:, hd, ck])], bank(), (V, A))
                tt(V, heads(qe, 4), heads(qe, 4), s.GqT[:, :, ck], ALU.mult, (A,))
            yield
            release(b, cp(A, U, b.ap[:, :], (b.done, V)))
            release(b2, cp(V, WT, b2.ap[:, :], (b2.done,)))
            S = S4[:, 2 + dr, :]
            yield from need(1)
            b = by_head(lambda sl, hd: [(WT[:, sl], S[:, sl])], bank(), (V,))
            if s.x:
                release(kq, tt(V, DT, DT, kq.ap[:, :], ALU.mult, (kq.done,)))
            yield
            release(b, tt(V, vn, U, b.ap[:, :], ALU.subtract, (b.done, A)))
            yield from need(2)
            b = by_head(lambda sl, hd: [(kt[:, sl], vn[:, sl])], bank(), (V,))
            if s.x:
                b2 = by_head(lambda sl, hd: [(DT[:, sl], vn[:, sl]), (qe[:, sl], S[:, sl])], bank(), (V,))
            yield
            if s.x:
                O = s.Ogdn[:, c, :]
                release(b2, tt(V, O, O, b2.ap[:, :], ALU.add, (b2.done,)))
            tt(V, heads(S, 4), heads(S, 4), bc(eg, 2, P), ALU.mult, (b.done,))
            release(b, tt(V, S, S, b.ap[:, :], ALU.add))

        prior_use = [None]

        def ret_chunk(s, dr, c, kd, qe, Dret):
            S = S4[:, dr, :]
            ck = slice(c * P, (c + 1) * P)
            if s.x:
                for hd in range(4):
                    t = act(qe[:, hd * P:(hd + 1) * P], C("up1") if dr == 0 else C("down"), ACT.Exp, (PE, V),
                            scale=rd[:, 4 * dr + hd:4 * dr + hd + 1])
                tt(V, heads(qe, 4), heads(qe, 4), s.RqT[:, :, ck], ALU.mult, (t,))
                yield from need(2)
                b = by_head(lambda sl, hd: [(qe[:, sl], S[:, sl])], bank(), (V, A))
                if dr == 0:
                    b2 = by_head(lambda sl, hd: [(s.RkT[:, hd, ck], s.RqT[:, hd, ck])], bank(), (V, A))
                yield
                O = s.Oret[:, c, :]
                release(b, tt(V, O, O, b.ap[:, :], ALU.add, (b.done,)))
                if dr == 0:
                    release(b2, tt(V, kd, Dret, b2.ap[:, :], ALU.mult, (b2.done,)))
                    yield from need(1)
                    b = by_head(lambda sl, hd: [(kd[:, sl], s.Rv[:, c, sl])], bank(), (V,))
                    yield
                    release(b, tt(V, O, O, b.ap[:, :], ALU.add, (b.done,)))
            tt(V, heads(kd, 4), heads(s.Rk[:, c, :], 4), bc(dec[:, 4 * dr:4 * dr + 4], 2, P), ALU.mult, (PE, A))
            yield from need(1)
            b = by_head(lambda sl, hd: [(kd[:, sl], s.Rv[:, c, sl])], bank(), (V, A))
            yield
            tt(V, heads(S, 4), heads(S, 4), bc(cd[:, 4 * dr:4 * dr + 4], 2, P), ALU.mult, (b.done,))
            release(b, tt(V, S, S, b.ap[:, :], ALU.add))

        def modulate(i0, i1):
            yield from modulation(i0, i1)
            if i0 == 0:
                stt(gsx, modT[:, 8:16], 1.0, nm[:, 0:8], ALU.add, ALU.mult)
                stt(gsc, cmT[:, 8:16], 1.0, nm[:, 0:8], ALU.add, ALU.mult)
            if i1 == 12:
                stt(gs2, modT[:, 32:40], 1.0, nm[:, 8:16], ALU.add, ALU.mult)

        def background0():
            s = ctx_side
            V.op(lambda e: e.memset(ar(20480, 2048), 0.0))
            cslot, before = take(2)
            SP.dma(lambda e: e.dma_start(cslot.ap.rearrange("p (c n) -> p c n", c=2),
                                         d["ctx"].rearrange("(c p) n -> p c n", p=P)), before, ring_sems[cslot.first])
            cx = cslot.ap.rearrange("p (c n) -> p c n", c=2)
            yield
            yield
            hcT = s.T(8, 4).rearrange("p (k t) -> p k t", k=8)
            yield from normed(cx, gsc, cmT[:, 0:8], s.T(0, 4).rearrange("p (c n) -> p c n", c=2), hcT,
                              sc8["css"], sc8["crs"], (cslot.ready,))
            cslot.free(V.now, A.now)
            show("hc", s.T(8, 4), (V, A))
            yield from row_features(s, hcT)
            yield from gate_columns(s, hcT)
            yield from conv_features(s, hcT)
            TT = [s.T(i) for i in range(13)]
            for dr, cs_ in ((0, (0, 1)), (1, (1, 0))):
                for c in cs_:
                    yield from gdn_chunk(s, dr, c, TT, gsm[0], ())
                    yield from ret_chunk(s, dr, c, s.T(13), None, None)
            for i in range(4):
                show(f"init{i}", S4[:, i, :], (V,))

        def second():
            s = x_side
            V.op(lambda e: e.memset(ar(10240, 2048), 0.0), (A, PE))
            xn = s.T(0, 4).rearrange("p (c n) -> p c n", c=2)
            run(normed(h, gsx, modT[:, 0:8], xn, hT, st["ss"], st["rs"]))
            show("hx", hT_sb[:, :], (V, A))
            run(row_features(s, hT), conv_features(s, hT, ((0, 2, 4), (2, 6, 0))), conv_features(s, hT, ((1, 3, 8),), 8), gate_columns(s, hT), ret_matrix(s.T(15), s.T(14)[:, 0:P], s.T(14)[:, P:2 * P]))
            show("rk", s.Rk, (V, G))
            show("gk", s.GG[:, 0, :, :], (V,))
            show("gq", s.GG[:, 2, :, :], (V,))
            show("log_a", la, (V,))
            show("beta", be, (A,))
            lane_b, before_b = take(7, None, False)
            gslot, before_g = take(6, None, False)
            gt = gslot.ap[:, 0:4096].rearrange("p (c n) -> p c n", c=2)
            rg = gslot.ap[:, 4096:5120].rearrange("p (c n) -> p c n", c=2)
            gz = gslot.ap[:, 5120:6144].rearrange("p (c n) -> p c n", c=2)

            def gdn_lane(dr, TT, first):
                for c in ((0, 1) if dr == 0 else (1, 0)):
                    yield from gdn_chunk(s, dr, c, TT, gsm[dr], first)

            def ret_lane():
                for dr, cs_ in ((0, (0, 1)), (1, (1, 0))):
                    for c in cs_:
                        yield from ret_chunk(s, dr, c, s.T(13), s.T(14), s.T(15))

            def gates():
                for dst, i in ((rg, 5), (gz, 7)):
                    w = load(d["w_in2"][i])

                    def out(c, b, ps, dst=dst):
                        t = act(dst[:, c, :], ps, ACT.Sigmoid, (b.done, V, *before_g))
                        return tt(V, dst[:, c, :], dst[:, c, :], ps, ALU.mult, (t,))
                    yield from token_mm(hT, w, 512, out, (), grain=GRAIN)
                    w.free(PE.now)
                for i in range(4):
                    w = load(d["w_in2"][8 + i])

                    def out(c, b, ps, i=i):
                        return act(gt[:, c, i * 512:(i + 1) * 512], ps, ACT.Sigmoid, (b.done, *before_g))
                    yield from token_mm(hT, w, 512, out, (), grain=GRAIN)
                    w.free(PE.now)

            run(gdn_lane(0, [s.T(i) for i in range(13)], ()),
                gdn_lane(1, [lane_b.ap[:, 512 * i:512 * (i + 1)] for i in range(13)], before_b),
                ret_lane(), gates())
            lane_b.free(V.now, A.now, PE.now, G.now)
            Oret, Ogdn = s.Oret, s.Ogdn
            show("ret_x", Oret, (V,))
            show("gdn_x", Ogdn, (V,))
            yT = ar(3072, 2048).rearrange("p (k t) -> p k t", k=8)
            mg = ar(5120, 2048).rearrange("p (c n) -> p c n", c=2)
            mo = ar(12288, 2048).rearrange("p (c n) -> p c n", c=2)
            nw = load_row("rows", 12)
            wro, wgo = load(d["w_ret_out"]), load(d["w_gdn_out"])

            def out_norm(c, y, g, o, mean, n):
                t5, m4, r4 = ar(512 * n, 512), asm[f"ms{n % 2}"][:, 4 * (n // 2):4 * (n // 2) + 4], \
                    asm[f"mr{n % 2}"][:, 4 * (n // 2):4 * (n // 2) + 4]
                if mean:
                    red(m4, heads(y, 4))
                    ts(V, m4, m4, -1.0 / P, None, ALU.mult, None)
                    tt(V, heads(y, 4), heads(y, 4), bc(m4, 2, P), ALU.add)
                t = act(t5, y, ACT.Square, (V, PE))
                yield
                red(m4, heads(t5, 4), after=(t,))
                rsqrt(r4, m4, 1.0 / P, 1e-6)
                tt(V, g[:, c, :], g[:, c, :], nw.ap[:, o:o + 512], ALU.mult, (nw.ready, A))
                tt(V, heads(y, 4), heads(y, 4), bc(r4, 2, P), ALU.mult)
                tt(V, y, y, g[:, c, :], ALU.mult)

            run(out_norm(0, Oret[:, 0, :], rg, 0, True, 0), out_norm(1, Oret[:, 1, :], rg, 0, True, 1),
                out_norm(0, Ogdn[:, 0, :], gz, 512, False, 2), out_norm(1, Ogdn[:, 1, :], gz, 512, False, 3))
            nw.free(V.now)
            run(transpose_to(yT[:, 0:4, :], lambda c, k: Oret[:, c, k * P:(k + 1) * P], 4, (V,)),
                transpose_to(yT[:, 4:8, :], lambda c, k: Ogdn[:, c, k * P:(k + 1) * P], 4, (V,)))
            for r, w in ((0, wro), (1, wgo)):
                for i in range(2):
                    def out(c, b, ps, i=i, r=r):
                        g = gt[:, c, r * 1024 + i * 512:r * 1024 + i * 512 + 512]
                        m = mg[:, c, i * 512:(i + 1) * 512]
                        if r == 0:
                            return tt(V, m, g, ps, ALU.mult, (b.done, A))
                        u = tt(V, g, g, ps, ALU.mult, (b.done, A))
                        tt(V, m, m, g, ALU.add)
                        return u
                    run(token_mm(yT[:, r * 4:r * 4 + 4, :], w, 512, out, (V, A), nk=4, woff=i * 512, wstride=1024))
                w.free(PE.now)
            gslot.free(V.now, A.now)
            wo = [load(d["w_o2"][i]) for i in range(2)]
            run(transpose_to(hT, lambda c, k: mg[:, c, k * P:(k + 1) * P], 8, (V, PE)))
            for i in range(2):
                def out(c, b, ps, i=i):
                    return cp((V, A)[i], mo[:, c, i * 512:(i + 1) * 512], ps, (b.done,))
                run(token_mm(hT, wo[i], 512, out, (V, A)))
                wo[i].free(PE.now)

            def add_gated(y, row, gate, gb, scr):
                w = load_row("rows", row)
                for i in range(2):
                    b = bank()
                    for j in range(4):
                        k = 4 * i + j
                        cp(V, scr[:, 0, j * P:(j + 1) * P], gate[:, k:k + 1].to_broadcast([P, P]), (PE, A))
                    for j in range(4):
                        mm(b, b.ap[:, j * P:(j + 1) * P], scr[:, 0, j * P:(j + 1) * P], ident, after=(V,), last=(j == 3))
                    release(b, cp(V, gb[:, i * 512:(i + 1) * 512], b.ap[:, :], (b.done,)))
                tt(V, gb, gb, w.ap, ALU.mult, (w.ready,))
                w.free(V.now)
                rms_rows(scr, y, D, st["ss"], st["rs"])
                for c in range(2):
                    stt(y[:, c, :], y[:, c, :], st["rs"][:, c:c + 1], gb, ALU.mult, ALU.mult, (A,))
                    tt(V, h[:, c, :], h[:, c, :], y[:, c, :], ALU.add)

            add_gated(mo, 13, modT[:, 16:24], ar(7168, 1024), ar(8192, 2048).rearrange("p (c n) -> p c n", c=2))
            show("xmix", h_sb[:, :], (V,))
            xn2 = ar(16384, 2048).rearrange("p (c n) -> p c n", c=2)
            run(normed(h, gs2, modT[:, 24:32], xn2, hT, st["ss"], st["rs"]))
            moe(xn2, modT, add_gated, gs2)

        def moe(xn, modT, add_gated, gs2):
            Wt = ar(0, 128).rearrange("p (c n) -> p c n", c=2)
            sg = ar(128, 128).rearrange("p (c n) -> p c n", c=2)
            bi = ar(256, 128).rearrange("p (c n) -> p c n", c=2)
            Mk = ar(384, 128).rearrange("p (c n) -> p c n", c=2)
            g8, m8, kp = ar(512, 64), ar(576, 8), ar(584, 8)
            gsum, ssum, big = ar(592, 8), ar(600, 8), ar(608, 64)
            TW = ar(672, 256).rearrange("p (c e x) -> p c e x", c=2, x=2)
            rk = ar(928, 128).rearrange("p (c n) -> p c n", c=2)
            ST = ar(1056, 256).rearrange("p (w e x) -> p w e x", w=2, x=2)
            ig = ar(1312, 128)
            OH = ar(1568, 2048).rearrange("p (c e s) -> p c e s", c=2, e=8)
            ysh = ar(3616, 2048).rearrange("p (c n) -> p c n", c=2)
            xg = [ar(5664 + 1024 * i, 1024) for i in range(4)]
            XT = [ar(9760 + 1024 * i, 1024) for i in range(2)]
            yb = [ar(11808 + 1024 * i, 1024) for i in range(2)]
            sgm = [ar(13856 + 512 * i, 512) for i in range(2)]
            hid = [ar(14880 + 512 * i, 512) for i in range(2)]
            yin = ar(18432, 2048).rearrange("p (c n) -> p c n", c=2)
            sh2 = modT[:, 24:32]

            rbs = load(d["router_bias"].to_broadcast([P, 64]), 1)
            w = load(d["w_router"], 1)
            wg, wd = load(d["w_gu_sh"]), load(d["w_down_sh"])
            ahead = {0: (load(d["w_gu"][0]), load(d["w_down"][0]))}
            SP.dma(lambda e: e.dma_start(x_tab.rearrange("(c p) n -> p c n", p=P), xn), [V.now], s_tab)
            V.op(lambda e: e.memset(yin, 0.0), (PE, A))
            SP.dma(lambda e: e.dma_start(y_tab[0:T, :].rearrange("(c p) n -> p c n", p=P), yin), [V.now], s_tab)
            tab_ready = (s_tab, 32)
            xg_zero = G.op(lambda e: e.memset(ar(5664, 4096), 0.0), (V, A, PE))

            def router_out(c, b, ps):
                act(sg[:, c, :], ps, ACT.Exp, (PE, V), scale=-1.0)
                u = A.now
                ts(V, sg[:, c, :], sg[:, c, :], 1.0, None, ALU.add, None, (A,))
                V.op(lambda e: e.reciprocal(sg[:, c, :], sg[:, c, :]))
                tt(V, bi[:, c, :], sg[:, c, :], rbs.ap[:, 0:64], ALU.add, (rbs.ready,))
                return u
            run(token_mm(hT, w, 64, router_out, (V, A), wstride=64))
            w.free(PE.now)
            rbs.free(V.now)
            bg, bu = bank(), bank()
            for f in range(4):
                bb = bg if f < 2 else bu
                feat_mm(hT, wg, f, bb.ap[:, (f % 2) * 256:(f % 2 + 1) * 256], bb, ())
            wg.free(PE.now)
            act(ysh[:, 0, 0:512], bg.ap[:, :], ACT.Sigmoid, (PE, V))
            act(ysh[:, 0, 512:1024], bg.ap[:, :], ACT.Copy)
            release(bg, A.now)
            release(bu, act(ysh[:, 1, 0:512], bu.ap[:, :], ACT.Copy))
            for c in range(2):
                for g in range(8):
                    V.op(lambda e, g=g, c=c: e.max(out=g8[:, 8 * g:8 * g + 8], in_=bi[:, c, 8 * g:8 * g + 8]))
                gv = heads(g8, 8)
                tt(V, gsum, gv[:, :, 0:1].rearrange("p a b -> p (a b)"), gv[:, :, 1:2].rearrange("p a b -> p (a b)"),
                   ALU.add)
                V.op(lambda e: e.max(out=m8, in_=gsum))
                V.op(lambda e: e.memset(m8[:, 4:8], 3e38))
                V.op(lambda e: e.match_replace(out=kp, in_to_replace=m8, in_values=gsum, imm_value=-2e38))
                ts(V, kp, kp, -1e38, -1e30, ALU.is_gt, ALU.mult)
                cb = Mk[:, c, :]
                tt(V, heads(cb, 8), heads(bi[:, c, :], 8), bc(kp, 2, 8), ALU.add)
                topm(m8, cb)
                ts(V, cb, cb, -1e38, None, ALU.is_lt, None)
                tt(V, Wt[:, c, :], sg[:, c, :], cb, ALU.mult)
                red(ssum[:, 0:1], Wt[:, c, :])
                V.op(lambda e: e.reciprocal(ssum[:, 0:1], ssum[:, 0:1]))
                ts(V, Wt[:, c, :], Wt[:, c, :], ssum[:, 0:1], 2.5, ALU.mult, ALU.mult)
                cp(V, TW[:, c, :, 1], Wt[:, c, :])
                ts(V, big, C("ones")[:, 0:64], C("col"), float(1 + c * P), ALU.mult, ALU.add)
                cp(V, TW[:, c, :, 0], big)
            for c in range(2):
                b = bank()
                if c == 1:
                    mm(b, b.ap[:, 0:64], C("ones"), Mk[:, 0, :], True, False, (V,))
                mm(b, b.ap[:, 0:64], C("up"), Mk[:, c, :], c == 0, True, (V,), last=True)
                release(b, cp(V, rk[:, c, :], b.ap[:, 0:64], (PE,)))
                stt(rk[:, c, :], Mk[:, c, :], -1000.0, rk[:, c, :], ALU.mult, ALU.add)
                ts(V, rk[:, c, :], rk[:, c, :], 1000.0, None, ALU.add, None)
            b = bank()
            for c in range(2):
                mm(b, b.ap[:, 0:64], C("ones"), Mk[:, c, :], c == 0, c == 1, (V,), last=(c == 1))
            release(b, red(ssum[:, 0:1], b.ap[:, 0:64], ALU.max, (PE,)))
            ts(V, ssum[:, 0:1], ssum[:, 0:1], float(P), None, ALU.is_gt, None)
            over = cp(V, flag[:, 0:1], ssum[:, 0:1])
            ready = {}

            def slots(wave):
                used = [None, None]
                for g in range(4):
                    b = bank()
                    for e0 in range(0, 16, 4):
                        i = (e0 // 4) % 2
                        o4 = OH[:, :, 4 * i:4 * i + 4, :]
                        for c in range(2):
                            t = tt(V, o4[:, c], bc(C("iota")[:, wave * P:(wave + 1) * P], 1, 4),
                                   bc(rk[:, c, 16 * g + e0:16 * g + e0 + 4], 2, P), ALU.is_equal, (used[i] or PE.now,))
                        for j in range(4):
                            for c in range(2):
                                o = (e0 + j) * 2
                                mm(b, b.ap[:, o:o + 2], o4[:, c, j, :], TW[:, c, 16 * g + e0 + j, :], c == 0, c == 1,
                                   (t,), last=(j == 3 and c == 1))
                        used[i] = PE.now
                        yield
                    part = slice(16 * g, 16 * g + 16)
                    release(b, cp(V, ST[:, wave, part], b.ap[:, 0:32].rearrange("p (e x) -> p e x", x=2), (b.done,)))
                    v = ST[:, wave, part, 0]
                    igv = ig[:, wave * 64 + 16 * g:wave * 64 + 16 * g + 16]
                    ts(V, igv, v, 0.0, 1000.0, ALU.is_equal, ALU.mult)
                    stt(igv, v, -1.0, igv, ALU.add, ALU.add)
                    ready[wave, g] = cp(V, iu[:, wave * 64 + 16 * g:wave * 64 + 16 * g + 16], igv, (G,))
                    yield

            more = slots(0)
            for _ in range(5):
                next(more)
            tt(V, hid[0], ysh[:, 0, 0:512], ysh[:, 0, 512:1024], ALU.mult, (A,))
            tt(V, hid[0], hid[0], ysh[:, 1, 0:512], ALU.mult)
            hv = hid[0].rearrange("p (f t) -> p f t", f=2)
            for c in range(2):
                for n in range(2):
                    b = bank()
                    for f in range(2):
                        mm(b, b.ap[:, :], hv[:, f, c * P:(c + 1) * P],
                           wd.ap[:, f * 1024 + n * 512:f * 1024 + n * 512 + 512], f == 0, f == 1, (wd.ready, V),
                           last=(f == 1))
                    release(b, cp((V, A)[n], ysh[:, c, n * 512:(n + 1) * 512], b.ap[:, :], (PE,)))
            wd.free(PE.now)

            def experts(wave, sems, x_sems, base, more, ahead):
                got, xt_done, hid_done, y_done, xt_ev, used_y = {}, {}, {}, {}, {}, {}
                h_done, w_of, banks_of = {}, {}, {}
                start = (V.now, A.now, PE.now)

                def fetch(e):
                    after = [ready[wave, e // 16], tab_ready, xg_zero, *start]
                    if e >= 4:
                        after.append(xt_done[e - 4])
                    n = e % 4
                    G.dma(lambda g: g.indirect_dma_start(
                        out=xg[n], out_offset=None, in_=x_tab,
                        in_offset=bass.IndirectOffsetOnAxis(ap=iu[:, wave * 64 + e:wave * 64 + e + 1], axis=0),
                        bounds_check=T - 1, oob_is_err=False),
                        after, x_sems[n])
                    got[e] = (x_sems[n], 16 * (e // 4 + 1))

                def turn(e):
                    w_of[e] = ahead.get(e) or (load(d["w_gu"][e], sems=sems), load(d["w_down"][e], sems=sems))
                    x, o = xg[e % 4], XT[e % 2]
                    after_x = [h_done[e - 2]] if e >= 2 else []
                    marks = []
                    for k0 in (0, 4):
                        b = bank()
                        for j in range(4):
                            tr(b, b.ap[:, j * P:(j + 1) * P], x[:, (k0 + j) * P:(k0 + j + 1) * P], (got[e],),
                               last=(j == 3))
                        for j in range(4):
                            k = k0 + j
                            a, r = o[:, k * P:(k + 1) * P], b.ap[:, j * P:(j + 1) * P]
                            if k0 == 0:
                                u = ts(V, a, r, gs2[:, k:k + 1], sh2[:, k:k + 1], ALU.mult, ALU.add,
                                       (b.done, *after_x), chain=False)
                            else:
                                u = A.op(lambda q, a=a, r=r, k=k: q.activation(
                                    a, r, ACT.Identity, bias=sh2[:, k:k + 1], scale=gs2[:, k:k + 1]),
                                    (b.done, *after_x), chain=False)
                        release(b, u)
                        marks.append(u)
                    xt_done[e] = PE.now
                    xt_ev[e] = marks

                def up(e):
                    wg, wd = w_of[e]
                    o = XT[e % 2]
                    b, b2 = bank(), bank()
                    for f in range(4):
                        bb = b if f < 2 else b2
                        for k in range(8):
                            mm(bb, bb.ap[:, (f % 2) * P:(f % 2 + 1) * P], wg.ap[:, k * 512 + f * P:k * 512 + (f + 1) * P],
                               o[:, k * P:(k + 1) * P], k == 0, k == 7, (wg.ready, *xt_ev[e]), last=(k == 7 and f % 2 == 1))
                        if f == 1:
                            tg = PE.now
                    wg.free(PE.now)
                    h_done[e] = PE.now
                    s, hd = sgm[e % 2][:, 0:256], hid[e % 2][:, 0:256]
                    prior = [used_y[e - 2][0]] if e >= 2 else []
                    t = act(s, b.ap[:, 0:256], ACT.Sigmoid, (tg, *prior, *([hid_done[e - 2]] if e >= 2 else [])))
                    release(b, tt(V, s, s, b.ap[:, 0:256], ALU.mult, (t,)))
                    hid_done[e] = tt(V, hd, s, b2.ap[:, 0:256], ALU.mult, (h_done[e], *prior))
                    release(b2, hid_done[e])

                def down(e):
                    wg, wd = w_of[e]
                    hd = hid[e % 2][:, 0:256].rearrange("p (f t) -> p f t", f=2)
                    y = yb[e % 2]
                    wcol = ST[:, wave, e, 1:2]
                    ev = []
                    for n in range(2):
                        b = bank()
                        for f in range(2):
                            mm(b, b.ap[:, :], hd[:, f, :], wd.ap[:, f * 1024 + n * 512:f * 1024 + n * 512 + 512],
                               f == 0, f == 1, (wd.ready, hid_done[e]), last=(f == 1))
                        o = y[:, n * 512:(n + 1) * 512]
                        free = [y_done[e - 2]] if e >= 2 else []
                        if n == 0:
                            u = ts(V, o, b.ap[:, :], wcol, None, ALU.mult, None, (b.done, *free))
                        else:
                            u = A.op(lambda q, o=o, b=b: q.activation(o, b.ap[:, :], ACT.Copy, scale=wcol),
                                     (b.done, ready[wave, e // 16], *free))
                        release(b, u)
                        ev.append(u)
                    used_y[e] = (PE.now,)
                    wd.free(PE.now)
                    n_y[0] += 16
                    G.dma(lambda g: g.indirect_dma_start(
                        out=y_tab, out_offset=bass.IndirectOffsetOnAxis(
                            ap=iu[:, wave * 64 + e:wave * 64 + e + 1], axis=0),
                        in_=y, in_offset=None, bounds_check=T - 1, oob_is_err=False, compute_op=ALU.add), [*ev, (base, n_y[0] - 16)], base)
                    y_done[e] = (base, n_y[0])

                n_y = [0]
                for e in range(3):
                    fetch(e)
                turn(0)
                for e in range(65):
                    next(more, None)
                    if e + 1 < 64:
                        turn(e + 1)
                    if e < 64:
                        up(e)
                        if e + 3 < 64:
                            fetch(e + 3)
                    if e >= 1:
                        down(e - 1)
                return (base, n_y[0])

            done = experts(0, None, xg_sems, s_y, more, ahead)
            for q in (PE, V, A, G, SP):
                q.begin_if(flag, over, done)
            over_slots = slots(1)
            run(over_slots)
            second_done = experts(1, ring2_sems, xg2_sems, s_y2, over_slots, {})
            V.op(lambda e: e.memset(m8, 0.0), (second_done, PE, A))
            for q in (PE, V, A, G, SP):
                q.end_if()
            y = yin
            SP.dma(lambda e: e.dma_start(yin, y_tab[0:T, :].rearrange("(c p) n -> p c n", p=P)), [done, V.now], s_yin)
            for c in range(2):
                tt(V, yin[:, c, :], yin[:, c, :], ysh[:, c, :], ALU.add, ((s_yin, 16), A))
            add_gated(y, 14, modT[:, 40:48], ar(5664, 1024), ar(7712, 2048).rearrange("p (c n) -> p c n", c=2))
            SP.dma(lambda e: e.dma_start(y_dram, h), [V.now], s_out)
            n_out[0] += 16

        def topm(m, x):
            V.op(lambda e: e.max(out=m, in_=x))
            V.op(lambda e: e.match_replace(out=x, in_to_replace=m, in_values=x, imm_value=-2e38))

        show("h0", h_sb[:, :], (V,))
        decays()
        for l in range(LAYERS):
            work.extend([modulate(0, 4), modulate(4, 8)] if l == 0 else [modulate(8, 12)])
            attention(l)
            show(f"hattn{l}", h_sb[:, :], (V,))
            if stop == f"attn{l}":
                break
            peer(l, [background0()] if l == 0 else [])
            show(f"h{l + 1}", h_sb[:, :], (V,))
            if stop == f"peer{l}":
                break
        if stop is None:
            second()
        else:
            SP.dma(lambda e: e.dma_start(y_dram, h), [V.now], s_out)
            n_out[0] += 16

        block = ctx.enter_context(nc.Block())

        @block.sync
        def _(e):
            SP.play(e)
            e.wait_ge(s_out, n_out[0])
            for x in dump_sems:
                e.wait_ge(x, 16)

        @block.gpsimd
        def _(e):
            G.play(e)

        @block.scalar
        def _(e):
            A.play(e)

        @block.vector
        def _(e):
            V.play(e)

        @block.tensor
        def _(e):
            PE.play(e)


TABLES = {"x_tab": T, "y_tab": T}


def constants():
    import numpy as np
    f = np.float32
    t = {}
    i = np.arange(P)
    t["ident"] = np.eye(P)
    t["triF"] = (i[:, None] <= i[None, :])
    t["triB"] = (i[:, None] >= i[None, :])
    t["low"] = (i[:, None] > i[None, :])
    t["up"] = (i[:, None] < i[None, :])
    tok = np.arange(T).reshape(2, P)
    dist = np.abs(tok[:, :, None] - np.arange(T)[None, None, :])
    t["dist"] = dist.transpose(1, 0, 2).reshape(P, -1)
    t["mask"] = np.where(dist <= 128, 0.0, -1e30).transpose(1, 0, 2).reshape(P, -1)
    t["iota16"] = np.tile(np.arange(16), (P, 1))
    pos = np.stack([np.arange(T) // 64, np.arange(T) % 64], -1).astype(f)
    inv = (f(10000.0) ** (-np.arange(16, dtype=f) / f(16))).astype(f)
    ang = (pos[:, :, None] * inv).astype(f).reshape(2, P, 32).transpose(1, 0, 2).reshape(P, 64)
    t["cos1"], t["sin1"] = np.cos(ang), np.sin(ang)
    inv = (f(10000.0) ** (-np.arange(32, dtype=f) / f(32))).astype(f)
    ang = np.concatenate([pos[:, 0:1] * inv, pos[:, 1:2] * inv], -1).astype(f)
    ang = ang.reshape(2, P, 64).transpose(1, 0, 2).reshape(P, 128)
    t["cos2"], t["sin2"] = np.cos(ang), np.sin(ang)
    for l in range(7):
        same = (i[:, None] >> (l + 1)) == (i[None, :] >> (l + 1))
        t[f"lvl{l}"] = same & ((i[:, None] >> l) != (i[None, :] >> l))
    t["up1"] = np.tile(i + 1, (P, 1))
    t["down"] = np.tile(P - i, (P, 1))
    t["col"] = i[:, None]
    t["ones"] = np.ones((P, P))
    t["iota"] = np.tile(np.arange(256), (P, 1))
    t["col257"] = i[:, None] + 257
    t["mhalf"] = np.full((P, 16), -0.5)
    t["rel"] = i[None, :] - i[:, None]
    at, o = {}, 0
    for k, v in t.items():
        at[k] = (o, v.shape[1])
        o += v.shape[1]
    return at, o, np.ascontiguousarray(np.concatenate([v.astype(f) for v in t.values()], 1))


CONST_AT, CONST_COLS, CONSTS = constants()


def tiles(w, n=512):
    import numpy as np
    k, m = w.shape[-2:]
    lead = w.shape[:-2]
    v = w.reshape(*lead, k // P, P, m // n, n)
    r = len(lead)
    v = np.moveaxis(v, r + 2, r)
    v = np.moveaxis(v, r + 2, r + 1)
    return np.ascontiguousarray(v).reshape(*lead, m // n, P, k // P * n)


def arrays_of(i):
    import numpy as np
    a = {k: np.asarray(v) for k, v in i.items()}
    r = {"consts": CONSTS, "x": a["x"][0]}
    rows = [a["ln_in_g"], a["ln_in_b"]]
    for l in range(LAYERS):
        rows += [np.concatenate([a["gn_a_g"][l], a["gn_b_g"][l]]), a["ln1_g"][l], a["ln1_b"][l],
                 a["ln2_g"][l], a["ln2_b"][l]]
    rows += [np.concatenate([a["ret_gn_w_2"][0], a["gdn_norm_w_2"][0]]), a["norm_mix_post_2"][0],
             a["norm_ffn_post_2"][0]]
    r["rows"] = np.stack(rows)
    r["qn_g"] = a["qn_g"].reshape(1, -1)
    r["kn_g"] = a["kn_g"].reshape(1, -1)
    r["sink"] = a["sink"].reshape(1, -1)
    r["a_log"] = a["gdn_a_log_2"].reshape(1, -1)
    r["dt_bias"] = a["gdn_dt_bias_2"].reshape(1, -1)
    r["ret_decay"] = a["ret_log_decay_2"].reshape(1, -1)
    cols = lambda v: v.reshape(-1, P).T
    r["b_mod"] = cols(a["b_mod_2"][0])
    r["cvec"] = np.stack([cols(a["c_2"][0]), cols(a["c_ctx_2"])], -1).reshape(P, -1)
    r["conv"] = a["gdn_conv_2"][0].reshape(3, 12, P).transpose(2, 0, 1).reshape(P, -1)
    r["norm_cols"] = np.concatenate([cols(a["norm_mix_pre_2"][0]), cols(a["norm_ffn_pre_2"][0])], 1)
    r["w_in"] = tiles(a["w_in"])
    r["w_o"] = tiles(a["w_o"])
    r["peer_wq"] = tiles(a["peer_wq"])
    r["peer_keys"] = a["peer_keys"].transpose(0, 4, 1, 2, 3).reshape(LAYERS, P, 2048)
    r["peer_u"] = a["peer_u"].reshape(-1, D)
    r["peer_v"] = a["peer_v"].reshape(-1, D)
    r["ctx"] = a["ctx_2"][0]
    r["w_mod"] = tiles(a["w_mod_2"][0])
    w = a["w_in_2"][0]
    r["w_in2"] = tiles(np.concatenate([w[:, 0:2048], w[:, 2064:]], 1))
    r["w_gab"] = tiles(w[:, 2048:2064], 16)[0]
    r["w_ret_out"] = tiles(a["w_ret_out_2"][0], 1024)[0]
    r["w_gdn_out"] = tiles(a["w_gdn_out_2"][0], 1024)[0]
    r["w_o2"] = tiles(a["w_o_2"][0])
    r["w_router"] = tiles(a["w_router_2"][0], 64)[0]
    r["router_bias"] = a["router_bias_2"].reshape(1, -1)
    r["w_gu"] = tiles(np.concatenate([a["w_gate_2"][0], a["w_up_2"][0]], -1))[:, 0]
    r["w_down"] = tiles(a["w_down_2"][0], 1024)[:, 0]
    r["w_gu_sh"] = tiles(np.concatenate([a["w_sh_gate_2"][0], a["w_sh_up_2"][0]], -1))[0]
    r["w_down_sh"] = tiles(a["w_sh_down_2"][0], 1024)[0]
    return {k: np.ascontiguousarray(v) for k, v in r.items()}


def kernel(**inputs):
    import concourse.bacc as _bacc
    from concourse import mybir as _mybir
    from concourse.bass_utils import run_bass_kernel_spmd as _run

    nc = _bacc.Bacc("TRN2", target_bir_lowering=False, num_devices=1)
    arrays, d = {}, {}
    for name, a in arrays_of(inputs).items():
        arrays[f"in_{name}"] = a
        d[name] = nc.dram_tensor(f"in_{name}", a.shape, _mybir.dt.from_np(a.dtype), kind="ExternalInput").ap()
    out = nc.dram_tensor("out_0", (T, D), F32, kind="ExternalOutput").ap()
    for name, rows in TABLES.items():
        d[name] = nc.dram_tensor(name, (rows, D), F32).ap()
    build(nc, d, out)
    r = _run(nc, [arrays], core_ids=[0])
    return r.results[0]["out_0"].reshape(1, T, D)
```
